# Optimizing a Trainium2 kernel written in Bass

```python
import math
import jax
import jax.numpy as jnp
from jax import lax
import numpy as np
import jax, jax.numpy as jnp

D_MODEL = 1024
BATCH = 1
SEQ = 512
DEPTH = 1

HEAD_DIM = 64
ROPE_THETA = 10000.0
RMS_EPS = 1e-6
NEG_INF = -1e30
BLOCK = 128

A_Q_HEADS = 8
A_KV_HEADS = 2
A_GROUP = A_Q_HEADS // A_KV_HEADS
WINDOW = 128
A_Q_WIDTH = A_Q_HEADS * HEAD_DIM
A_KV_WIDTH = A_KV_HEADS * HEAD_DIM

HY_WIDTH = D_MODEL // 2
HY_ORDER = 2
HY_DIRS = 2
HY_SHORT = 3
HY_BANDS = 16
HY_POS_DIM = 1 + 2 * HY_BANDS
HY_FILTER_HIDDEN = 64
HY_DECAY_TARGET = 1e-2
HY_FAST_PCT = 0.3
HY_SLOW_PCT = 1.5

C_HEADS = 4
C_WIDTH = C_HEADS * 2 * HEAD_DIM

N_BRANCH = 3
IN_SIZES = (A_Q_WIDTH, A_KV_WIDTH, A_KV_WIDTH, (HY_ORDER + 1) * HY_WIDTH, C_WIDTH, C_WIDTH, C_WIDTH, N_BRANCH * D_MODEL)
IN_COLS = sum(IN_SIZES)
IN_SPLITS = tuple(sum(IN_SIZES[:i + 1]) for i in range(len(IN_SIZES) - 1))

D_FF = -(-8 * D_MODEL // (3 * 256)) * 256


def rms_norm(x, g):
    xf = x.astype(jnp.float32)
    y = xf * lax.rsqrt(jnp.mean(xf * xf, axis=-1, keepdims=True) + RMS_EPS)
    return (y * g.astype(jnp.float32)).astype(x.dtype)

def rope_tables(seq):
    pos = jnp.arange(seq, dtype=jnp.float32)
    inv = ROPE_THETA ** (-jnp.arange(0, HEAD_DIM, 2, dtype=jnp.float32) / HEAD_DIM)
    ang = pos[:, None] * inv[None, :]
    return jnp.cos(ang), jnp.sin(ang)

def apply_rope(x, cos, sin):
    c = cos[None, :, None, :].astype(x.dtype)
    s = sin[None, :, None, :].astype(x.dtype)
    x1, x2 = jnp.split(x, 2, axis=-1)
    return jnp.concatenate([x1 * c - x2 * s, x2 * c + x1 * s], axis=-1)

def window_attention(q, k, v, sink):
    B, S = q.shape[0], q.shape[1]
    nb = S // BLOCK
    span = BLOCK + 2 * WINDOW
    qb = q.reshape(B, nb, BLOCK, A_KV_HEADS, A_GROUP, HEAD_DIM)
    pad = ((0, 0), (WINDOW, WINDOW), (0, 0), (0, 0))
    kp = jnp.pad(k, pad)
    vp = jnp.pad(v, pad)
    idx = jnp.arange(nb)[:, None] * BLOCK + jnp.arange(span)[None, :]
    kb = kp[:, idx]
    vb = vp[:, idx]
    s = jnp.einsum('bnqhgd,bnkhd->bnhgqk', qb, kb).astype(jnp.float32) / math.sqrt(HEAD_DIM)
    q_pos = jnp.arange(nb)[:, None] * BLOCK + jnp.arange(BLOCK)[None, :]
    k_pos = idx - WINDOW
    dist = k_pos[:, None, :] - q_pos[:, :, None]
    valid = (jnp.abs(dist) <= WINDOW) & (k_pos[:, None, :] >= 0) & (k_pos[:, None, :] < S)
    s = jnp.where(valid[None, :, None, None], s, NEG_INF)
    sink_b = jnp.broadcast_to(sink.astype(jnp.float32).reshape(A_KV_HEADS, A_GROUP)[None, None, :, :, None, None], s.shape[:-1] + (1,))
    p = jax.nn.softmax(jnp.concatenate([s, sink_b], axis=-1), axis=-1)[..., :-1]
    o = jnp.einsum('bnhgqk,bnkhd->bnqhgd', p.astype(v.dtype), vb)
    return o.reshape(B, S, A_Q_HEADS * HEAD_DIM)

def diff_attention(q, k, v, lam):
    B, S = q.shape[0], q.shape[1]
    nb = S // BLOCK
    qb = q.reshape(B, nb, BLOCK, C_HEADS, 2, HEAD_DIM).transpose(1, 0, 3, 4, 2, 5)
    kt = k.transpose(0, 2, 3, 1, 4)
    vt = v.transpose(0, 2, 1, 3)

    def one_block(qblk):
        s = jnp.einsum('bhcqd,bhckd->bhcqk', qblk, kt).astype(jnp.float32) / math.sqrt(HEAD_DIM)
        p = jax.nn.softmax(s, axis=-1)
        a = p[:, :, 0] - lam * p[:, :, 1]
        return jnp.einsum('bhqk,bhkd->bhqd', a.astype(v.dtype), vt)

    o = lax.map(one_block, qb)
    return o.transpose(1, 0, 3, 2, 4).reshape(B, S, C_HEADS, 2 * HEAD_DIM)

def short_conv(u, w, b):
    L = u.shape[1]
    up = jnp.pad(u, ((0, 0), (1, 1), (0, 0)))
    return up[:, :L] * w[0] + up[:, 1:L + 1] * w[1] + up[:, 2:] * w[2] + b

def hyena_filters(L, w1, b1, f1, w2, b2, f2, w3):
    f32 = jnp.float32
    pos = jnp.arange(L, dtype=f32)
    t = pos / max(L - 1, 1)
    bands = jnp.arange(1, HY_BANDS + 1, dtype=f32)
    ang = 2.0 * math.pi * pos[:, None] * bands[None, :] / L
    z = jnp.concatenate([t[:, None], jnp.cos(ang), jnp.sin(ang)], axis=-1)
    h = jnp.sin(f1.astype(f32) * (z @ w1.astype(f32) + b1.astype(f32)))
    h = jnp.sin(f2.astype(f32) * (h @ w2.astype(f32) + b2.astype(f32)))
    h = (h @ w3.astype(f32)).reshape(L, HY_ORDER, HY_DIRS, HY_WIDTH)
    min_decay = math.log(HY_DECAY_TARGET) / HY_SLOW_PCT
    max_decay = math.log(HY_DECAY_TARGET) / HY_FAST_PCT
    deltas = jnp.abs(jnp.linspace(min_decay, max_decay, HY_WIDTH, dtype=f32))
    decay = jnp.exp(-t[:, None] * deltas[None, :])
    h = h * decay[:, None, None, :]
    fwd, bwd = h[:, :, 0], h[:, :, 1]
    c = jnp.concatenate([fwd[:1] + bwd[:1], fwd[1:], jnp.zeros_like(fwd[:1]), bwd[1:][::-1]], axis=0)
    return c * lax.rsqrt(jnp.sum(c * c, axis=0, keepdims=True) + RMS_EPS)

def fft_conv(u, cf):
    L = u.shape[1]
    U = jnp.fft.rfft(u.astype(jnp.float32), n=2 * L, axis=1)
    y = jnp.fft.irfft(U * cf[None], n=2 * L, axis=1)[:, :L]
    return y.astype(u.dtype)

def hyena_branch(u, conv_w, conv_b, w1, b1, f1, w2, b2, f2, w3, hy_d):
    L = u.shape[1]
    u = short_conv(u, conv_w, conv_b)
    v, x1, x2 = jnp.split(u, 3, axis=-1)
    cf = jnp.fft.rfft(hyena_filters(L, w1, b1, f1, w2, b2, f2, w3), axis=0)
    z = x1 * (fft_conv(v, cf[:, 0]) + hy_d[0] * v)
    z = x2 * (fft_conv(z, cf[:, 1]) + hy_d[1] * z)
    return z

def first_inputs(seed: int = 0) -> dict:
    key = jax.random.key(seed)
    ks = jax.random.split(key, 40)

    def nrm(i, shape, scale):
        return jax.random.normal(ks[i], shape, dtype=jnp.float32) * scale

    def gain(i, shape):
        return 1.0 + nrm(i, shape, 0.05)

    L = DEPTH
    return {
        'x': nrm(0, (BATCH, SEQ, D_MODEL), 1.0),
        'norm1_g': gain(1, (L, D_MODEL)),
        'w_in': nrm(2, (L, D_MODEL, IN_COLS), D_MODEL ** -0.5),
        'sink_a': nrm(3, (L, A_Q_HEADS), 0.5),
        'qn_a': gain(4, (L, HEAD_DIM)),
        'kn_a': gain(5, (L, HEAD_DIM)),
        'conv_w': nrm(6, (L, HY_SHORT, (HY_ORDER + 1) * HY_WIDTH), 0.6),
        'conv_b': nrm(7, (L, (HY_ORDER + 1) * HY_WIDTH), 0.01),
        'filt_w1': nrm(8, (L, HY_POS_DIM, HY_FILTER_HIDDEN), HY_POS_DIM ** -0.5),
        'filt_b1': nrm(9, (L, HY_FILTER_HIDDEN), 0.1),
        'filt_f1': gain(10, (L, HY_FILTER_HIDDEN)),
        'filt_w2': nrm(11, (L, HY_FILTER_HIDDEN, HY_FILTER_HIDDEN), HY_FILTER_HIDDEN ** -0.5),
        'filt_b2': nrm(12, (L, HY_FILTER_HIDDEN), 0.1),
        'filt_f2': gain(13, (L, HY_FILTER_HIDDEN)),
        'filt_w3': nrm(14, (L, HY_FILTER_HIDDEN, HY_ORDER * HY_DIRS * HY_WIDTH), HY_FILTER_HIDDEN ** -0.5),
        'hy_d': nrm(15, (L, HY_ORDER, HY_WIDTH), 0.1),
        'qn_c': gain(16, (L, HEAD_DIM)),
        'kn_c': gain(17, (L, HEAD_DIM)),
        'lam_q1': nrm(18, (L, HEAD_DIM), 0.1),
        'lam_k1': nrm(19, (L, HEAD_DIM), 0.1),
        'lam_q2': nrm(20, (L, HEAD_DIM), 0.1),
        'lam_k2': nrm(21, (L, HEAD_DIM), 0.1),
        'subln_c': gain(22, (L, 2 * HEAD_DIM)),
        'w_oa': nrm(23, (L, A_Q_WIDTH, D_MODEL), A_Q_WIDTH ** -0.5),
        'w_ob': nrm(24, (L, HY_WIDTH, D_MODEL), HY_WIDTH ** -0.5),
        'w_oc': nrm(25, (L, C_WIDTH, D_MODEL), C_WIDTH ** -0.5),
        'w_out': nrm(26, (L, D_MODEL, D_MODEL), D_MODEL ** -0.5),
        'norm2_g': gain(27, (L, D_MODEL)),
        'ffn_w1': nrm(28, (L, D_MODEL, D_FF), D_MODEL ** -0.5),
        'ffn_w3': nrm(29, (L, D_MODEL, D_FF), D_MODEL ** -0.5),
        'ffn_w2': nrm(30, (L, D_FF, D_MODEL), D_FF ** -0.5),
    }

def first_block(x, norm1_g, w_in, sink_a, qn_a, kn_a, conv_w, conv_b, filt_w1, filt_b1, filt_f1, filt_w2, filt_b2, filt_f2, filt_w3, hy_d, qn_c, kn_c, lam_q1, lam_k1, lam_q2, lam_k2, subln_c, w_oa, w_ob, w_oc, w_out, norm2_g, ffn_w1, ffn_w3, ffn_w2):
    B, S = x.shape[0], x.shape[1]
    cos, sin = rope_tables(S)
    for l in range(DEPTH):
        h = rms_norm(x, norm1_g[l])
        proj = h @ w_in[l]
        qa, ka, va, hy_in, qc, kc, vc, gate_logits = jnp.split(proj, IN_SPLITS, axis=-1)

        qa = apply_rope(rms_norm(qa.reshape(B, S, A_Q_HEADS, HEAD_DIM), qn_a[l]), cos, sin)
        ka = apply_rope(rms_norm(ka.reshape(B, S, A_KV_HEADS, HEAD_DIM), kn_a[l]), cos, sin)
        va = va.reshape(B, S, A_KV_HEADS, HEAD_DIM)
        out_a = window_attention(qa, ka, va, sink_a[l])

        out_b = hyena_branch(hy_in, conv_w[l], conv_b[l], filt_w1[l], filt_b1[l], filt_f1[l], filt_w2[l], filt_b2[l], filt_f2[l], filt_w3[l], hy_d[l])

        lambda_init = 0.8 - 0.6 * math.exp(-0.3 * l)
        lam = (jnp.exp(jnp.sum(lam_q1[l].astype(jnp.float32) * lam_k1[l].astype(jnp.float32)))
               - jnp.exp(jnp.sum(lam_q2[l].astype(jnp.float32) * lam_k2[l].astype(jnp.float32)))
               + lambda_init)
        qc = apply_rope(rms_norm(qc.reshape(B, S, 2 * C_HEADS, HEAD_DIM), qn_c[l]), cos, sin).reshape(B, S, C_HEADS, 2, HEAD_DIM)
        kc = apply_rope(rms_norm(kc.reshape(B, S, 2 * C_HEADS, HEAD_DIM), kn_c[l]), cos, sin).reshape(B, S, C_HEADS, 2, HEAD_DIM)
        vc = vc.reshape(B, S, C_HEADS, 2 * HEAD_DIM)
        out_c = diff_attention(qc, kc, vc, lam)
        out_c = (rms_norm(out_c, subln_c[l]) * (1.0 - lambda_init)).reshape(B, S, C_WIDTH)

        g = jax.nn.sigmoid(gate_logits.astype(jnp.float32)).reshape(B, S, N_BRANCH, D_MODEL).astype(x.dtype)
        merged = (g[:, :, 0] * (out_a @ w_oa[l])
                  + g[:, :, 1] * (out_b @ w_ob[l])
                  + g[:, :, 2] * (out_c @ w_oc[l]))
        x = x + merged @ w_out[l]

        h2 = rms_norm(x, norm2_g[l])
        x = x + (jax.nn.silu(h2 @ ffn_w1[l]) * (h2 @ ffn_w3[l])) @ ffn_w2[l]
    return x


N_HEADS = D_MODEL // HEAD_DIM
N_FOX_HEADS = N_HEADS // 2
N_SB_HEADS = N_HEADS - N_FOX_HEADS
FOX_WIDTH = N_FOX_HEADS * HEAD_DIM
SB_WIDTH = N_SB_HEADS * HEAD_DIM
MIX_WIDTH = FOX_WIDTH + SB_WIDTH
IN_COLS_2 = 3 * FOX_WIDTH + N_FOX_HEADS + 3 * SB_WIDTH
D_FF_2 = ((8 * D_MODEL // 3 + 127) // 128) * 128
CONV_WIDTH = 3
BLOCK_Q = 128
EPS = 1e-6


def rmsnorm(x, g):
    xf = x.astype(jnp.float32)
    y = xf * lax.rsqrt(jnp.mean(xf * xf, axis=-1, keepdims=True) + EPS)
    return (y * g.astype(jnp.float32)).astype(x.dtype)

def split_heads(t, n_heads):
    b, s, _ = t.shape
    return t.reshape(b, s, n_heads, HEAD_DIM).transpose(0, 2, 1, 3)

def merge_heads(t):
    b, h, s, d = t.shape
    return t.transpose(0, 2, 1, 3).reshape(b, s, h * d)

def to_blocks(t):
    b, h, s = t.shape[:3]
    t = t.reshape(b, h, s // BLOCK_Q, BLOCK_Q, *t.shape[3:])
    return jnp.moveaxis(t, 2, 0)

def from_blocks(t):
    nb, b, h, bq, d = t.shape
    return jnp.moveaxis(t, 0, 2).reshape(b, h, nb * bq, d)

def fox_attention(q, k, v, log_f):
    s_len = q.shape[2]
    scale = HEAD_DIM ** -0.5
    kf = k.astype(jnp.float32)
    vf = v.astype(jnp.float32)
    F = jnp.cumsum(log_f, axis=-1)
    kpos = jnp.arange(s_len)

    def block(args):
        i, qi, Fi = args
        qpos = i * BLOCK_Q + jnp.arange(BLOCK_Q)
        logits = (jnp.einsum('bhqd,bhkd->bhqk', qi.astype(jnp.float32), kf) * scale
                  + Fi[..., :, None] - F[:, :, None, :])
        logits = jnp.where(kpos[None, :] <= qpos[:, None], logits, -jnp.inf)
        p = jax.nn.softmax(logits, axis=-1)
        return jnp.einsum('bhqk,bhkd->bhqd', p, vf)

    out = lax.map(block, (jnp.arange(s_len // BLOCK_Q), to_blocks(q), to_blocks(F)))
    return from_blocks(out).astype(v.dtype)

def stick_breaking_attention(q, k, v):
    s_len = q.shape[2]
    scale = HEAD_DIM ** -0.5
    kf = k.astype(jnp.float32)
    vf = v.astype(jnp.float32)
    kpos = jnp.arange(s_len)

    def block(args):
        i, qi = args
        qpos = i * BLOCK_Q + jnp.arange(BLOCK_Q)
        mask = kpos[None, :] < qpos[:, None]
        z = jnp.einsum('bhqd,bhkd->bhqk', qi.astype(jnp.float32), kf) * scale
        log_beta = jax.nn.log_sigmoid(z)
        log_one_minus = jnp.where(mask, jax.nn.log_sigmoid(-z), 0.0)
        after = lax.cumsum(log_one_minus, axis=3, reverse=True) - log_one_minus
        weights = jnp.where(mask, jnp.exp(log_beta + after), 0.0)
        return jnp.einsum('bhqk,bhkd->bhqd', weights, vf)

    out = lax.map(block, (jnp.arange(s_len // BLOCK_Q), to_blocks(q)))
    return from_blocks(out).astype(v.dtype)

def causal_dwconv(u, w, b):
    s_len = u.shape[1]
    up = jnp.pad(u, ((0, 0), (CONV_WIDTH - 1, 0), (0, 0)))
    out = b + w[0] * up[:, 0:s_len]
    for kk in range(1, CONV_WIDTH):
        out = out + w[kk] * up[:, kk:kk + s_len]
    return out

def second_inputs(seed: int = 0) -> dict:
    key = jax.random.key(seed)
    ks = jax.random.split(key, 13)
    f32 = jnp.float32
    x = jax.random.normal(ks[0], (BATCH, SEQ, D_MODEL), f32)
    attn_norm_g = 1.0 + 0.05 * jax.random.normal(ks[1], (DEPTH, D_MODEL), f32)
    w_in = jax.random.normal(ks[2], (DEPTH, D_MODEL, IN_COLS_2), f32) * D_MODEL ** -0.5
    forget_bias = (jnp.linspace(1.0, 6.0, N_FOX_HEADS, dtype=f32)[None, :]
                   + 0.1 * jax.random.normal(ks[3], (DEPTH, N_FOX_HEADS), f32))
    fox_out_g = 1.0 + 0.05 * jax.random.normal(ks[4], (DEPTH, FOX_WIDTH), f32)
    sb_out_g = 1.0 + 0.05 * jax.random.normal(ks[5], (DEPTH, SB_WIDTH), f32)
    w_out = jax.random.normal(ks[6], (DEPTH, MIX_WIDTH, D_MODEL), f32) * MIX_WIDTH ** -0.5
    ffn_norm_g = 1.0 + 0.05 * jax.random.normal(ks[7], (DEPTH, D_MODEL), f32)
    w_up = jax.random.normal(ks[8], (DEPTH, D_MODEL, 2 * D_FF_2), f32) * D_MODEL ** -0.5
    conv_w = jax.random.normal(ks[9], (DEPTH, CONV_WIDTH, 2 * D_FF_2), f32) * CONV_WIDTH ** -0.5
    conv_b = 0.02 * jax.random.normal(ks[10], (DEPTH, 2 * D_FF_2), f32)
    w_down = jax.random.normal(ks[11], (DEPTH, D_FF_2, D_MODEL), f32) * D_FF_2 ** -0.5
    final_norm_g = 1.0 + 0.05 * jax.random.normal(ks[12], (D_MODEL,), f32)
    return {"x": x, "attn_norm_g": attn_norm_g, "w_in": w_in, "forget_bias": forget_bias,
            "fox_out_g": fox_out_g, "sb_out_g": sb_out_g, "w_out": w_out,
            "ffn_norm_g": ffn_norm_g, "w_up": w_up, "conv_w": conv_w, "conv_b": conv_b,
            "w_down": w_down, "final_norm_g": final_norm_g}

def second_block(x, attn_norm_g, w_in, forget_bias, fox_out_g, sb_out_g, w_out,
              ffn_norm_g, w_up, conv_w, conv_b, w_down, final_norm_g):
    b, s_len, _ = x.shape
    splits = [FOX_WIDTH, 2 * FOX_WIDTH, 3 * FOX_WIDTH, 3 * FOX_WIDTH + N_FOX_HEADS,
              3 * FOX_WIDTH + N_FOX_HEADS + SB_WIDTH,
              3 * FOX_WIDTH + N_FOX_HEADS + 2 * SB_WIDTH]
    for l in range(DEPTH):
        h = rmsnorm(x, attn_norm_g[l])
        proj = h @ w_in[l]
        fq, fk, fv, f_logit, sq, sk, sv = jnp.split(proj, splits, axis=-1)
        log_f = jax.nn.log_sigmoid(
            (f_logit + forget_bias[l]).astype(jnp.float32)).transpose(0, 2, 1)
        o_fox = fox_attention(split_heads(fq, N_FOX_HEADS), split_heads(fk, N_FOX_HEADS),
                              split_heads(fv, N_FOX_HEADS), log_f)
        o_sb = stick_breaking_attention(split_heads(sq, N_SB_HEADS), split_heads(sk, N_SB_HEADS),
                                        split_heads(sv, N_SB_HEADS))
        o = jnp.concatenate([rmsnorm(merge_heads(o_fox), fox_out_g[l]),
                             rmsnorm(merge_heads(o_sb), sb_out_g[l])], axis=-1)
        x = x + o @ w_out[l]
        h = rmsnorm(x, ffn_norm_g[l])
        u = causal_dwconv(h @ w_up[l], conv_w[l], conv_b[l])
        gate, val = jnp.split(u, 2, axis=-1)
        x = x + (jax.nn.silu(gate) * val) @ w_down[l]
    return rmsnorm(x, final_norm_g)


def setup_inputs(seed=0):
    out = dict(first_inputs(seed))
    for name, value in second_inputs(seed + 1).items():
        if name != "x":
            out[name + "_2"] = value
    return out


def reference(
    x, norm1_g, w_in, sink_a, qn_a, kn_a, conv_w, conv_b, filt_w1, filt_b1, filt_f1, filt_w2,
    filt_b2, filt_f2, filt_w3, hy_d, qn_c, kn_c, lam_q1, lam_k1, lam_q2, lam_k2, subln_c, w_oa,
    w_ob, w_oc, w_out, norm2_g, ffn_w1, ffn_w3, ffn_w2, attn_norm_g_2, w_in_2, forget_bias_2,
    fox_out_g_2, sb_out_g_2, w_out_2, ffn_norm_g_2, w_up_2, conv_w_2, conv_b_2, w_down_2,
    final_norm_g_2,
):
    x = first_block(
        x, norm1_g, w_in, sink_a, qn_a, kn_a, conv_w, conv_b, filt_w1, filt_b1, filt_f1,
        filt_w2, filt_b2, filt_f2, filt_w3, hy_d, qn_c, kn_c, lam_q1, lam_k1, lam_q2, lam_k2,
        subln_c, w_oa, w_ob, w_oc, w_out, norm2_g, ffn_w1, ffn_w3, ffn_w2,
    )
    return second_block(
        x, attn_norm_g_2, w_in_2, forget_bias_2, fox_out_g_2, sb_out_g_2, w_out_2, ffn_norm_g_2,
        w_up_2, conv_w_2, conv_b_2, w_down_2, final_norm_g_2,
    )


_drawn_inputs = setup_inputs


def setup_inputs(seed=0):
    import zlib

    import numpy as np

    out = dict(_drawn_inputs(seed))
    spreads = {}
    factors = {'sink_a': 8.0,
     'qn_a': 8.0,
     'kn_a': 8.0,
     'lam_q2': 2.769,
     'conv_b_2': 5.77,
     'subln_c': 3.019,
     'conv_b': 2.951,
     'filt_f1': 2.914,
     'filt_f2': 3.016,
     'fox_out_g_2': 3.291,
     'sb_out_g_2': 3.264,
     'ffn_norm_g_2': 2.796}
    for name, (base, spread) in spreads.items():
        noise = np.random.default_rng([zlib.crc32(name.encode()), seed]).standard_normal(out[name].shape)
        drawn = base * np.exp(spread * noise) if base else spread * noise
        out[name] = jnp.asarray(drawn.astype(out[name].dtype))
    for name, factor in factors.items():
        out[name] = (out[name] * factor).astype(out[name].dtype)
    return out
```

```python
import math
import numpy as np
import concourse.bass as bass
from concourse import mybir

F32 = mybir.dt.float32
F32R = mybir.dt.float32r
ALU = mybir.AluOpType
ACT = mybir.ActivationFunctionType
AX = mybir.AxisListType

S = 512
D = 1024
NEG = -1e30
EPS = 1e-6
LAM0 = 0.2
RAW, HL, LA = 3, 3, 2


def vec_layout():
    names = [
        ("g1", 8), ("g2", 8), ("g3", 8), ("g4", 8), ("cw", 36), ("cb", 12), ("hd", 8), ("gfox", 4), ("gsb", 4),
        ("cw2", 132), ("cb2", 44), ("subln", 1), ("sink", 8), ("fb", 1), ("b1", 1), ("f1", 1), ("b2", 1), ("f2", 1),
        ("qna", 64), ("kna", 64), ("qnc", 64), ("knc", 64), ("lq1", 64), ("lk1", 64), ("lq2", 64), ("lk2", 64),
        ("ident", 128), ("one", 1), ("wS0", 1), ("wD0", 1), ("half", 1), ("mhalf", 8), ("cos", 256), ("sin", 256),
        ("w1", 64), ("w2", 64),
    ]
    at, o = {}, 0
    for n, w in names:
        at[n] = (o, w)
        o += w
    return at, o


def groups():
    out = []
    for i in range(3):
        out.append(("hy%d" % i, 8, 512, "feat"))
    out += [("qa", 8, 512, "tok"), ("kva", 8, 256, "tok"), ("gB0", 8, 512, "feat"), ("bB0", 4, 512, "feat"),
            ("gB1", 8, 512, "feat"), ("bB1", 4, 512, "feat"), ("qc", 8, 512, "tok"), ("kc", 8, 512, "tok"),
            ("vc", 8, 512, "tok"), ("gA0", 8, 512, "feat"), ("bA0", 4, 512, "feat"), ("gA1", 8, 512, "feat"),
            ("bA1", 4, 512, "feat"), ("gC0", 8, 512, "feat"), ("gC1", 8, 512, "feat"), ("bC0", 4, 512, "feat"),
            ("bC1", 4, 512, "feat"), ("wo0", 8, 512, "tok"), ("wo1", 8, 512, "tok")]
    for i in range(11):
        out.append(("up%d" % i, 8, 512, "feat"))
    out += [("dn0", 22, 512, "tok"), ("dn1", 22, 512, "tok")]
    out += [("sq", 8, 512, "feat"), ("sk", 8, 512, "feat"), ("sv", 8, 512, "tok"), ("fl", 8, 128, "feat"),
            ("fq", 8, 512, "feat"), ("fk", 8, 512, "feat"), ("fv", 8, 512, "tok"),
            ("xo0", 8, 512, "tok"), ("xo1", 8, 512, "tok")]
    for i in range(11):
        out.append(("vp%d" % i, 8, 512, "feat"))
    out += [("vd0", 22, 512, "tok"), ("vd1", 22, 512, "tok")]
    return out


def slot_table():
    table, offs, o = {}, [], 0
    for name, nk, n, mode in groups():
        first = len(offs)
        for _ in range(nk // 2):
            offs.append((o, 2 * n))
            o += 128 * 2 * n
        table[name] = (first, nk // 2, n, mode)
    return table, offs, o


class Item:
    def __init__(self, eng, fn, after, sem=None):
        self.eng, self.fn, self.after, self.sem = eng, fn, after, sem
        self.used, self.value = False, 0


def flat(xs):
    for x in xs:
        if x is None:
            continue
        if isinstance(x, (list, tuple)):
            yield from flat(x)
        else:
            yield x


class Queues:
    IN_ORDER = ("vector", "scalar", "gpsimd")
    ENGINES = ("tensor", "vector", "scalar", "gpsimd", "sync")

    def __init__(self, nc):
        self.nc = nc
        self.q = {e: [] for e in self.ENGINES}
        self.sem = {e: nc.alloc_semaphore("done_" + e) for e in self.ENGINES[:4]}
        self.dma_count = {}

    def put(self, eng, fn, after):
        it = Item(eng, fn, list(flat(after)))
        if eng in self.IN_ORDER and self.q[eng]:
            it.after.append(self.q[eng][-1])
        for a in it.after:
            a.used = True
        self.q[eng].append(it)
        return it

    def dma(self, eng, out, in_, sem, after):
        it = Item(eng, lambda e: e.dma_start(out, in_), list(flat(after)), sem)
        for a in it.after:
            a.used = True
        n = self.dma_count.get(id(sem), 0) + 16
        self.dma_count[id(sem)] = n
        it.value = n
        self.q[eng].append(it)
        return it

    def last(self, *engs):
        return [self.q[e][-1] for e in engs if self.q[e]]

    def number(self):
        for e in self.ENGINES[:4]:
            n = 0
            for it in self.q[e]:
                if it.sem is None and it.used:
                    n += 1
                    it.value = n

    def run(self, name, eng):
        seen = {}
        for it in self.q[name]:
            need = {}
            for a in it.after:
                sem = a.sem if a.sem is not None else self.sem[a.eng]
                if a.value > need.get(id(sem), (0, None))[0]:
                    need[id(sem)] = (a.value, sem)
            for k, (v, sem) in need.items():
                if seen.get(k, 0) < v:
                    eng.wait_ge(sem, v)
                    seen[k] = v
            ins = it.fn(eng)
            if it.sem is not None:
                ins.then_inc(it.sem, 16)
            elif it.used:
                ins.then_inc(self.sem[name], 1)


def build(nc, d, out):
    B0 = 16512
    VEC, NV = vec_layout()
    TABLE, OFFS, _ = slot_table()

    def sb(name, kb, shape, dt=F32):
        return nc.alloc_sbuf_tensor_at(name, shape, dt, offset=B0 + int(kb * 1024))

    AR = 75
    hThi = sb("hThi", 0, [128, 8, S], F32R)
    hTlo = sb("hTlo", 16, [128, 8, S], F32R)
    wraw = [sb(f"wraw{i}", 32 + 4 * i, [128, 1024]) for i in range(RAW)]
    whi = [sb(f"whi{i}", 44 + 4 * i, [128, 1024], F32R) for i in range(HL)]
    wlo = [sb(f"wlo{i}", 56 + 4 * i, [128, 1024], F32R) for i in range(HL)]
    vec = sb("vec", 68, [128, NV])
    ps = [nc.alloc_psum_tensor(f"ps{i}", [128, 512], F32) for i in range(8)]
    bank_free = [[] for _ in range(8)]

    Q = Queues(nc)

    def V(fn, *after):
        return Q.put("vector", fn, after)

    def A(fn, *after):
        return Q.put("scalar", fn, after)

    def G(fn, *after):
        return Q.put("gpsimd", fn, after)

    def P(fn, *after):
        return Q.put("tensor", fn, after)

    def sem(name):
        return nc.alloc_semaphore(name)

    def load(out_, in_, s, *after, eng="sync"):
        return Q.dma(eng, out_, in_, s, after)

    def col(name, i=0, n=1, p=128):
        o, _ = VEC[name]
        return vec[0:p, o + i:o + i + n]

    ident = col("ident", 0, 128)

    s_vec = sem("s_vec")
    t_vec = load(vec[:], d["vec"], s_vec)

    s_raw = [sem(f"s_raw{i}") for i in range(RAW)]
    dma_tok, hi_tok, lo_tok, pe_tok = {}, {}, {}, {}
    n_slots = len(OFFS)
    state = {"dma": 0, "split": 0}

    def raw_view(i):
        o, w = OFFS[i]
        return d["ws"][o:o + 128 * w].rearrange("(p c) -> p c", p=128), w

    def issue_dma(upto):
        while state["dma"] < min(upto, n_slots):
            i = state["dma"]
            src, w = raw_view(i)
            dma_tok[i] = load(wraw[i % RAW][:, 0:w], src, s_raw[i % RAW],
                              lo_tok[i - RAW] if i >= RAW else None)
            state["dma"] += 1

    def issue_split(upto):
        while state["split"] < min(upto, n_slots):
            i = state["split"]
            issue_dma(i + 1)
            _, w = raw_view(i)
            r, h = wraw[i % RAW], i % HL
            hi_tok[i] = A(lambda e, r=r, h=h, w=w: e.activation(whi[h][:, 0:w], r[:, 0:w], ACT.Copy),
                          dma_tok[i], pe_tok[i - HL] if i >= HL else None)
            lo_tok[i] = V(lambda e, r=r, h=h, w=w: e.tensor_tensor(wlo[h][:, 0:w], r[:, 0:w],
                                                                 whi[h][:, 0:w].bitcast(F32), ALU.subtract),
                          hi_tok[i])
            state["split"] += 1
            issue_dma(i + RAW)

    background, deferred = [], []

    def flush():
        while deferred:
            deferred.pop(0)[1]()

    def pump(n=1):
        for x in deferred:
            x[0] -= 1
        while deferred and deferred[0][0] <= 0:
            deferred.pop(0)[1]()
        for _ in range(n):
            if background:
                try:
                    next(background[0])
                except StopIteration:
                    background.pop(0)

    def drain():
        while background:
            pump()

    turn = [0]

    def gemm(name, act, ready, evac, rate=1, banks=0):
        first, n_s, n, mode = TABLE[name]
        b0 = 4 * turn[0] if banks else 0
        turn[0] = (turn[0] + 1) % 2 if banks else 1
        nb = 4 if mode == "tok" else n // 128
        for s in range(n_s):
            i = first + s
            issue_split(i + 1 + LA)
            h = i % HL
            for b in range(nb):
                for kk in range(2):
                    k = 2 * s + kk
                    ahi, alo = act(k)
                    if mode == "tok":
                        c0, c1 = kk * n, kk * n + n
                        pairs = [(ahi[:, b * 128:b * 128 + 128], whi[h][:, c0:c1]),
                                 (ahi[:, b * 128:b * 128 + 128], wlo[h][:, c0:c1]),
                                 (alo[:, b * 128:b * 128 + 128], whi[h][:, c0:c1])]
                        o = ps[b0 + b][:, 0:n]
                    else:
                        c0 = kk * n + b * 128
                        pairs = [(whi[h][:, c0:c0 + 128], ahi), (whi[h][:, c0:c0 + 128], alo),
                                 (wlo[h][:, c0:c0 + 128], ahi)]
                        o = ps[b0 + b][:]
                    for j, (l, r) in enumerate(pairs):
                        st = s == 0 and kk == 0 and j == 0
                        sp = s == n_s - 1 and kk == 1 and j == 2
                        w = [lo_tok[i]] if (b == 0 and kk == 0 and j == 0) else []
                        if st:
                            w = w + [bank_free[b0 + b]]
                        if j == 0 and ready is not None:
                            w = w + [ready(k)]
                        last = P(lambda e, o=o, l=l, r=r, st=st, sp=sp: e.matmul(o, l, r, start=st, stop=sp), *w)
                if s == n_s - 1:
                    bank_free[b0 + b] = evac(b, ps[b0 + b], last)
            pe_tok[i] = last
            pump(rate)

    def mm(o, l, r, st, sp, *after):
        return P(lambda e: e.matmul(o, l, r, start=st, stop=sp), *after)

    def tr(o, i, *after, n=128):
        return P(lambda e: e.transpose(o, i, ident[0:n, 0:n] if n < 128 else ident), t_vec, *after)

    def split_out(hi, lo, src, scale, *after):
        a = A(lambda e: e.activation(hi, src, ACT.Copy, scale=scale), *after)
        v = V(lambda e: e.scalar_tensor_tensor(lo, src, scale, hi.bitcast(F32), ALU.mult, ALU.subtract), a)
        return v

    small = sb("small", 68 + (NV * 4 + 31) // 32 * 32 / 1024, [128, 64])
    assert NV * 4 + 64 * 4 <= 7 * 1024, NV

    h_ready = {}

    def hT(k):
        return hThi[:, k, :], hTlo[:, k, :]

    def half_square(x, i, half, junk, *after):
        return A(lambda e: e.activation(junk, x[:, i, half * 512:half * 512 + 512], ACT.Square,
                                        accum_out=small[:, 48 + 2 * i + half:49 + 2 * i + half]), *after)

    def row_rstd(i, halves):
        c = 48 + 2 * i
        g = G(lambda e: e.tensor_scalar(small[:, i:i + 1], small[:, c:c + 1], 1.0 / D, EPS, ALU.mult, ALU.add),
              halves[0], t_vec)
        g = G(lambda e: e.tensor_scalar(small[:, 4 + i:5 + i], small[:, c + 1:c + 2], 1.0 / D, small[:, i:i + 1],
                                        ALU.mult, ALU.add), halves[1], g)
        return G(lambda e: e.tensor_tensor(small[:, 8 + i:9 + i], small[:, 4 + i:5 + i], col("mhalf"), ALU.pow), g)

    def norm(x, xs, g, sq_toks, h_free, xs_free):
        toks = []
        for i in range(4):
            r = row_rstd(i, sq_toks[i])
            toks.append(V(lambda e, i=i: e.tensor_scalar(xs[:, i, :], x[:, i, :], small[:, 8 + i:9 + i], None,
                                                         ALU.mult), r, xs_free))
        for k in range(8):
            b = (4 + k) % 8
            for i in range(4):
                t = tr(ps[b][:, i * 128:(i + 1) * 128], xs[:, i, k * 128:(k + 1) * 128], toks[i], bank_free[b])
            v = split_out(hThi[:, k, :], hTlo[:, k, :], ps[b][:], col(g, k), t, h_free)
            bank_free[b] = [v]
            h_ready[k] = v
        turn[0] = 1
        return v

    s_x = sem("s_x")
    x1 = sb("x1", AR + 32, [128, 4, D])
    x_dram = d["x"].rearrange("b (i p) c -> p (b i) c", p=128)
    tx = load(x1[:], x_dram, s_x)
    junk1 = sb("junk1", AR, [128, 512])
    issue_split(LA)

    s_f = sem("s_f")
    zT = sb("zT", AR + 126, [33, S])
    w3 = sb("w3", AR + 88, [64, 4, 512])
    cu = sb("cu", AR + 48, [128, 4, 512])
    su = sb("su", AR + 56, [128, 4, 512])
    dec = sb("dec", AR + 80, [128, 4, 512])
    fs = sb("fs", AR + 64, [128, 4, 512])
    fd = sb("fd", AR + 72, [128, 4, 512])
    sq = [sb(f"sq{i}", AR + 98 + 2 * i, [128, 512]) for i in range(2)]
    h1 = sb("h1", AR + 128, [64, S])
    h2 = sb("h2", AR + 96, [64, S])
    ma = [sb(f"ma{i}", AR + 102 + 2 * i, [64, S]) for i in range(4)]
    rrow = sb("rrow", AR + 130, [1, 512])
    Cre = [sb(f"Cre{o}", AR + 16 * o, [128, 4, 512]) for o in range(2)]
    Cim = [sb(f"Cim{o}", AR + 16 * o + 8, [128, 4, 512]) for o in range(2)]
    cs = sb("cs", AR + 32, [128, 4, 512])
    ss = sb("ss", AR + 40, [128, 4, 512])
    rn = small[:, 16:24]

    t_z = load(zT[:], d["zT"], s_f)
    t_w3 = load(w3[:], d["w3"].rearrange("h (g c) -> h g c", g=4), s_f)
    t_f = load(cu[:], d["cu"], s_f)
    t_f = load(su[:], d["su"], s_f)
    t_f = load(dec[:], d["dec"], s_f)

    norm_tok = norm(x1, x1, "g1", [[half_square(x1, i, h, junk1[:], tx) for h in range(2)] for i in range(4)],
                    None, None)
    s_cs = sem("s_cs")
    t_cs = load(cs[:], d["cs"], s_cs, norm_tok, Q.last("tensor"))
    t_cs = load(ss[:], d["ss"], s_cs, norm_tok)

    TWO_PI = 2 * math.pi
    MAGIC = 1.5 * 2 ** 23
    C1 = 6.28125
    C2 = TWO_PI - C1

    def sine(dst, src, b, f, t):
        t = V(lambda e: e.tensor_scalar(ma[0][:], src, col(b, p=64), col(f, p=64), ALU.add, ALU.mult), t)
        u = V(lambda e: e.tensor_scalar(ma[1][:], ma[0][:], 1 / TWO_PI, MAGIC, ALU.mult, ALU.add), t)
        u = V(lambda e: e.tensor_scalar(ma[2][:], ma[1][:], MAGIC, None, ALU.subtract), u)
        u = V(lambda e: e.scalar_tensor_tensor(ma[3][:], ma[2][:], -C1, ma[0][:], ALU.mult, ALU.add), u)
        u = V(lambda e: e.scalar_tensor_tensor(ma[1][:], ma[2][:], -C2, ma[3][:], ALU.mult, ALU.add), u)
        u = V(lambda e: e.tensor_scalar(ma[3][:], ma[1][:], 3.1415925, -3.1415925, ALU.min, ALU.max), u)
        return t, A(lambda e: e.activation(dst, ma[3][:], ACT.Sin), u)

    t = mm(ps[0][0:64, :], col("w1", 0, 64, p=33), zT[:], True, True, t_f, t_vec, bank_free[0])
    bf, t = sine(h1[:], ps[0][0:64, :], "b1", "f1", t)
    bank_free[0] = [bf]
    t = mm(ps[1][0:64, :], col("w2", 0, 64, p=64), h1[:], True, True, t, bank_free[1])
    bf, t_h2 = sine(h2[:], ps[1][0:64, :], "b2", "f2", t)
    bank_free[1] = [bf]
    w3v = w3[:]
    t_ws = []
    for o in range(2):
        f, b = w3v[:, 2 * o, :], w3v[:, 2 * o + 1, :]
        t = V(lambda e, b=b, f=f: e.tensor_tensor(ma[0][:], f, b, ALU.add), t_f, t_h2)
        t = V(lambda e, b=b, f=f: e.tensor_tensor(b, f, b, ALU.subtract), t)
        t = V(lambda e, f=f: e.tensor_copy(f, ma[0][:]), t)
        t_ws.append(t)
    t_rn_ = {}
    ma_done = Q.last("vector", "scalar", "tensor")
    f_free = []

    def filters():
        f_free = []
        for o in range(2):
            td = []
            rb = 7
            for tt in range(4):
                for j, (dst, wc) in enumerate(((fs, "wS0"), (fd, "wD0"))):
                    b = 4 + j
                    t = mm(ps[b][:], h2[:, tt * 128:(tt + 1) * 128], w3v[:, 2 * o + j, :], True, True,
                           t_h2, t_ws[o], bank_free[b])
                    v = V(lambda e, b=b, dst=dst, tt=tt: e.tensor_tensor(dst[:, tt, :], ps[b][:], dec[:, tt, :],
                                                                         ALU.mult), t, t_f, f_free)
                    bank_free[b] = [v]
                    td.append(v)
                    a = A(lambda e, j=j, dst=dst, tt=tt: e.activation(sq[j][:], dst[:, tt, :], ACT.Square), v,
                          Q.last("tensor"))
                    wcol = col(wc) if tt == 0 else col("half")
                    t = mm(ps[rb][0:1, :], wcol, sq[j][:], tt == 0 and j == 0, tt == 3 and j == 1, a,
                           bank_free[rb] if tt == 0 and j == 0 else None)
                yield
            v = V(lambda e: e.tensor_copy(rrow[:], ps[rb][0:1, :]), t)
            bank_free[rb] = [v]
            for c in range(4):
                t = mm(ps[6][:, c:c + 1], rrow[:, c * 128:(c + 1) * 128], col("one", p=1), True, True, v, bank_free[6])
            v = V(lambda e, o=o: e.tensor_scalar(small[:, 24:28], ps[6][:, 0:4], EPS, None, ALU.add), t)
            bank_free[6] = [v]
            g = G(lambda e: e.tensor_tensor(small[:, 28:32], small[:, 24:28], col("mhalf", 0, 4), ALU.pow), v)
            t_rn_[o] = V(lambda e, o=o: e.tensor_scalar(small[:, 16 + 4 * o:20 + 4 * o], small[:, 28:32], 1.0 / 512, None,
                                                    ALU.mult), g)
            for ft in range(4):
                for j, (tab, src, dst) in enumerate(((cu, fs, Cre[o]), (su, fd, Cim[o]))):
                    b = 4 + (2 * ft + j) % 3
                    for tt in range(4):
                        t = mm(ps[b][:], tab[:, tt, ft * 128:(ft + 1) * 128], src[:, tt, :], tt == 0, tt == 3,
                               td, t_f, bank_free[b])
                    a = A(lambda e, b=b, dst=dst, ft=ft: e.activation(dst[:, ft, :], ps[b][:], ACT.Copy), t, norm_tok)
                    bank_free[b] = [a]
                yield
            f_free[:] = Q.last("tensor", "scalar", "vector")

    uT = [sb(f"uT{i}", AR + 102 + 8 * i, [128, 4, S]) for i in range(3)]
    tok = sb("tok", AR + 48, [128, 4, 512])
    Yre = sb("Yre", AR + 64, [128, 4, 512])
    Yn = sb("Yn", AR + 72, [128, 4, 512])
    tm = [sb(f"tm{i}", AR + 80 + 2 * i, [128, 512]) for i in range(4)]
    dv = [sb(f"dv{i}", AR + 88 + 2 * i, [128, 512]) for i in range(2)]
    obhi = sb("obhi", AR + 0, [128, 4, S], F32R)
    oblo = sb("oblo", AR + 8, [128, 4, S], F32R)

    hready = lambda k: h_ready[k]
    u_tok = {}
    background.append(filters())
    for gidx in range(3):
        def evac(b, p, t, gidx=gidx):
            f = gidx * 4 + b
            dst = uT[gidx][:, b, :]
            a = A(lambda e: e.activation(dst, p[:], ACT.Identity, bias=col("cb", f), scale=col("cw", 12 + f)),
                  t, ma_done)
            v = V(lambda e: e.scalar_tensor_tensor(dst[:, 1:S], p[:, 0:S - 1], col("cw", f), dst[:, 1:S],
                                                   ALU.mult, ALU.add), a)
            v = V(lambda e: e.scalar_tensor_tensor(dst[:, 0:S - 1], p[:, 1:S], col("cw", 24 + f),
                                                   dst[:, 0:S - 1], ALU.mult, ALU.add), v)
            u_tok[gidx, b] = v
            return [v]
        gemm("hy%d" % gidx, hT, hready, evac, rate=3)
    drain()
    t_C = Q.last("scalar")
    f_done = Q.last("tensor", "vector", "scalar", "gpsimd")

    vT, x1T, x2T = uT
    src, src_tok = vT, [u_tok[0, b] for b in range(4)]
    tok_free, y_free = [], []
    ob_tok = None
    for o in range(2):
        tk = []
        for tt in range(4):
            b = 4 + tt
            for c in range(4):
                t = tr(ps[b][:, c * 128:(c + 1) * 128], src[:, c, tt * 128:(tt + 1) * 128], src_tok[c], bank_free[b])
            a = A(lambda e, b=b, tt=tt: e.activation(tok[:, tt, :], ps[b][:], ACT.Copy), t, tok_free, f_done)
            bank_free[b] = [a]
            tk.append(a)
        yt = []
        for ft in range(4):
            br, bi = 4 + (2 * ft) % 4, 4 + (2 * ft + 1) % 4
            for bk, tab in ((br, cs), (bi, ss)):
                for tt in range(4):
                    t = mm(ps[bk][:], tab[:, tt, ft * 128:(ft + 1) * 128], tok[:, tt, :], tt == 0, tt == 3,
                           tk[tt], t_cs, bank_free[bk])
            cre, cim = Cre[o][:, ft, :], Cim[o][:, ft, :]
            v0 = V(lambda e, br=br, cre=cre: e.tensor_tensor(tm[0][:], ps[br][:], cre, ALU.mult), t, t_C,
                   Q.last("gpsimd"))
            v1 = V(lambda e, bi=bi, cim=cim: e.tensor_tensor(tm[1][:], ps[bi][:], cim, ALU.mult))
            g1 = G(lambda e, ft=ft: e.tensor_tensor(Yre[:, ft, :], tm[0][:], tm[1][:], ALU.add), v0, v1, y_free)
            v2 = V(lambda e, bi=bi, cre=cre: e.tensor_tensor(tm[2][:], ps[bi][:], cre, ALU.mult))
            v3 = V(lambda e, br=br, cim=cim: e.tensor_tensor(tm[3][:], ps[br][:], cim, ALU.mult))
            g2 = G(lambda e, ft=ft: e.tensor_tensor(Yn[:, ft, :], tm[2][:], tm[3][:], ALU.subtract), v2, v3)
            bank_free[br] = [v3]
            bank_free[bi] = [v3]
            yt.append(g2)
        tok_free = Q.last("tensor")
        nt = []
        for c in range(4):
            b = 4 + c
            a = A(lambda e, c=c, o=o, src=src: e.activation(dv[c % 2][:], src[:, c, :], ACT.Copy, scale=col("hd", 4 * o + c)),
                  src_tok[c], Q.last("vector"))
            for ft in range(4):
                for tab, y in ((cs, Yre), (ss, Yn)):
                    t = mm(ps[b][:], y[:, ft, c * 128:(c + 1) * 128], tab[:, ft, :], ft == 0 and tab is cs,
                           ft == 3 and tab is ss, yt, bank_free[b])
            v = V(lambda e, c=c, o=o, b=b: e.scalar_tensor_tensor(dv[c % 2][:], ps[b][:],
                                                                  small[:, 16 + 4 * o + c:17 + 4 * o + c],
                                                                  dv[c % 2][:], ALU.mult, ALU.add), t, a, t_rn_[o])
            bank_free[b] = [v]
            if o == 0:
                v = V(lambda e, c=c: e.tensor_tensor(x1T[:, c, :], x1T[:, c, :], dv[c % 2][:], ALU.mult), v,
                      u_tok[1, c])
                nt.append(v)
            else:
                v = V(lambda e, c=c: e.tensor_tensor(x2T[:, c, :], x2T[:, c, :], dv[c % 2][:], ALU.mult), v,
                      u_tok[2, c])
                a = A(lambda e, c=c: e.activation(obhi[:, c, :], x2T[:, c, :], ACT.Copy), v, y0_done)
                ob_tok = V(lambda e, c=c: e.tensor_tensor(oblo[:, c, :], x2T[:, c, :], obhi[:, c, :].bitcast(F32),
                                                          ALU.subtract), a)
        y_free = Q.last("tensor")
        y0_done = Q.last("vector", "gpsimd")
        src, src_tok = x1T, nt
    hy_done = Q.last("tensor", "vector", "scalar", "gpsimd")

    rt = sb("rt", AR + 64, [128, 8, 4, 64])
    raw = [sb(f"raw{i}", AR + 72 + 2 * i, [128, 512]) for i in range(4)]
    tp = [sb(f"tp{i}", AR + 80 + 2 * i, [128, 512]) for i in range(3)]
    cosv = col("cos", 0, 256).rearrange("p (t d) -> p t d", t=4)
    sinv = col("sin", 0, 256).rearrange("p (t d) -> p t d", t=4)
    for gi, nm in enumerate(("qna", "kna", "qnc", "knc")):
        o, _ = VEC[nm]
        g0 = vec[:, o:o + 64].unsqueeze(1).to_broadcast([128, 4, 64])
        glo = vec[:, o:o + 32].unsqueeze(1).to_broadcast([128, 4, 32])
        ghi = vec[:, o + 32:o + 64].unsqueeze(1).to_broadcast([128, 4, 32])
        G(lambda e, gi=gi, g0=g0: e.tensor_tensor(rt[:, 2 * gi, :, :], cosv, g0, ALU.mult), hy_done, t_vec)
        G(lambda e, gi=gi, ghi=ghi: e.tensor_tensor(rt[:, 2 * gi + 1, :, 0:32], sinv[:, :, 0:32], ghi, ALU.mult))
        G(lambda e, gi=gi, glo=glo: e.tensor_tensor(rt[:, 2 * gi + 1, :, 32:64], sinv[:, :, 32:64], glo, ALU.mult))
    t_rt = Q.last("gpsimd")
    lam = small[:, 40:41]
    v1 = V(lambda e: e.tensor_tensor_reduce(tp[2][:, 0:64], col("lq1", 0, 64), col("lk1", 0, 64), 1.0, 0.0, ALU.mult,
                                            ALU.add, small[:, 36:37]), hy_done)
    v2 = V(lambda e: e.tensor_tensor_reduce(tp[2][:, 64:128], col("lq2", 0, 64), col("lk2", 0, 64), 1.0, 0.0,
                                            ALU.mult, ALU.add, small[:, 37:38]))
    a = A(lambda e: e.activation(small[:, 38:40], small[:, 36:38], ACT.Exp), v1, v2)
    v = V(lambda e: e.tensor_tensor(small[:, 41:42], small[:, 39:40], small[:, 38:39], ALU.subtract), a)
    t_lam = V(lambda e: e.tensor_scalar(lam, small[:, 41:42], LAM0, None, ALU.subtract), v)

    qaT = sb("qaT", AR + 86, [128, 4, S])
    kaT = sb("kaT", AR + 94, [128, 1, S])
    va = sb("va", AR + 96, [128, 4, 128])
    T8 = [sb(f"T8_{i}", AR + 98 + 1.5 * i, [128, 384]) for i in range(3)]
    PT = [sb(f"PT{i}", AR + 102.5 + 1.5 * i, [128, 384]) for i in range(2)]
    maskA = sb("maskA", AR + 105.5, [128, 384])
    st = sb("st", AR + 107, [128, 128])
    qcT = sb("qcT", AR + 107.5, [128, 4, S])
    kcT = sb("kcT", AR + 115.5, [128, 4, S])
    vc = sb("vc", AR + 123.5, [128, 4, 512])
    oahi = sb("oahi", AR + 48, [128, 4, S], F32R)
    oalo = sb("oalo", AR + 56, [128, 4, S], F32R)
    merged = sb("merged", AR + 16, [128, 8, S])
    gate = [sb(f"gate{i}", AR + 32 + 8 * i, [128, 4, S]) for i in range(2)]
    s_m = sem("s_m")
    t_maskA = load(maskA[:], d["maskA"], s_m, hy_done)

    raw_free = [[] for _ in range(4)]
    tp_free = [[] for _ in range(2)]

    def rope(b, p, t, H, ti, dst, toks, key):
        W = H * 64
        hv = lambda ap: ap.rearrange("p (h d) -> p h d", h=H)
        r, q0, q1 = raw[b][:, 0:W], tp[b % 2][:, 0:W], tp[2][:, 0:W]
        s0 = 64 + 16 * b
        ss_, ms_, rs_ = (st[:, s0 + i * 8:s0 + i * 8 + H] for i in (0, 1, 0))
        done = A(lambda e: e.activation(r, p[:, 0:W], ACT.Copy), t, raw_free[b], t_rt)
        a = A(lambda e: e.activation(q0, r, ACT.Square), done, tp_free[b % 2])
        v = V(lambda e: e.tensor_reduce(ss_, hv(q0), AX.X, ALU.add), a)
        g = G(lambda e: e.tensor_scalar(ms_, ss_, 1.0 / 64, EPS, ALU.mult, ALU.add), v)
        g = G(lambda e: e.tensor_tensor(rs_, ms_, col("mhalf", 0, H), ALU.pow), g)
        v = V(lambda e: e.tensor_tensor(hv(r), hv(r), rs_.unsqueeze(2).to_broadcast([128, H, 64]), ALU.mult), g)
        cg = rt[:, 2 * ti, b, :].unsqueeze(1).to_broadcast([128, H, 64])
        sa = rt[:, 2 * ti + 1, b, 0:32].unsqueeze(1).to_broadcast([128, H, 32])
        sb_ = rt[:, 2 * ti + 1, b, 32:64].unsqueeze(1).to_broadcast([128, H, 32])
        r1, r2_ = hv(r)[:, :, 0:32], hv(r)[:, :, 32:64]
        o1, o2 = hv(q1)[:, :, 0:32], hv(q1)[:, :, 32:64]
        G(lambda e: e.tensor_tensor(o1, r2_, sa, ALU.mult), v, Q.last("vector"))
        g = G(lambda e: e.tensor_tensor(o2, r1, sb_, ALU.mult))
        v = V(lambda e: e.tensor_tensor(hv(q0), hv(r), cg, ALU.mult), v)
        v = V(lambda e: e.tensor_tensor(r, q0, q1, ALU.add), v, g)
        tp_free[b % 2] = [v]
        nj = W // 128

        def turn_round():
            for j in range(nj):
                t = tr(ps[6][:, j * 128:(j + 1) * 128], r[:, j * 128:(j + 1) * 128], v, bank_free[6])
            raw_free[b] = [t]
            a = A(lambda e: e.activation(dst[:, :, b * 128:(b + 1) * 128],
                                         ps[6][:, 0:W].rearrange("p (j t) -> p j t", j=nj), ACT.Copy), t, hy_done)
            bank_free[6] = [a]
            toks[key, b] = a

        deferred.append([1 + b if nj > 1 else 2, turn_round])
        return [done]

    ra = {}

    def evac_kva(b, p, t):
        a2 = A(lambda e: e.activation(va[:, b, :], p[:, 128:256], ACT.Copy), t, hy_done)
        return rope(b, p, t, 2, 1, kaT, ra, "k") + [a2]

    gemm("qa", hT, hready, lambda b, p, t: rope(b, p, t, 8, 0, qaT, ra, "q"))
    gemm("kva", hT, hready, evac_kva)

    def att_a():
        units = [(n, h) for n in range(4) for h in range(8)]
        info = {}
        while len(ra) < 8:
            yield
        ra_all = list(ra.values())

        def s1(u):
            n, h = units[u]
            b, j, base, kv = 4 + u % 2, h % 4, 64 * (h // 4), h // 4
            k0, k1 = max(n - 1, 0), min(n + 1, 3)
            W = 128 * (k1 - k0 + 1)
            m0 = 0 if n > 0 else 128
            t = mm(ps[b][:, 0:W], qaT[base:base + 64, j, n * 128:(n + 1) * 128], kaT[base:base + 64, 0, k0 * 128:k0 * 128 + W],
                   True, True, ra_all, bank_free[b])
            T = T8[u % 3]
            c = 24 + 8 * (u % 4)
            prev = info[u - 3]["pt"] if u >= 3 else None
            v = V(lambda e: e.tensor_tensor_reduce(T[:, 0:W], ps[b][:, 0:W], maskA[:, m0:m0 + W], 0.125,
                                                   col("sink", h), ALU.add, ALU.max, st[:, c:c + 1]),
                  t, t_maskA, prev, hy_done)
            bank_free[b] = [v]
            v = V(lambda e: e.tensor_scalar(st[:, c + 1:c + 2], st[:, c:c + 1], -1.0, None, ALU.mult), v)
            a1 = A(lambda e: e.activation(T[:, 0:W], T[:, 0:W], ACT.Exp, bias=st[:, c + 1:c + 2],
                                          accum_out=st[:, c + 2:c + 3]), v)
            a2 = A(lambda e: e.activation(st[:, c + 3:c + 4], col("sink", h), ACT.Exp, bias=st[:, c + 1:c + 2]))
            v = V(lambda e: e.tensor_tensor(st[:, c + 4:c + 5], st[:, c + 2:c + 3], st[:, c + 3:c + 4], ALU.add),
                  a1, a2)
            v = V(lambda e: e.reciprocal(st[:, c + 5:c + 6], st[:, c + 4:c + 5]), v)
            v = V(lambda e: e.tensor_scalar(T[:, 0:W], T[:, 0:W], st[:, c + 5:c + 6], None, ALU.mult), v)
            info[u] = dict(k0=k0, W=W, T=T, tok=v)

        def s2(u):
            i = info[u]
            for k in range(i["W"] // 128):
                t = tr(ps[6][:, k * 128:(k + 1) * 128], i["T"][:, k * 128:(k + 1) * 128], i["tok"], bank_free[6])
            i["pt"] = t
            W = i["W"]
            prev = info[u - 2]["pv"] if u >= 2 else None
            a = A(lambda e: e.activation(PT[u % 2][:, 0:W], ps[6][:, 0:W], ACT.Copy), t, prev, hy_done)
            bank_free[6] = [a]
            i["ev"] = a

        def s3(u):
            n, h = units[u]
            i = info[u]
            j, base, kv = h % 4, 64 * (h // 4), h // 4
            nk = i["W"] // 128
            for k in range(nk):
                t = mm(ps[7][base:base + 64, j * 128:(j + 1) * 128], va[:, i["k0"] + k, kv * 64:kv * 64 + 64],
                       PT[u % 2][:, k * 128:(k + 1) * 128], k == 0, k == nk - 1, i["ev"], bank_free[7])
            i["pv"] = t
            if h == 7:
                hi = oahi[:, :, n * 128:(n + 1) * 128]
                lo = oalo[:, :, n * 128:(n + 1) * 128]
                src = ps[7][:].rearrange("p (j t) -> p j t", j=4)
                a = A(lambda e: e.activation(hi, src, ACT.Copy), t, hy_done)
                v = V(lambda e: e.tensor_tensor(lo, src, hi.bitcast(F32), ALU.subtract), a)
                bank_free[7] = [v]
                info["oa", n] = v

        for u in range(len(units) + 2):
            if u < len(units):
                s1(u)
            if 1 <= u <= len(units):
                s2(u - 1)
            if u >= 2:
                s3(u - 2)
            yield
        oa_tok.extend(info["oa", n] for n in range(4))

    oa_tok = []
    gate_n = [0]
    gate_tok, gate_free, mtok = {}, [[], []], {}

    def gate_group(name):
        i = gate_n[0] % 2
        gate_n[0] += 1

        def evac(b, p, t):
            a = A(lambda e: e.activation(gate[i][:, b, :], p[:], ACT.Tanh, scale=0.5), t, gate_free[i], hy_done)
            gate_tok[i, b] = a
            return [a]
        gemm(name, hT, hready, evac)
        return i

    def branch_group(name, gi, act, ready, half, first):
        def evac(b, p, t):
            m = merged[:, 4 * half + b, :]
            gt = gate[gi][:, b, :]
            if first:
                v = V(lambda e: e.scalar_tensor_tensor(m, gt, 1.0, p[:], ALU.add, ALU.mult), t, gate_tok[gi, b],
                      hy_done)
                mtok[half, b] = v
                return [v]
            v = V(lambda e: e.scalar_tensor_tensor(gt, gt, 1.0, p[:], ALU.add, ALU.mult), t, gate_tok[gi, b])
            mtok[half, b] = G(lambda e: e.tensor_tensor(m, m, gt, ALU.add), v, mtok[half, b])
            return [v]
        gemm(name, act, ready, evac)
        gate_free[gi] = Q.last("vector", "gpsimd")

    background.append(att_a())
    for half in range(2):
        gi = gate_group("gB%d" % half)
        branch_group("bB%d" % half, gi, lambda k: (obhi[:, k, :], oblo[:, k, :]), lambda k: ob_tok, half, True)

    rc = {}

    def evac_vc(b, p, t):
        a = A(lambda e: e.activation(vc[:, b, :], p[:], ACT.Copy), t, hy_done)
        rc["v", b] = a
        return [a]

    gemm("qc", hT, hready, lambda b, p, t: rope(b, p, t, 8, 2, qcT, rc, "q"))
    gemm("kc", hT, hready, lambda b, p, t: rope(b, p, t, 8, 3, kcT, rc, "k"))
    gemm("vc", hT, hready, evac_vc)
    flush()
    drain()
    a_done = Q.last("tensor", "vector", "scalar", "gpsimd")
    rc_all = [rc[k] for k in sorted(rc)]

    Pc = [sb(f"Pc{i}", AR + 72 + 2 * i, [128, 512]) for i in range(4)]
    oc = sb("oc", AR + 82, [128, 512])
    ocs = sb("ocs", AR + 84, [128, 512])
    PTc = [sb(f"PTc{i}", AR + 86 + 2 * i, [128, 512]) for i in range(2)]
    ochi = sb("ochi", AR + 0, [128, 4, S], F32R)
    oclo = sb("oclo", AR + 8, [128, 4, S], F32R)
    oc_tok = {}

    def att_c():
        units = [(n, h) for n in range(4) for h in range(4)]
        info = {}

        def s1(u):
            n, h = units[u]
            prev = info[u - 2]["pt"] if u >= 2 else None
            P2 = [Pc[2 * (u % 2)], Pc[2 * (u % 2) + 1]]
            rr = []
            for c in range(2):
                b = 4 + c
                base = 64 * c
                o = 24 + 16 * (u % 2) + 8 * c
                t = mm(ps[b][:], qcT[base:base + 64, h, n * 128:(n + 1) * 128], kcT[base:base + 64, h, :], True, True,
                       rc_all, bank_free[b])
                v = V(lambda e, b=b, o=o: e.tensor_reduce(st[:, o:o + 1], ps[b][:], AX.X, ALU.max), t, a_done)
                v = V(lambda e, o=o: e.tensor_scalar(st[:, o + 1:o + 2], st[:, o:o + 1], -0.125, None, ALU.mult), v)
                a = A(lambda e, b=b, o=o, c=c: e.activation(P2[c][:], ps[b][:], ACT.Exp, bias=st[:, o + 1:o + 2],
                                                            scale=0.125, accum_out=st[:, o + 2:o + 3]), v, prev, a_done)
                bank_free[b] = [a]
                v = V(lambda e, o=o: e.reciprocal(st[:, o + 3:o + 4], st[:, o + 2:o + 3]), a)
                rr.append(v)
            o = 24 + 16 * (u % 2)
            v1 = V(lambda e: e.tensor_scalar(P2[0][:], P2[0][:], st[:, o + 3:o + 4], None, ALU.mult), rr)
            v2 = V(lambda e: e.tensor_tensor(st[:, o + 12:o + 13], st[:, o + 11:o + 12], lam, ALU.mult), t_lam, rr)
            v = V(lambda e: e.scalar_tensor_tensor(P2[0][:], P2[1][:], st[:, o + 12:o + 13], P2[0][:], ALU.mult,
                                                   ALU.add), v1, v2)
            info[u] = dict(P=P2[0], tok=v)

        def s2(u):
            i = info[u]
            for k in range(4):
                t = tr(ps[6][:, k * 128:(k + 1) * 128], i["P"][:, k * 128:(k + 1) * 128], i["tok"], bank_free[6])
            i["pt"] = t
            a = A(lambda e: e.activation(PTc[u % 2][:], ps[6][:], ACT.Copy), t,
                  info[u - 2]["pv"] if u >= 2 else None, a_done)
            bank_free[6] = [a]
            i["ev"] = a

        def s3(u):
            n, h = units[u]
            i = info[u]
            for k in range(4):
                t = mm(ps[7][:, h * 128:(h + 1) * 128], PTc[u % 2][:, k * 128:(k + 1) * 128],
                       vc[:, k, h * 128:(h + 1) * 128], k == 0, k == 3, i["ev"], bank_free[7])
            i["pv"] = t
            if h == 3:
                hv = lambda ap: ap.rearrange("p (h d) -> p h d", h=4)
                a = A(lambda e: e.activation(oc[:], ps[7][:], ACT.Square), t, a_done, Q.last("vector"))
                v = V(lambda e: e.tensor_reduce(st[:, 100:104], hv(oc[:]), AX.X, ALU.add), a)
                g = G(lambda e: e.tensor_scalar(st[:, 104:108], st[:, 100:104], 1.0 / 128, EPS, ALU.mult, ALU.add), v)
                g = G(lambda e: e.tensor_tensor(st[:, 108:112], st[:, 104:108], col("mhalf", 0, 4), ALU.pow), g)
                g = G(lambda e: e.tensor_scalar(st[:, 112:116], st[:, 108:112], 1.0 - LAM0, 0.0, ALU.mult, ALU.add), g)
                v = V(lambda e: e.tensor_tensor(hv(ocs[:]), hv(ps[7][:]),
                                                st[:, 112:116].unsqueeze(2).to_broadcast([128, 4, 128]), ALU.mult),
                      g, Q.last("tensor"))
                bank_free[7] = [v]
                info["ocs"] = (n, v)

        def s4():
            n, v = info.pop("ocs")
            for k in range(4):
                t = tr(ps[6][:, k * 128:(k + 1) * 128], ocs[:, k * 128:(k + 1) * 128], v, bank_free[6])
            src = ps[6][:].rearrange("p (j t) -> p j t", j=4)
            hi, lo = ochi[:, :, n * 128:(n + 1) * 128], oclo[:, :, n * 128:(n + 1) * 128]
            a = A(lambda e: e.activation(hi, src, ACT.Copy, scale=col("subln")), t, a_done)
            oc_tok[n] = V(lambda e: e.scalar_tensor_tensor(lo, src, col("subln"), hi.bitcast(F32), ALU.mult,
                                                           ALU.subtract), a)
            bank_free[6] = [oc_tok[n]]

        for u in range(len(units) + 3):
            if u < len(units):
                s1(u)
            if 1 <= u <= len(units):
                s2(u - 1)
            if "ocs" in info:
                s4()
            if 2 <= u < len(units) + 2:
                s3(u - 2)
            yield

    background.append(att_c())
    for half in range(2):
        gi = gate_group("gA%d" % half)
        branch_group("bA%d" % half, gi, lambda k: (oahi[:, k, :], oalo[:, k, :]), lambda k: oa_tok, half, False)
    gis = [gate_group("gC%d" % half) for half in range(2)]
    drain()
    h_free1 = Q.last("tensor")
    oct = [oc_tok[n] for n in range(4)]
    x = sb("x", AR + 88, [128, 4, D])
    c_done = Q.last("tensor", "vector", "scalar", "gpsimd")
    tx2 = load(x[:], x_dram, s_x, c_done)
    m_ready = {}
    for half in range(2):
        def evac(b, p, t, half=half):
            gi = gis[half]
            k = 4 * half + b
            m, gt = merged[:, k, :], gate[gi][:, b, :]
            v = V(lambda e: e.scalar_tensor_tensor(gt, gt, 1.0, p[:], ALU.add, ALU.mult), t, gate_tok[gi, b])
            g = G(lambda e: e.tensor_tensor(m, m, gt, ALU.add), v, mtok[half, b])
            a = A(lambda e: e.activation(hThi[:, k, :], m, ACT.Copy, scale=0.5), g, h_free1)
            m_ready[k] = V(lambda e: e.scalar_tensor_tensor(hTlo[:, k, :], m, 0.5, hThi[:, k, :].bitcast(F32),
                                                            ALU.mult, ALU.subtract), a)
            return [v]
        gemm("bC%d" % half, lambda k: (ochi[:, k, :], oclo[:, k, :]), lambda k: oct, evac)

    xs = sb("xs", AR + 16, [128, 4, D])
    junk = sb("junk", AR + 130, [128, 512])

    def residual(names, act, ready, junk_free=None):
        toks = {}
        for half in range(2):
            def evac(b, p, t, half=half):
                xa = x[:, b, half * 512:half * 512 + 512]
                v = V(lambda e: e.tensor_tensor(xa, p[:], xa, ALU.add), t, tx2)
                toks[half, b] = half_square(x, b, half, junk[:], v, junk_free)
                return [v]
            gemm(names % half, act, ready, evac, banks=1)
        return [[toks[0, b], toks[1, b]] for b in range(4)]

    xt = residual("wo%d", hT, lambda k: m_ready[k], Q.last("tensor", "vector", "scalar", "gpsimd"))

    achi = sb("achi", AR + 0, [128, 22, S], F32R)
    aclo = sb("aclo", AR + 44, [128, 22, S], F32R)
    ft = [sb(f"ft{i}", AR + 104 + 2 * i, [128, S]) for i in range(8)]
    ft_free = [[] for _ in range(8)]

    def ffn(tag, conv):
        a_free = Q.last("tensor", "vector", "scalar", "gpsimd")
        ready = {}
        for j in range(11):
            pend = {}

            def evac(b, p, t, j=j):
                f = 2 * j + b % 2
                i = 4 * (j % 2) + b
                if conv:
                    c = f + 22 * (b // 2)
                    dst = ft[i]
                    a = A(lambda e: e.activation(dst[:], p[:], ACT.Identity, bias=col("cb2", c),
                                                 scale=col("cw2", 88 + c)), t, a_free, ft_free[i])
                    v = V(lambda e: e.scalar_tensor_tensor(dst[:, 1:S], p[:, 0:S - 1], col("cw2", 44 + c),
                                                           dst[:, 1:S], ALU.mult, ALU.add), a)
                    v = V(lambda e: e.scalar_tensor_tensor(dst[:, 2:S], p[:, 0:S - 2], col("cw2", c),
                                                           dst[:, 2:S], ALU.mult, ALU.add), v)
                    free = [v]
                    if b < 2:
                        pend[b] = A(lambda e: e.activation(dst[:], dst[:], ACT.Silu), v)
                    else:
                        g = ft[i - 2]
                        v = V(lambda e: e.tensor_tensor(g[:], g[:], dst[:], ALU.mult), v, pend[b - 2])
                else:
                    if b < 2:
                        pend[b] = A(lambda e: e.activation(ft[i][:], p[:], ACT.Silu), t, a_free, ft_free[i])
                        free = [pend[b]]
                    else:
                        g = ft[i - 2]
                        v = V(lambda e: e.tensor_tensor(g[:], g[:], p[:], ALU.mult), t, pend[b - 2])
                        free = [v]
                if b >= 2:
                    g = ft[i - 2]
                    a = A(lambda e: e.activation(achi[:, f, :], g[:], ACT.Copy), v, a_free)
                    ready[f] = V(lambda e: e.tensor_tensor(aclo[:, f, :], g[:], achi[:, f, :].bitcast(F32),
                                                           ALU.subtract), a)
                    ft_free[i] = [ready[f]]
                    ft_free[i - 2] = [ready[f]]
                return free
            gemm("%s%d" % (tag, j), hT, hready, evac, banks=1)
        return lambda k: (achi[:, k, :], aclo[:, k, :]), lambda k: ready[k]

    norm(x, xs, "g2", xt, Q.last("tensor"), Q.last("tensor", "vector", "scalar", "gpsimd"))
    act, ready = ffn("up", False)
    xt = residual("dn%d", act, ready)

    norm(x, xs, "g3", xt, Q.last("tensor"), Q.last("tensor", "vector", "scalar", "gpsimd"))
    b2 = Q.last("tensor", "vector", "scalar", "gpsimd")
    sqT = sb("sqT", AR + 0, [128, 4, S])
    skT = sb("skT", AR + 8, [128, 4, S])
    sv = sb("sv", AR + 16, [128, 4, 512])
    ohi = sb("ohi", AR + 24, [128, 8, S], F32R)
    olo = sb("olo", AR + 40, [128, 8, S], F32R)
    Qf = sb("Qf", AR + 56, [66, 8, S])
    Kf = sb("Kf", AR + 72, [66, 8, S])
    fv = sb("fv", AR + 104, [128, 4, 512])
    W5 = [sb(f"W5_{i}", AR + 112 + 2 * i, [128, 512]) for i in range(6)]
    PT2 = [sb(f"PT2_{i}", AR + 124 + 2 * i, [128, 512]) for i in range(2)]
    mk = sb("mk", AR + 128, [128, 640])
    st2 = sb("st2", AR + 130.5, [128, 96])
    s_mk = sem("s_mk")
    t_mk = load(mk[:], d["mask2"], s_mk, b2)
    r2 = {}

    def copy_evac(dst, key, scale):
        def evac(b, p, t):
            a = A(lambda e: e.activation(dst[:, b, :], p[:], ACT.Copy, scale=scale), t, b2)
            r2[key, b] = a
            return [a]
        return evac

    gemm("sq", hT, hready, copy_evac(sqT, "sq", 0.125))
    gemm("sk", hT, hready, copy_evac(skT, "sk", 1.0))
    gemm("sv", hT, hready, copy_evac(sv, "sv", 1.0))
    rs = [r2[k] for k in sorted(r2)]
    o_tok = {}

    def out_norm(n, src, j0, gname, key, *after):
        a = A(lambda e: e.activation(W5[4][:], src, ACT.Square, accum_out=st2[:, 80:81]), *after, Q.last("vector", "tensor"))
        g = G(lambda e: e.tensor_scalar(st2[:, 81:82], st2[:, 80:81], 1.0 / 512, EPS, ALU.mult, ALU.add), a)
        g = G(lambda e: e.tensor_tensor(st2[:, 82:83], st2[:, 81:82], col("mhalf"), ALU.pow), g)
        v = V(lambda e: e.tensor_scalar(W5[5][:], src, st2[:, 82:83], None, ALU.mult), g, Q.last("tensor"))

        def later():
            for k in range(4):
                t = tr(ps[6][:, k * 128:(k + 1) * 128], W5[5][:, k * 128:(k + 1) * 128], v, bank_free[6])
            fr = []
            for k in range(4):
                hi = ohi[:, j0 + k, n * 128:(n + 1) * 128]
                lo = olo[:, j0 + k, n * 128:(n + 1) * 128]
                p = ps[6][:, k * 128:(k + 1) * 128]
                a = A(lambda e, hi=hi, p=p, k=k: e.activation(hi, p, ACT.Copy, scale=col(gname, k)), t, b2, fr)
                fr = [a]
            for k in range(4):
                hi = ohi[:, j0 + k, n * 128:(n + 1) * 128]
                lo = olo[:, j0 + k, n * 128:(n + 1) * 128]
                p = ps[6][:, k * 128:(k + 1) * 128]
                w = V(lambda e, hi=hi, lo=lo, p=p, k=k: e.scalar_tensor_tensor(lo, p, col(gname, k), hi.bitcast(F32),
                                                                              ALU.mult, ALU.subtract), a)
            o_tok[key, n] = w
            bank_free[6] = [w]
        return v, later

    def att_s():
        units = [(n, h) for n in range(4) for h in range(8)]
        info = {}
        pend = []

        def s1(u):
            n, h = units[u]
            b, base, j = 4 + u % 2, 64 * (h % 2), h // 2
            W = 128 * (n + 1)
            i0 = 2 * (u % 2)
            nr, L = W5[i0], W5[i0 + 1]
            mm(ps[b][:, 0:W], sqT[base:base + 64, j, n * 128:(n + 1) * 128], skT[base:base + 64, j, 0:W],
               True, False, rs, bank_free[b])
            t = mm(ps[b][:, n * 128:W], ident, mk[:, 512:640], False, True, t_mk)
            prev = info[u - 2]["pt"] if u >= 2 else None
            a = A(lambda e: e.activation(L[:, 0:W], ps[b][:, 0:W], ACT.Abs), t, prev, b2)
            v = V(lambda e: e.tensor_scalar(nr[:, 0:W], ps[b][:, 0:W], -1.0, 0.0, ALU.mult, ALU.min), a)
            a = A(lambda e: e.activation(L[:, 0:W], L[:, 0:W], ACT.Exp, scale=-1.0), a)
            a = A(lambda e: e.activation(L[:, 0:W], L[:, 0:W], ACT.Ln, bias=col("one")), a)
            v = V(lambda e: e.tensor_tensor_scan(nr[:, 0:W][:, ::-1], nr[:, 0:W][:, ::-1], L[:, 0:W][:, ::-1], 0.0,
                                                 ALU.add, ALU.subtract), v, a)
            v = V(lambda e: e.tensor_tensor(L[:, 0:W], ps[b][:, 0:W], nr[:, 0:W], ALU.add), v)
            bank_free[b] = [v]
            a = A(lambda e: e.activation(L[:, 0:W], L[:, 0:W], ACT.Exp), v)
            info[u] = dict(T=L, tok=a, W=W)

        def s2(u):
            i = info[u]
            W = i["W"]
            for k in range(W // 128):
                t = tr(ps[6][:, k * 128:(k + 1) * 128], i["T"][:, k * 128:(k + 1) * 128], i["tok"], bank_free[6])
            i["pt"] = t
            v = V(lambda e: e.tensor_copy(PT2[u % 2][:, 0:W], ps[6][:, 0:W]), t,
                  info[u - 2]["pv"] if u >= 2 else None, b2)
            bank_free[6] = [v]
            i["ev"] = v

        def s3(u):
            n, h = units[u]
            i = info[u]
            for k in range(n + 1):
                t = mm(ps[7][:, h * 64:(h + 1) * 64], PT2[u % 2][:, k * 128:(k + 1) * 128],
                       sv[:, k, h * 64:(h + 1) * 64], k == 0, k == n, i["ev"], bank_free[7])
            i["pv"] = t
            if h == 7:
                v, later = out_norm(n, ps[7][:], 4, "gsb", "s", t)
                bank_free[7] = [v]
                pend.append(later)

        for u in range(len(units) + 3):
            if u < len(units):
                s1(u)
            if 1 <= u <= len(units):
                s2(u - 1)
            if pend:
                pend.pop()()
            if 2 <= u < len(units) + 2:
                s3(u - 2)
            yield

    fz = [sb(f"fz{i}", AR + 88 + 2 * i, [8, S]) for i in range(0)]
    fw = [W5[i] for i in range(4)]
    s_F = sem("s_F")
    fF = {}

    def evac_fl(b, p, t):
        z, e_, m_, s_ = (w[0:8, :] for w in fw)
        v = V(lambda e: e.tensor_scalar(z, p[0:8, :], col("fb", p=8), None, ALU.add), t, b2)
        a = A(lambda e: e.activation(e_, z, ACT.Abs), v)
        a = A(lambda e: e.activation(e_, e_, ACT.Exp, scale=-1.0), a)
        a = A(lambda e: e.activation(e_, e_, ACT.Ln, bias=col("one", p=8)), a)
        v2 = V(lambda e: e.tensor_scalar(m_, z, 0.0, None, ALU.min), v)
        v3 = V(lambda e: e.tensor_tensor_scan(s_, m_, e_, 0.0, ALU.add, ALU.subtract), v2, a)
        v4 = V(lambda e: e.tensor_scalar(z, s_, 8.0, None, ALU.mult), v3)
        v5 = V(lambda e: e.tensor_scalar(m_, s_, -8.0, None, ALU.mult), v3)
        m1 = V(lambda e: e.memset(Qf[64:66, :, :], 1.0), b2)
        m2 = V(lambda e: e.memset(Kf[64:66, :, :], 1.0))
        fF[0] = load(Qf[65:66, :, :], z, s_F, v4, m1)
        fF[1] = load(Kf[64:65, :, :], m_, s_F, v5, m2)
        return [v]

    A(lambda e: e.preload_act_table_set("natural_log_exp_and_others"), b2)
    gemm("fl", hT, hready, evac_fl)
    W5_guard = [fF[0], fF[1]]
    b2 = b2 + W5_guard
    background.append(att_s())

    def head_evac(dst, key):
        def evac(b, p, t):
            a = A(lambda e: e.activation(dst[0:64, 2 * b, :], p[0:64, :], ACT.Copy), t, b2)
            a2 = A(lambda e: e.activation(dst[0:64, 2 * b + 1, :], p[64:128, :], ACT.Copy))
            r2[key, b] = a2
            return [a2]
        return evac

    gemm("fq", hT, hready, head_evac(Qf, "fq"), rate=2)
    gemm("fk", hT, hready, head_evac(Kf, "fk"), rate=2)
    gemm("fv", hT, hready, copy_evac(fv, "fv", 1.0), rate=2)
    drain()
    rf = [r2[k, b] for k in ("fq", "fk", "fv") for b in range(4)] + [fF[0], fF[1]]
    s_done = Q.last("tensor", "vector", "scalar", "gpsimd")

    def att_f():
        units = [(n, h) for n in range(4) for h in range(8)]
        info = {}
        pend = []

        def s1(u):
            n, h = units[u]
            b = 4 + u % 2
            W = 128 * (n + 1)
            T = W5[u % 3]
            t = mm(ps[b][:, 0:W], Qf[:, h, n * 128:(n + 1) * 128], Kf[:, h, 0:W], True, True, rf, bank_free[b])
            c = 4 * (u % 4)
            m0 = 128 * (3 - n)
            v = V(lambda e: e.tensor_tensor_reduce(T[:, 0:W], ps[b][:, 0:W], mk[:, m0:m0 + W], 0.125, -3e38, ALU.add,
                                                   ALU.max, st2[:, c:c + 1]), t, t_mk, s_done,
                  info[u - 3]["pt"] if u >= 3 else None)
            bank_free[b] = [v]
            v = V(lambda e: e.tensor_scalar(st2[:, c + 1:c + 2], st2[:, c:c + 1], -1.0, None, ALU.mult), v)
            sm = st2[:, 16 + 8 * (n % 2) + h:17 + 8 * (n % 2) + h]
            a = A(lambda e: e.activation(T[:, 0:W], T[:, 0:W], ACT.Exp, bias=st2[:, c + 1:c + 2], accum_out=sm), v)
            info[u] = dict(T=T, tok=a, W=W)

        def s2(u):
            i = info[u]
            W = i["W"]
            for k in range(W // 128):
                t = tr(ps[6][:, k * 128:(k + 1) * 128], i["T"][:, k * 128:(k + 1) * 128], i["tok"], bank_free[6])
            i["pt"] = t
            v = V(lambda e: e.tensor_copy(PT2[u % 2][:, 0:W], ps[6][:, 0:W]), t,
                  info[u - 2]["pv"] if u >= 2 else None, s_done)
            bank_free[6] = [v]
            i["ev"] = v

        def s3(u):
            n, h = units[u]
            i = info[u]
            for k in range(n + 1):
                t = mm(ps[7][:, h * 64:(h + 1) * 64], PT2[u % 2][:, k * 128:(k + 1) * 128],
                       fv[:, k, h * 64:(h + 1) * 64], k == 0, k == n, i["ev"], bank_free[7])
            i["pv"] = t
            if h == 7:
                c = 16 + 8 * (n % 2)
                v = V(lambda e: e.reciprocal(st2[:, 40:48], st2[:, c:c + 8]), i["tok"])
                v = V(lambda e: e.tensor_tensor(W5[3][:].rearrange("p (h d) -> p h d", h=8),
                                                ps[7][:].rearrange("p (h d) -> p h d", h=8),
                                                st2[:, 40:48].unsqueeze(2).to_broadcast([128, 8, 64]), ALU.mult),
                      v, t, Q.last("scalar", "tensor"))
                bank_free[7] = [v]
                v, later = out_norm(n, W5[3][:], 0, "gfox", "f", v)
                pend.append(later)

        for u in range(len(units) + 3):
            if u < len(units):
                s1(u)
            if 1 <= u <= len(units):
                s2(u - 1)
            if pend:
                pend.pop()()
            if 2 <= u < len(units) + 2:
                s3(u - 2)
            yield

    background.append(att_f())
    drain()
    ot = [o_tok[k] for k in sorted(o_tok)]
    xt = residual("xo%d", lambda k: (ohi[:, k, :], olo[:, k, :]), lambda k: ot)
    norm(x, xs, "g4", xt, Q.last("tensor"), Q.last("tensor", "vector", "scalar", "gpsimd"))
    act, ready = ffn("vp", True)
    fg = sb("fg", AR + 104, [128, D])
    s_fg = sem("s_fg")
    t_fg = load(fg[:], d["fg"], s_fg, Q.last("tensor", "vector", "scalar", "gpsimd"))
    xt = residual("vd%d", act, ready)

    fin = Q.last("tensor", "vector", "scalar", "gpsimd")
    s_out = sem("s_out")
    o_dram = out.rearrange("b (i p) c -> p (b i) c", p=128)
    for i in range(4):
        g = row_rstd(i, xt[i])
        v = V(lambda e, i=i: e.scalar_tensor_tensor(xs[:, i, :], x[:, i, :], small[:, 8 + i:9 + i], fg[:], ALU.mult,
                                                    ALU.mult), g, t_fg, fin)
        t_out = load(o_dram[:, i, :], xs[:, i, :], s_out, v)
    t_out.used = True
    assert state["split"] == n_slots
    Q.number()

    with nc.Block() as block:
        @block.sync
        def _(e):
            Q.run("sync", e)
            e.wait_ge(s_out, 64)

        @block.tensor
        def _(e):
            Q.run("tensor", e)

        @block.vector
        def _(e):
            Q.run("vector", e)

        @block.scalar
        def _(e):
            Q.run("scalar", e)

        @block.gpsimd
        def _(e):
            Q.run("gpsimd", e)


def _tables():
    f = np.float32
    t = {}
    pos = np.arange(S, dtype=f)
    inv = f(10000.0) ** (-np.arange(0, 64, 2, dtype=f) / f(64))
    ang = pos[:, None] * inv[None, :]
    c, s = np.cos(ang).astype(f), np.sin(ang).astype(f)
    tile = lambda a: np.ascontiguousarray(a.reshape(4, 128, -1).transpose(1, 0, 2))
    t["cos"] = tile(np.concatenate([c, c], 1)).reshape(128, 256)
    t["sin"] = tile(np.concatenate([-s, s], 1)).reshape(128, 256)
    tt = pos / f(S - 1)
    bands = np.arange(1, 17, dtype=f)
    a2 = (f(2.0 * math.pi) * pos[:, None] * bands[None, :] / f(S)).astype(f)
    z = np.concatenate([tt[:, None], np.cos(a2), np.sin(a2)], -1).astype(f)
    t["zT"] = np.ascontiguousarray(z.T)
    deltas = np.abs(np.linspace(math.log(1e-2) / 1.5, math.log(1e-2) / 0.3, 512, dtype=f))
    t["dec"] = tile(np.exp(-tt[:, None] * deltas[None, :]).astype(f))
    m = np.arange(S, dtype=np.int64)
    ph = (np.outer(m, 2 * m + 1) % 2048) * (math.pi / 1024)
    t["cu"], t["su"] = tile(np.cos(ph).astype(f)), tile(-np.sin(ph).astype(f))
    ph = (np.outer(2 * m + 1, 2 * m + 1) % 4096) * (math.pi / 2048)
    t["cs"], t["ss"] = tile(np.cos(ph).astype(f)), tile(np.sin(ph).astype(f))
    i, j = np.arange(128)[:, None], np.arange(128)[None, :]
    zero = np.zeros((128, 128), f)
    n = f(NEG)
    t["maskA"] = np.concatenate([np.where(j >= i, f(0), n), zero, np.where(j <= i, f(0), n)], 1).astype(f)
    t["mask2"] = np.concatenate([zero, zero, zero, np.where(j <= i, f(0), n), np.where(j < i, f(0), n)], 1).astype(f)
    return t


def _layout(inp):
    f = np.float32
    g = {k: np.asarray(v) for k, v in inp.items()}
    tb = _tables()
    VEC, NV = vec_layout()
    vec = np.zeros((128, NV), f)

    def put(name, a, p=128):
        o, w = VEC[name]
        vec[0:p, o:o + w] = a

    cols = lambda v: v.reshape(-1, 128).T
    row = lambda v: np.broadcast_to(v.reshape(1, -1), (128, v.size))
    put("g1", cols(g["norm1_g"]))
    put("g2", cols(g["norm2_g"]))
    put("g3", cols(g["attn_norm_g_2"]))
    put("g4", cols(g["ffn_norm_g_2"]))
    put("cw", cols(g["conv_w"]))
    put("cb", cols(g["conv_b"]))
    put("hd", cols(g["hy_d"]))
    put("gfox", cols(g["fox_out_g_2"]))
    put("gsb", cols(g["sb_out_g_2"]))
    put("cw2", cols(g["conv_w_2"]))
    put("cb2", cols(g["conv_b_2"]))
    put("subln", cols(g["subln_c"]))
    put("sink", row(g["sink_a"]))
    put("fb", g["forget_bias_2"].reshape(8, 1), 8)
    for a, b in (("b1", "filt_b1"), ("f1", "filt_f1"), ("b2", "filt_b2"), ("f2", "filt_f2")):
        put(a, g[b].reshape(64, 1), 64)
    for a, b in (("qna", "qn_a"), ("kna", "kn_a"), ("qnc", "qn_c"), ("knc", "kn_c"), ("lq1", "lam_q1"),
                 ("lk1", "lam_k1"), ("lq2", "lam_q2"), ("lk2", "lam_k2")):
        put(a, row(g[b]))
    put("ident", np.eye(128, dtype=f))
    put("one", 1.0)
    put("half", 0.5)
    put("mhalf", -0.5)
    put("wS0", 0.5)
    put("wD0", 0.5)
    vec[0, VEC["wS0"][0]] = 1.0
    vec[0, VEC["wD0"][0]] = 0.0
    put("cos", tb.pop("cos"))
    put("sin", tb.pop("sin"))
    put("w1", g["filt_w1"][0], 33)
    put("w2", g["filt_w2"][0], 64)

    TABLE, OFFS, total = slot_table()
    ws = np.empty(total, f)

    def pack(name, w):
        first, n_s, n, _ = TABLE[name]
        a = w.reshape(n_s, 2, 128, n).transpose(0, 2, 1, 3)
        o = OFFS[first][0]
        ws[o:o + a.size] = np.ascontiguousarray(a).reshape(-1)

    w = g["w_in"][0]
    perm = [0, 4, 1, 5, 2, 6, 3, 7]
    hp = np.concatenate([np.arange(h * 64, h * 64 + 64) for h in perm])
    pack("qa", w[:, :512][:, hp])
    pack("kva", w[:, 512:768])
    for i in range(3):
        pack("hy%d" % i, w[:, 768 + 512 * i:1280 + 512 * i])
    for i, nm in enumerate(("qc", "kc", "vc")):
        pack(nm, w[:, 2304 + 512 * i:2816 + 512 * i])
    for i, nm in enumerate(("gA", "gB", "gC")):
        for j in range(2):
            o = 3840 + 1024 * i + 512 * j
            pack("%s%d" % (nm, j), w[:, o:o + 512])
    for nm, src in (("bA", g["w_oa"][0][hp]), ("bB", g["w_ob"][0]), ("bC", g["w_oc"][0]), ("wo", g["w_out"][0]),
                    ("dn", g["ffn_w2"][0]), ("xo", g["w_out_2"][0]), ("vd", g["w_down_2"][0])):
        for j in range(2):
            pack("%s%d" % (nm, j), src[:, 512 * j:512 * j + 512])
    for tag, a, b in (("up", g["ffn_w1"][0], g["ffn_w3"][0]),
                      ("vp", g["w_up_2"][0][:, :2816], g["w_up_2"][0][:, 2816:])):
        for j in range(11):
            c = slice(256 * j, 256 * j + 256)
            pack("%s%d" % (tag, j), np.concatenate([a[:, c], b[:, c]], 1))
    w = g["w_in_2"][0]
    for nm, o in (("fq", 0), ("fk", 512), ("fv", 1024), ("sq", 1544), ("sk", 2056), ("sv", 2568)):
        pack(nm, w[:, o:o + 512])
    pad = np.zeros((1024, 128), f)
    pad[:, 0:8] = w[:, 1536:1544]
    pack("fl", pad)
    arrays = dict(tb)
    arrays["vec"] = vec
    arrays["ws"] = ws
    arrays["x"] = g["x"]
    arrays["w3"] = g["filt_w3"][0]
    arrays["fg"] = np.ascontiguousarray(row(g["final_norm_g_2"]))
    return {k: np.ascontiguousarray(v) for k, v in arrays.items()}


def kernel(**inputs):
    import concourse.bacc as bacc
    from concourse.bass_utils import run_bass_kernel_spmd

    nc = bacc.Bacc("TRN2", target_bir_lowering=False, num_devices=1)
    arrays = _layout(inputs)
    d = {k: nc.dram_tensor("in_" + k, a.shape, F32, kind="ExternalInput").ap() for k, a in arrays.items()}
    out = nc.dram_tensor("out", (1, S, D), F32, kind="ExternalOutput").ap()
    build(nc, d, out)
    r = run_bass_kernel_spmd(nc, [{"in_" + k: a for k, a in arrays.items()}], core_ids=[0])
    return r.results[0]["out"]
```

```python
import math
import numpy as np
import concourse.bass as bass
from concourse import mybir

F32 = mybir.dt.float32
F32R = mybir.dt.float32r
ALU = mybir.AluOpType
ACT = mybir.ActivationFunctionType
AX = mybir.AxisListType

S = 512
D = 1024
NEG = -1e30
EPS = 1e-6
LAM0 = 0.2
RAW, HL, LA = 3, 3, 2


def vec_layout():
    names = [
        ("g1", 8), ("g2", 8), ("g3", 8), ("g4", 8), ("cw", 36), ("cb", 12), ("hd", 8), ("gfox", 4), ("gsb", 4),
        ("cw2", 132), ("cb2", 44), ("subln", 1), ("sink", 8), ("fb", 1), ("b1", 1), ("f1", 1), ("b2", 1), ("f2", 1),
        ("qna", 64), ("kna", 64), ("qnc", 64), ("knc", 64), ("lq1", 64), ("lk1", 64), ("lq2", 64), ("lk2", 64),
        ("ident", 128), ("one", 1), ("wS0", 1), ("wD0", 1), ("half", 1), ("mhalf", 8), ("cos", 256), ("sin", 256),
        ("w1", 64), ("w2", 64),
    ]
    at, o = {}, 0
    for n, w in names:
        at[n] = (o, w)
        o += w
    return at, o


def groups():
    out = []
    for i in range(3):
        out.append(("hy%d" % i, 8, 512, "feat"))
    out += [("gB0", 8, 512, "feat"), ("gB1", 8, 512, "feat"), ("qa", 8, 512, "tok"), ("kva", 8, 256, "tok"),
            ("bB0", 4, 512, "feat"), ("bB1", 4, 512, "feat"), ("qc", 8, 512, "tok"), ("kc", 8, 512, "tok"),
            ("vc", 8, 512, "tok"), ("gA0", 8, 512, "feat"), ("gA1", 8, 512, "feat"), ("bA0", 4, 512, "feat"),
            ("bA1", 4, 512, "feat"), ("gC0", 8, 512, "feat"), ("gC1", 8, 512, "feat"), ("bC0", 4, 512, "feat"),
            ("bC1", 4, 512, "feat"), ("wo0", 8, 512, "tok"), ("wo1", 8, 512, "tok")]
    for i in range(11):
        out.append(("up%d" % i, 8, 512, "feat"))
    out += [("dn0", 22, 512, "tok"), ("dn1", 22, 512, "tok")]
    out += [("sq", 8, 512, "feat"), ("sk", 8, 512, "feat"), ("sv", 8, 512, "tok"), ("fl", 8, 128, "feat"),
            ("fq", 8, 512, "feat"), ("fk", 8, 512, "feat"), ("fv", 8, 512, "tok"),
            ("xo0", 8, 512, "tok"), ("xo1", 8, 512, "tok")]
    for i in range(11):
        out.append(("vp%d" % i, 8, 512, "feat"))
    out += [("vd0", 22, 512, "tok"), ("vd1", 22, 512, "tok")]
    return out


def slot_table():
    table, offs, o = {}, [], 0
    for name, nk, n, mode in groups():
        first = len(offs)
        for _ in range(nk // 2):
            offs.append((o, 2 * n))
            o += 128 * 2 * n
        table[name] = (first, nk // 2, n, mode)
    return table, offs, o


class Item:
    def __init__(self, eng, fn, after, sem=None):
        self.eng, self.fn, self.after, self.sem = eng, fn, after, sem
        self.used, self.value = False, 0


def flat(xs):
    for x in xs:
        if x is None:
            continue
        if isinstance(x, (list, tuple)):
            yield from flat(x)
        else:
            yield x


class Queues:
    IN_ORDER = ("vector", "scalar", "gpsimd")
    ENGINES = ("tensor", "vector", "scalar", "gpsimd", "sync")

    def __init__(self, nc):
        self.nc = nc
        self.q = {e: [] for e in self.ENGINES}
        self.sem = {e: nc.alloc_semaphore("done_" + e) for e in self.ENGINES[:4]}
        self.dma_count = {}

    def put(self, eng, fn, after):
        it = Item(eng, fn, list(flat(after)))
        if eng in self.IN_ORDER and self.q[eng]:
            it.after.append(self.q[eng][-1])
        for a in it.after:
            a.used = True
        self.q[eng].append(it)
        return it

    def dma(self, eng, out, in_, sem, after):
        it = Item(eng, lambda e: e.dma_start(out, in_), list(flat(after)), sem)
        for a in it.after:
            a.used = True
        n = self.dma_count.get(id(sem), 0) + 16
        self.dma_count[id(sem)] = n
        it.value = n
        self.q[eng].append(it)
        return it

    def last(self, *engs):
        return [self.q[e][-1] for e in engs if self.q[e]]

    def number(self):
        for e in self.ENGINES[:4]:
            n = 0
            for it in self.q[e]:
                if it.sem is None and it.used:
                    n += 1
                    it.value = n

    def run(self, name, eng):
        seen = {}
        for it in self.q[name]:
            need = {}
            for a in it.after:
                sem = a.sem if a.sem is not None else self.sem[a.eng]
                if a.value > need.get(id(sem), (0, None))[0]:
                    need[id(sem)] = (a.value, sem)
            for k, (v, sem) in need.items():
                if seen.get(k, 0) < v:
                    eng.wait_ge(sem, v)
                    seen[k] = v
            ins = it.fn(eng)
            if it.sem is not None:
                ins.then_inc(it.sem, 16)
            elif it.used:
                ins.then_inc(self.sem[name], 1)


def build(nc, d, out):
    B0 = 16512
    VEC, NV = vec_layout()
    TABLE, OFFS, _ = slot_table()

    def sb(name, kb, shape, dt=F32):
        return nc.alloc_sbuf_tensor_at(name, shape, dt, offset=B0 + int(kb * 1024))

    AR = 75
    hThi = sb("hThi", 0, [128, 8, S], F32R)
    hTlo = sb("hTlo", 16, [128, 8, S], F32R)
    wraw = [sb(f"wraw{i}", 32 + 4 * i, [128, 1024]) for i in range(RAW)]
    whi = [sb(f"whi{i}", 44 + 4 * i, [128, 1024], F32R) for i in range(HL)]
    wlo = [sb(f"wlo{i}", 56 + 4 * i, [128, 1024], F32R) for i in range(HL)]
    vec = sb("vec", 68, [128, NV])
    ps = [nc.alloc_psum_tensor(f"ps{i}", [128, 512], F32) for i in range(8)]
    bank_free = [[] for _ in range(8)]

    Q = Queues(nc)

    def V(fn, *after):
        return Q.put("vector", fn, after)

    def A(fn, *after):
        return Q.put("scalar", fn, after)

    def G(fn, *after):
        return Q.put("gpsimd", fn, after)

    def P(fn, *after):
        return Q.put("tensor", fn, after)

    def sem(name):
        return nc.alloc_semaphore(name)

    def load(out_, in_, s, *after, eng="sync"):
        return Q.dma(eng, out_, in_, s, after)

    def col(name, i=0, n=1, p=128):
        o, _ = VEC[name]
        return vec[0:p, o + i:o + i + n]

    ident = col("ident", 0, 128)

    s_vec = sem("s_vec")
    t_vec = load(vec[:], d["vec"], s_vec)

    s_raw = [sem(f"s_raw{i}") for i in range(RAW)]
    dma_tok, hi_tok, lo_tok, pe_tok = {}, {}, {}, {}
    n_slots = len(OFFS)
    state = {"dma": 0, "split": 0}

    def raw_view(i):
        o, w = OFFS[i]
        return d["ws"][o:o + 128 * w].rearrange("(p c) -> p c", p=128), w

    def issue_dma(upto):
        while state["dma"] < min(upto, n_slots):
            i = state["dma"]
            src, w = raw_view(i)
            dma_tok[i] = load(wraw[i % RAW][:, 0:w], src, s_raw[i % RAW],
                              lo_tok[i - RAW] if i >= RAW else None)
            state["dma"] += 1

    def issue_split(upto):
        while state["split"] < min(upto, n_slots):
            i = state["split"]
            issue_dma(i + 1)
            _, w = raw_view(i)
            r, h = wraw[i % RAW], i % HL
            hi_tok[i] = A(lambda e, r=r, h=h, w=w: e.activation(whi[h][:, 0:w], r[:, 0:w], ACT.Copy),
                          dma_tok[i], pe_tok[i - HL] if i >= HL else None)
            lo_tok[i] = V(lambda e, r=r, h=h, w=w: e.tensor_tensor(wlo[h][:, 0:w], r[:, 0:w],
                                                                 whi[h][:, 0:w].bitcast(F32), ALU.subtract),
                          hi_tok[i])
            state["split"] += 1
            issue_dma(i + RAW)

    background, deferred = [], []

    def later(n, fn):
        deferred.append([n, fn])

    def flush():
        for x in sorted(deferred, key=lambda x: x[0]):
            x[1]()
        deferred.clear()

    def tick():
        for x in deferred:
            x[0] -= 1
        due = [x for x in deferred if x[0] <= 0]
        deferred[:] = [x for x in deferred if x[0] > 0]
        for x in due:
            x[1]()

    def pump(n=1):
        for _ in range(n):
            if background:
                try:
                    next(background[0])
                except StopIteration:
                    background.pop(0)

    def drain():
        while background:
            pump()

    turn = [0]

    def gemm(name, act, ready, evac, rate=1, banks=0):
        first, n_s, n, mode = TABLE[name]
        b0 = 4 * turn[0] if banks else 0
        turn[0] = (turn[0] + 1) % 2 if banks else 1
        nb = 4 if mode == "tok" else n // 128
        for s in range(n_s):
            i = first + s
            issue_split(i + 1 + LA)
            h = i % HL
            for b in range(nb):
                for kk in range(2):
                    k = 2 * s + kk
                    ahi, alo = act(k)
                    if mode == "tok":
                        c0, c1 = kk * n, kk * n + n
                        pairs = [(ahi[:, b * 128:b * 128 + 128], whi[h][:, c0:c1]),
                                 (ahi[:, b * 128:b * 128 + 128], wlo[h][:, c0:c1]),
                                 (alo[:, b * 128:b * 128 + 128], whi[h][:, c0:c1])]
                        o = ps[b0 + b][:, 0:n]
                    else:
                        c0 = kk * n + b * 128
                        pairs = [(whi[h][:, c0:c0 + 128], ahi), (whi[h][:, c0:c0 + 128], alo),
                                 (wlo[h][:, c0:c0 + 128], ahi)]
                        o = ps[b0 + b][:]
                    for j, (l, r) in enumerate(pairs):
                        st = s == 0 and kk == 0 and j == 0
                        sp = s == n_s - 1 and kk == 1 and j == 2
                        w = [lo_tok[i]] if (b == 0 and kk == 0 and j == 0) else []
                        if st:
                            w = w + [bank_free[b0 + b]]
                        if j == 0 and ready is not None:
                            w = w + [ready(k)]
                        last = P(lambda e, o=o, l=l, r=r, st=st, sp=sp: e.matmul(o, l, r, start=st, stop=sp), *w)
                if s == n_s - 1:
                    bank_free[b0 + b] = evac(b, ps[b0 + b], last)
                if b < nb - 1:
                    pump((b + 1) * rate // nb - b * rate // nb)
            pe_tok[i] = last
            tick()
            pump(rate - (nb - 1) * rate // nb)

    def mm(o, l, r, st, sp, *after):
        return P(lambda e: e.matmul(o, l, r, start=st, stop=sp), *after)

    def tr(o, i, *after, n=128):
        return P(lambda e: e.transpose(o, i, ident[0:n, 0:n] if n < 128 else ident), t_vec, *after)

    def split_out(hi, lo, src, scale, *after):
        a = A(lambda e: e.activation(hi, src, ACT.Copy, scale=scale), *after)
        v = V(lambda e: e.scalar_tensor_tensor(lo, src, scale, hi.bitcast(F32), ALU.mult, ALU.subtract), a)
        return v

    small = sb("small", 68 + (NV * 4 + 31) // 32 * 32 / 1024, [128, 64])
    assert NV * 4 + 64 * 4 <= 7 * 1024, NV

    h_ready = {}

    def hT(k):
        return hThi[:, k, :], hTlo[:, k, :]

    def half_square(x, i, half, junk, *after):
        return A(lambda e: e.activation(junk, x[:, i, half * 512:half * 512 + 512], ACT.Square,
                                        accum_out=small[:, 48 + 2 * i + half:49 + 2 * i + half]), *after)

    def row_rstd(i, halves):
        c = 48 + 2 * i
        g = G(lambda e: e.tensor_scalar(small[:, i:i + 1], small[:, c:c + 1], 1.0 / D, EPS, ALU.mult, ALU.add),
              halves[0], t_vec)
        g = G(lambda e: e.tensor_scalar(small[:, 4 + i:5 + i], small[:, c + 1:c + 2], 1.0 / D, small[:, i:i + 1],
                                        ALU.mult, ALU.add), halves[1], g)
        return G(lambda e: e.tensor_tensor(small[:, 8 + i:9 + i], small[:, 4 + i:5 + i], col("mhalf"), ALU.pow), g)

    def norm(x, xs, g, sq_toks, h_free, xs_free):
        toks = []
        for i in range(4):
            r = row_rstd(i, sq_toks[i])
            toks.append(V(lambda e, i=i: e.tensor_scalar(xs[:, i, :], x[:, i, :], small[:, 8 + i:9 + i], None,
                                                         ALU.mult), r, xs_free))
        for k in range(8):
            b = (4 + k) % 8
            for i in range(4):
                t = tr(ps[b][:, i * 128:(i + 1) * 128], xs[:, i, k * 128:(k + 1) * 128], toks[i], bank_free[b])
            v = split_out(hThi[:, k, :], hTlo[:, k, :], ps[b][:], col(g, k), t, h_free)
            bank_free[b] = [v]
            h_ready[k] = v
        turn[0] = 1
        return v

    s_x = [sem(f"s_x{i}") for i in range(4)]
    s_z = sem("s_z")
    x1 = sb("x1", AR + 32, [128, 4, D])
    x_dram = d["x"].rearrange("b (i p) c -> p (b i) c", p=128)
    zT = sb("zT", AR + 126, [33, S])
    t_z = load(zT[:], d["zT"], s_z)
    tx = [load(x1[:, i, :], x_dram[:, i, :], s_x[i]) for i in range(4)]
    junk1 = sb("junk1", AR, [128, 512])
    issue_split(LA)

    s_f = sem("s_f")
    w3 = sb("w3", AR + 88, [64, 4, 512])
    cu = sb("cu", AR + 48, [128, 4, 256])
    su = sb("su", AR + 52, [128, 4, 256])
    dec = sb("dec", AR + 80, [128, 4, 512])
    fs = sb("fs", AR + 64, [128, 4, 512])
    fd = sb("fd", AR + 72, [128, 4, 512])
    sq = [sb(f"sq{i}", AR + 32 + 2 * i, [128, 512]) for i in range(4)]
    h1 = sb("h1", AR + 128, [64, S])
    h2 = sb("h2", AR + 96, [64, S])
    ma = [sb(f"ma{i}", AR + 104 + 2 * i, [64, S]) for i in range(4)]
    et = [sb("et0", AR + 102, [128, 512]), sb("et1", AR + 130, [128, 512])]
    Cre = [sb(f"Cre{o}", AR + 16 * o, [128, 4, 512]) for o in range(2)]
    Cim = [sb(f"Cim{o}", AR + 16 * o + 8, [128, 4, 512]) for o in range(2)]
    fwd = [sb("fp", AR + 56, [128, 2, 512]), sb("fm", AR + 60, [128, 2, 512])]
    inv = [sb("ip", AR + 88, [128, 4, 256]), sb("im", AR + 92, [128, 4, 256])]

    t_w3 = load(w3[:], d["w3"].rearrange("h (g c) -> h g c", g=4), s_f)
    t_f = load(dec[:], d["dec"], s_f)
    t_f = load(cu[:], d["cu"], s_f)
    t_f = load(su[:], d["su"], s_f)
    t_f = load(fwd[0][:], d["fp"], s_f)
    t_f = load(fwd[1][:], d["fm"], s_f)

    TWO_PI = 2 * math.pi
    MAGIC = 1.5 * 2 ** 23
    C1 = 6.28125
    C2 = TWO_PI - C1

    def sine(dst, src, b, f, t):
        t = V(lambda e: e.tensor_scalar(ma[0][:], src, col(b, p=64), col(f, p=64), ALU.add, ALU.mult), t)
        u = V(lambda e: e.tensor_scalar(ma[1][:], ma[0][:], 1 / TWO_PI, MAGIC, ALU.mult, ALU.add), t)
        u = V(lambda e: e.tensor_scalar(ma[2][:], ma[1][:], MAGIC, None, ALU.subtract), u)
        u = V(lambda e: e.scalar_tensor_tensor(ma[3][:], ma[2][:], -C1, ma[0][:], ALU.mult, ALU.add), u)
        u = V(lambda e: e.scalar_tensor_tensor(ma[1][:], ma[2][:], -C2, ma[3][:], ALU.mult, ALU.add), u)
        u = V(lambda e: e.tensor_scalar(ma[3][:], ma[1][:], 3.1415925, -3.1415925, ALU.min, ALU.max), u)
        return t, A(lambda e: e.activation(dst, ma[3][:], ACT.Sin), u)

    t = mm(ps[0][0:64, :], col("w1", 0, 64, p=33), zT[:], True, True, t_z, t_vec)
    bf, t = sine(h1[:], ps[0][0:64, :], "b1", "f1", t)
    bank_free[0] = [bf]
    t = mm(ps[1][0:64, :], col("w2", 0, 64, p=64), h1[:], True, True, t)
    bf, t_h2 = sine(h2[:], ps[1][0:64, :], "b2", "f2", t)
    bank_free[1] = [bf]
    ma_done = Q.last("vector", "scalar", "tensor")

    norm_tok = norm(x1, x1, "g1", [[half_square(x1, i, h, junk1[:], tx[i]) for h in range(2)] for i in range(4)],
                    None, None)
    x_done = Q.last("tensor", "scalar", "vector")
    w3v = w3[:]
    t_ws = []
    for o in range(2):
        f, b = w3v[:, 2 * o, :], w3v[:, 2 * o + 1, :]
        t = V(lambda e, b=b, f=f: e.tensor_tensor(ma[0][:], f, b, ALU.add), t_f, ma_done)
        t = V(lambda e, b=b, f=f: e.tensor_tensor(b, f, b, ALU.subtract), t)
        t = V(lambda e, f=f: e.tensor_copy(f, ma[0][:]), t)
        t_ws.append(t)
    ma_done = Q.last("vector", "scalar", "tensor")
    rn_tok = {}

    def filters():
        f_free = []

        def row_sums(sums):
            for tt, j, a in sums:
                wcol = col(("wS0", "wD0")[j]) if tt == 0 else col("half")
                q = sq[2 * (tt % 2) + j]
                for c in range(4):
                    t = mm(ps[6][:, 8 * c + 2 * tt + j:8 * c + 2 * tt + j + 1], q[:, c * 128:(c + 1) * 128], wcol,
                           True, True, a, bank_free[6])
                sq_free[2 * (tt % 2) + j] = t
            return t

        sq_free = [None] * 4
        for o in range(2):
            td, sums = [], []
            for tt in range(4):
                now = []
                for j, dst in enumerate((fs, fd)):
                    b = 4 + j
                    t = mm(ps[b][:], h2[:, tt * 128:(tt + 1) * 128], w3v[:, 2 * o + j, :], True, True,
                           t_h2, t_ws[o], bank_free[b])
                    v = V(lambda e, b=b, dst=dst, tt=tt: e.tensor_tensor(dst[:, tt, :], ps[b][:], dec[:, tt, :],
                                                                         ALU.mult), t, t_f, f_free)
                    bank_free[b] = [v]
                    td.append(v)
                    i = 2 * (tt % 2) + j
                    a = A(lambda e, i=i, dst=dst, tt=tt: e.activation(sq[i][:], dst[:, tt, :], ACT.Square), v, x_done,
                          sq_free[i])
                    now.append((tt, j, a))
                if sums:
                    row_sums(sums)
                sums = now
                yield
            t = row_sums(sums)
            v = V(lambda e: e.tensor_reduce(small[:, 24:28], ps[6][:, 0:32].rearrange("p (c t) -> p c t", c=4), AX.X,
                                            ALU.add), t)
            bank_free[6] = [v]
            v = V(lambda e: e.tensor_scalar(small[:, 24:28], small[:, 24:28], EPS, None, ALU.add), v)
            g = G(lambda e: e.tensor_tensor(small[:, 28:32], small[:, 24:28], col("mhalf", 0, 4), ALU.pow), v)
            V(lambda e, o=o: e.tensor_scalar(small[:, 16 + 4 * o:20 + 4 * o], small[:, 28:32], 1.0 / 1024, None,
                                             ALU.mult), g)
            rn_tok[o] = V(lambda e, o=o: e.tensor_scalar(small[:, 56 + 4 * o:60 + 4 * o], small[:, 28:32], -1.0 / 1024,
                                                         None, ALU.mult), g)
            for kt in range(2):
                for j, (tab, src, dst) in enumerate(((cu, fs, Cre[o]), (su, fd, Cim[o]))):
                    be, bo = 4 + 2 * j, 5 + 2 * j
                    for b, t0 in ((be, 0), (bo, 2)):
                        for t1 in range(2):
                            t = mm(ps[b][:], tab[:, t0 + t1, kt * 128:(kt + 1) * 128], src[:, t0 + t1, :], t1 == 0, t1 == 1,
                                   td, t_f, bank_free[b])
                        if b == be:
                            a = A(lambda e, be=be, j=j: e.activation(et[j][:], ps[be][:], ACT.Copy), t, ma_done,
                                  Q.last("vector"))
                    v1 = V(lambda e, bo=bo, j=j, dst=dst, kt=kt: e.tensor_tensor(dst[:, kt, :], ps[bo][:], et[j][:], ALU.add),
                           t, a, x_done)
                    if j == 0:
                        v2 = V(lambda e, bo=bo, dst=dst, kt=kt: e.tensor_tensor(dst[:, 2 + kt, :], et[0][:], ps[bo][:],
                                                                                ALU.subtract))
                    else:
                        v2 = V(lambda e, bo=bo, dst=dst, kt=kt: e.tensor_tensor(dst[:, 2 + kt, :], ps[bo][:], et[1][:],
                                                                                ALU.subtract))
                    bank_free[be] = [a]
                    bank_free[bo] = [v2]
                yield
            f_free = Q.last("tensor", "scalar", "vector")

    uT = [sb(f"uT{i}", AR + 104 + 8 * i, [128, 4, S]) for i in range(3)]
    tok = sb("tok", AR + 48, [128, 4, 512])
    U = sb("U", AR + 64, [128, 4, 512])
    W = sb("W", AR + 72, [128, 4, 512])
    tm = [sb(f"tm{i}", AR + 80 + 2 * i, [128, 512]) for i in range(4)]
    sd = sb("sd", AR + 96, [128, 4, 512])
    dv = [sb(f"dv{i}", AR + 128 + 2 * i, [128, 512]) for i in range(2)]
    obhi = sb("obhi", AR + 0, [128, 4, S], F32R)
    oblo = sb("oblo", AR + 8, [128, 4, S], F32R)
    gate = [sb(f"gate{i}", AR + 32 + 8 * i, [128, 4, S]) for i in range(2)]

    hready = lambda k: h_ready[k]
    u_tok = {}
    background.append(filters())
    for gidx in range(3):
        def evac(b, p, t, gidx=gidx):
            f = gidx * 4 + b
            dst = uT[gidx][:, b, :]
            a = A(lambda e: e.activation(dst, p[:], ACT.Identity, bias=col("cb", f), scale=col("cw", 12 + f)),
                  t, ma_done)
            v = V(lambda e: e.scalar_tensor_tensor(dst[:, 1:S], p[:, 0:S - 1], col("cw", f), dst[:, 1:S],
                                                   ALU.mult, ALU.add), a)
            v = V(lambda e: e.scalar_tensor_tensor(dst[:, 0:S - 1], p[:, 1:S], col("cw", 24 + f),
                                                   dst[:, 0:S - 1], ALU.mult, ALU.add), v)
            u_tok[gidx, b] = v
            return [v]
        gemm("hy%d" % gidx, hT, hready, evac, rate=2)
    drain()
    f_done = Q.last("tensor", "vector", "scalar", "gpsimd")
    s_inv = sem("s_inv")
    t_inv = load(inv[0][:], d["ip"], s_inv, f_done)
    t_inv = load(inv[1][:], d["im"], s_inv, f_done)

    vT, x1T, x2T = uT
    ob_tok = [None]

    def hyena():
        src, src_tok = vT, [u_tok[0, b] for b in range(4)]
        sd_free, tok_free, y_free = f_done, f_done, f_done
        for o in range(2):
            tk, sdt = [], []
            for c in range(4):
                lo_, hi_ = src[:, c, 0:256], src[:, c, 256:512][:, ::-1]
                g = G(lambda e, c=c, lo_=lo_, hi_=hi_: e.tensor_tensor(sd[:, c, 0:256], lo_, hi_, ALU.add), src_tok[c],
                      sd_free)
                v = V(lambda e, c=c, lo_=lo_, hi_=hi_: e.tensor_tensor(sd[:, c, 256:512], lo_, hi_, ALU.subtract),
                      src_tok[c], sd_free)
                sdt.append([g, v])
            for tt in range(4):
                b = 4 + tt
                for c in range(4):
                    t = tr(ps[b][:, c * 128:(c + 1) * 128], sd[:, c, tt * 128:(tt + 1) * 128], sdt[c], bank_free[b])
                a = A(lambda e, b=b, tt=tt: e.activation(tok[:, tt, :], ps[b][:], ACT.Copy), t, tok_free)
                bank_free[b] = [a]
                tk.append(a)
            sd_free = Q.last("tensor")
            yield
            yt = []
            for ft in range(4):
                bp, bm = (4, 5) if ft % 2 == 0 else (6, 7)
                for bk, tab, s0 in ((bp, fwd[0], 0 if ft < 2 else 2), (bm, fwd[1], 2 if ft < 2 else 0)):
                    for tt in range(2):
                        t = mm(ps[bk][:], tab[:, tt, ft * 128:(ft + 1) * 128], tok[:, s0 + tt, :], tt == 0, tt == 1,
                               tk[s0 + tt], bank_free[bk])
                cre, cim = Cre[o][:, ft, :], Cim[o][:, ft, :]
                t0, t1 = tm[2 * (ft % 2)], tm[2 * (ft % 2) + 1]
                tm_free = yt[-2] if len(yt) >= 2 else y_free
                V(lambda e, bp=bp, cre=cre, ft=ft: e.tensor_tensor(U[:, ft, :], ps[bp][:], cre, ALU.mult), t, y_free)
                v1 = V(lambda e, bm=bm, cim=cim, t0=t0: e.tensor_tensor(t0[:], ps[bm][:], cim, ALU.mult), tm_free)
                G(lambda e, ft=ft, t0=t0: e.tensor_tensor(U[:, ft, :], U[:, ft, :], t0[:], ALU.subtract), v1)
                V(lambda e, bp=bp, cim=cim, ft=ft: e.tensor_tensor(W[:, ft, :], ps[bp][:], cim, ALU.mult))
                v3 = V(lambda e, bm=bm, cre=cre, t1=t1: e.tensor_tensor(t1[:], ps[bm][:], cre, ALU.mult))
                g = G(lambda e, ft=ft, t1=t1: e.tensor_tensor(W[:, ft, :], W[:, ft, :], t1[:], ALU.add), v3)
                bank_free[bp] = [v3]
                bank_free[bm] = [v3]
                yt.append(g)
                yield
            tok_free = Q.last("tensor")
            nt = []
            for c in range(4):
                b = 4 + c
                z = dv[c % 2]
                z0, z1 = z[:, 0:256], z[:, 256:512][:, ::-1]
                s_, d_ = ps[b][:, 0:256], ps[b][:, 256:512]
                rp, rm = small[:, 16 + 4 * o + c:17 + 4 * o + c], small[:, 56 + 4 * o + c:57 + 4 * o + c]
                a = A(lambda e, c=c, o=o, src=src, z=z: e.activation(z[:], src[:, c, :], ACT.Copy,
                                                                     scale=col("hd", 4 * o + c)), Q.last("vector"))
                for ap, parts in ((s_, ((U, 0, 0), (U, 0, 1), (W, 1, 2), (W, 1, 3))),
                                  (d_, ((W, 1, 0), (W, 1, 1), (U, 0, 2), (U, 0, 3)))):
                    for i, (y, tb, ft) in enumerate(parts):
                        t = mm(ap, y[:, ft, c * 128:(c + 1) * 128], inv[tb][:, ft, :], i == 0, i == 3, yt[ft], t_inv,
                               bank_free[b])
                for out_, in_, r in ((z0, s_, rp), (z0, d_, rp), (z1, s_, rp), (z1, d_, rm)):
                    v = V(lambda e, out_=out_, in_=in_, r=r: e.scalar_tensor_tensor(out_, in_, r, out_, ALU.mult, ALU.add),
                          t, a, rn_tok[o])
                bank_free[b] = [v]
                g = uT[1 + o]
                v = V(lambda e, c=c, g=g, z=z: e.tensor_tensor(g[:, c, :], g[:, c, :], z[:], ALU.mult), v,
                      u_tok[1 + o, c])
                nt.append(v)
                if o == 1:
                    a = A(lambda e, c=c: e.activation(obhi[:, c, :], x2T[:, c, :], ACT.Copy), v, y0_done)
                    ob_tok[0] = V(lambda e, c=c: e.tensor_tensor(oblo[:, c, :], x2T[:, c, :],
                                                                 obhi[:, c, :].bitcast(F32), ALU.subtract), a)
                yield
            y_free = Q.last("tensor")
            y0_done = Q.last("vector", "gpsimd")
            src, src_tok = x1T, nt

    gate_n = [0]
    gate_tok, gate_free, mtok = {}, [f_done, f_done], {}

    def gate_group(name, rate=1):
        i = gate_n[0] % 2
        gate_n[0] += 1

        def evac(b, p, t):
            a = A(lambda e: e.activation(gate[i][:, b, :], p[:], ACT.Tanh, scale=0.5), t, gate_free[i], x_done)
            gate_tok[i, b] = a
            return [a]
        gemm(name, hT, hready, evac, rate=rate)
        return i

    background.append(hyena())
    for half in range(2):
        gate_group("gB%d" % half, rate=2)
    drain()
    hy_done = Q.last("tensor", "vector", "scalar", "gpsimd")

    rt = sb("rt", AR + 64, [128, 8, 4, 64])
    raw = [sb(f"raw{i}", AR + 72 + 2 * i, [128, 512]) for i in range(4)]
    tp = [sb(f"tp{i}", AR + 80 + 2 * i, [128, 512]) for i in range(3)]
    cosv = col("cos", 0, 256).rearrange("p (t d) -> p t d", t=4)
    sinv = col("sin", 0, 256).rearrange("p (t d) -> p t d", t=4)
    for gi, nm in enumerate(("qna", "kna", "qnc", "knc")):
        o, _ = VEC[nm]
        g0 = vec[:, o:o + 64].unsqueeze(1).to_broadcast([128, 4, 64])
        glo = vec[:, o:o + 32].unsqueeze(1).to_broadcast([128, 4, 32])
        ghi = vec[:, o + 32:o + 64].unsqueeze(1).to_broadcast([128, 4, 32])
        G(lambda e, gi=gi, g0=g0: e.tensor_tensor(rt[:, 2 * gi, :, :], cosv, g0, ALU.mult), hy_done, t_vec)
        G(lambda e, gi=gi, ghi=ghi: e.tensor_tensor(rt[:, 2 * gi + 1, :, 0:32], sinv[:, :, 0:32], ghi, ALU.mult))
        G(lambda e, gi=gi, glo=glo: e.tensor_tensor(rt[:, 2 * gi + 1, :, 32:64], sinv[:, :, 32:64], glo, ALU.mult))
    t_rt = Q.last("gpsimd")
    lam = small[:, 40:41]
    nsink = small[:, 24:32]
    t_nsink = V(lambda e: e.tensor_scalar(nsink, col("sink", 0, 8), -1.0, None, ALU.mult), hy_done)
    v1 = V(lambda e: e.tensor_tensor_reduce(tp[2][:, 0:64], col("lq1", 0, 64), col("lk1", 0, 64), 1.0, 0.0, ALU.mult,
                                            ALU.add, small[:, 36:37]), hy_done)
    v2 = V(lambda e: e.tensor_tensor_reduce(tp[2][:, 64:128], col("lq2", 0, 64), col("lk2", 0, 64), 1.0, 0.0,
                                            ALU.mult, ALU.add, small[:, 37:38]))
    a = A(lambda e: e.activation(small[:, 38:40], small[:, 36:38], ACT.Exp), v1, v2)
    v = V(lambda e: e.tensor_tensor(small[:, 41:42], small[:, 39:40], small[:, 38:39], ALU.subtract), a)
    t_lam = V(lambda e: e.tensor_scalar(lam, small[:, 41:42], LAM0, None, ALU.subtract), v)

    qaT = sb("qaT", AR + 86, [128, 4, S])
    kaT = sb("kaT", AR + 94, [128, 1, S])
    va = sb("va", AR + 96, [128, 4, 128])
    T8 = [sb(f"T8_{i}", AR + 98 + 1.5 * i, [128, 384]) for i in range(3)]
    PT = [sb(f"PT{i}", AR + 102.5 + 1.5 * i, [128, 384]) for i in range(2)]
    maskA = sb("maskA", AR + 105.5, [128, 384])
    st = sb("st", AR + 107, [128, 128])
    qcT = sb("qcT", AR + 107.5, [128, 4, S])
    kcT = sb("kcT", AR + 115.5, [128, 4, S])
    vc = sb("vc", AR + 123.5, [128, 4, 512])
    oahi = sb("oahi", AR + 48, [128, 4, S], F32R)
    oalo = sb("oalo", AR + 56, [128, 4, S], F32R)
    merged = sb("merged", AR + 16, [128, 8, S])
    s_m = sem("s_m")
    t_maskA = load(maskA[:], d["maskA"], s_m, hy_done)

    raw_free = [[] for _ in range(4)]
    tp_free = [[] for _ in range(2)]
    tp2_free = [None]

    def rope(b, p, t, H, ti, dst, toks, key):
        W = H * 64
        hv = lambda ap: ap.rearrange("p (h d) -> p h d", h=H)
        r, q0, q1 = raw[b][:, 0:W], tp[b % 2][:, 0:W], tp[2][:, 0:W]
        s0 = 64 + 16 * b
        ss_, ms_, rs_ = (st[:, s0 + i * 8:s0 + i * 8 + H] for i in (0, 1, 0))
        done = A(lambda e: e.activation(r, p[:, 0:W], ACT.Copy), t, raw_free[b], t_rt)
        a = A(lambda e: e.activation(q0, r, ACT.Square), done, tp_free[b % 2])
        v = V(lambda e: e.tensor_reduce(ss_, hv(q0), AX.X, ALU.add), a)
        tp_free[b % 2] = [v]
        g = G(lambda e: e.tensor_scalar(ms_, ss_, 1.0 / 64, EPS, ALU.mult, ALU.add), v)
        g_rs = G(lambda e: e.tensor_tensor(rs_, ms_, col("mhalf", 0, H), ALU.pow), g)
        nj = W // 128

        def turn():
            cg = rt[:, 2 * ti, b, :].unsqueeze(1).to_broadcast([128, H, 64])
            sa = rt[:, 2 * ti + 1, b, 0:32].unsqueeze(1).to_broadcast([128, H, 32])
            sb_ = rt[:, 2 * ti + 1, b, 32:64].unsqueeze(1).to_broadcast([128, H, 32])
            r1, r2_ = hv(r)[:, :, 0:32], hv(r)[:, :, 32:64]
            o1, o2 = hv(q1)[:, :, 0:32], hv(q1)[:, :, 32:64]
            v = V(lambda e: e.tensor_tensor(hv(r), hv(r), rs_.unsqueeze(2).to_broadcast([128, H, 64]), ALU.mult), g_rs)
            G(lambda e: e.tensor_tensor(o1, r2_, sa, ALU.mult), v, tp2_free[0])
            g = G(lambda e: e.tensor_tensor(o2, r1, sb_, ALU.mult))
            v = V(lambda e: e.tensor_tensor(hv(q0), hv(r), cg, ALU.mult), v, tp_free[b % 2])
            v = V(lambda e: e.tensor_tensor(r, q0, q1, ALU.add), v, g)
            tp_free[b % 2] = [v]
            tp2_free[0] = v

            def across():
                for j in range(nj):
                    t = tr(ps[6][:, j * 128:(j + 1) * 128], r[:, j * 128:(j + 1) * 128], v, bank_free[6])
                raw_free[b] = [t]
                a = A(lambda e: e.activation(dst[:, :, b * 128:(b + 1) * 128],
                                             ps[6][:, 0:W].rearrange("p (j t) -> p j t", j=nj), ACT.Copy), t, hy_done)
                bank_free[6] = [a]
                toks[key, b] = a

            later(1, across)

        later(1 + b // 2, turn)
        return [done]

    ra = {}

    def evac_kva(b, p, t):
        a2 = A(lambda e: e.activation(va[:, b, :], p[:, 128:256], ACT.Copy), t, hy_done)
        return rope(b, p, t, 2, 1, kaT, ra, "k") + [a2]

    gemm("qa", hT, hready, lambda b, p, t: rope(b, p, t, 8, 0, qaT, ra, "q"))
    gemm("kva", hT, hready, evac_kva)

    def att_a():
        units = [(n, h) for n in range(4) for h in range(8)]
        info = {}
        while len(ra) < 8:
            yield
        ra_all = list(ra.values())

        def s1(u):
            n, h = units[u]
            b, j, base, kv = 4 + u % 2, h % 4, 64 * (h // 4), h // 4
            k0, k1 = max(n - 1, 0), min(n + 1, 3)
            W = 128 * (k1 - k0 + 1)
            m0 = 0 if n > 0 else 128
            t = mm(ps[b][:, 0:W], qaT[base:base + 64, j, n * 128:(n + 1) * 128], kaT[base:base + 64, 0, k0 * 128:k0 * 128 + W],
                   True, True, ra_all, bank_free[b])
            T = T8[u % 3]
            c = 24 + 8 * (u % 4)
            prev = info[u - 3]["pt"] if u >= 3 else None
            v = V(lambda e: e.tensor_tensor_reduce(T[:, 0:W], ps[b][:, 0:W], maskA[:, m0:m0 + W], -0.125, nsink[:, h:h + 1],
                                                   ALU.add, ALU.min, st[:, c:c + 1]), t, t_maskA, prev, t_nsink)
            bank_free[b] = [v]
            a1 = A(lambda e: e.activation(T[:, 0:W], T[:, 0:W], ACT.Exp, bias=st[:, c:c + 1], scale=-1.0,
                                          accum_out=st[:, c + 2:c + 3]), v)
            a2 = A(lambda e: e.activation(st[:, c + 3:c + 4], col("sink", h), ACT.Exp, bias=st[:, c:c + 1]))
            info[u] = dict(k0=k0, W=W, T=T, c=c, tok=[a1, a2])

        def s1b(u):
            i = info[u]
            c, T, W = i["c"], i["T"], i["W"]
            v = V(lambda e: e.tensor_tensor(st[:, c + 4:c + 5], st[:, c + 2:c + 3], st[:, c + 3:c + 4], ALU.add),
                  i["tok"])
            v = V(lambda e: e.reciprocal(st[:, c + 5:c + 6], st[:, c + 4:c + 5]), v)
            i["tok"] = V(lambda e: e.tensor_scalar(T[:, 0:W], T[:, 0:W], st[:, c + 5:c + 6], None, ALU.mult), v)

        def s2(u):
            i = info[u]
            for k in range(i["W"] // 128):
                t = tr(ps[6][:, k * 128:(k + 1) * 128], i["T"][:, k * 128:(k + 1) * 128], i["tok"], bank_free[6])
            i["pt"] = t
            W = i["W"]
            prev = info[u - 2]["pv"] if u >= 2 else None
            a = A(lambda e: e.activation(PT[u % 2][:, 0:W], ps[6][:, 0:W], ACT.Copy), t, prev, hy_done)
            bank_free[6] = [a]
            i["ev"] = a

        def s3(u):
            n, h = units[u]
            i = info[u]
            j, base, kv = h % 4, 64 * (h // 4), h // 4
            nk = i["W"] // 128
            for k in range(nk):
                t = mm(ps[7][base:base + 64, j * 128:(j + 1) * 128], va[:, i["k0"] + k, kv * 64:kv * 64 + 64],
                       PT[u % 2][:, k * 128:(k + 1) * 128], k == 0, k == nk - 1, i["ev"], bank_free[7])
            i["pv"] = t
            if h == 7:
                hi = oahi[:, :, n * 128:(n + 1) * 128]
                lo = oalo[:, :, n * 128:(n + 1) * 128]
                src = ps[7][:].rearrange("p (j t) -> p j t", j=4)
                a = A(lambda e: e.activation(hi, src, ACT.Copy), t, hy_done)
                v = V(lambda e: e.tensor_tensor(lo, src, hi.bitcast(F32), ALU.subtract), a)
                bank_free[7] = [v]
                info["oa", n] = v

        for u in range(len(units) + 3):
            if u < len(units):
                s1(u)
            if 1 <= u <= len(units):
                s1b(u - 1)
            if 2 <= u < len(units) + 2:
                s2(u - 2)
            if u >= 3:
                s3(u - 3)
            yield
        oa_tok.extend(info["oa", n] for n in range(4))

    oa_tok = []
    def branch_group(name, gi, act, ready, half, first, rate=1):
        def evac(b, p, t):
            m = merged[:, 4 * half + b, :]
            gt = gate[gi][:, b, :]
            if first:
                v = V(lambda e: e.scalar_tensor_tensor(m, gt, 1.0, p[:], ALU.add, ALU.mult), t, gate_tok[gi, b],
                      hy_done)
                mtok[half, b] = v
                return [v]
            v = V(lambda e: e.scalar_tensor_tensor(gt, gt, 1.0, p[:], ALU.add, ALU.mult), t, gate_tok[gi, b])
            mtok[half, b] = G(lambda e: e.tensor_tensor(m, m, gt, ALU.add), v, mtok[half, b])
            return [v]
        gemm(name, act, ready, evac, rate=rate)
        gate_free[gi] = Q.last("vector", "gpsimd")

    background.append(att_a())
    for half in range(2):
        branch_group("bB%d" % half, half, lambda k: (obhi[:, k, :], oblo[:, k, :]), lambda k: ob_tok[0], half, True, rate=2)

    rc = {}

    def evac_vc(b, p, t):
        a = A(lambda e: e.activation(vc[:, b, :], p[:], ACT.Copy), t, hy_done)
        rc["v", b] = a
        return [a]

    gemm("qc", hT, hready, lambda b, p, t: rope(b, p, t, 8, 2, qcT, rc, "q"), rate=2)
    gemm("kc", hT, hready, lambda b, p, t: rope(b, p, t, 8, 3, kcT, rc, "k"), rate=2)
    gemm("vc", hT, hready, evac_vc, rate=2)
    flush()
    for half in range(2):
        gate_group("gA%d" % half, rate=2)
    drain()
    a_done = Q.last("tensor", "vector", "scalar", "gpsimd")
    rc_all = [rc[k] for k in sorted(rc)]

    Pc = [sb(f"Pc{i}", AR + 72 + 2 * i, [128, 512]) for i in range(6)]
    oc = sb("oc", AR + 84, [128, 512])
    ocs = sb("ocs", AR + 86, [128, 512])
    PTc = [sb(f"PTc{i}", AR + 88 + 2 * i, [128, 512]) for i in range(3)]
    ochi = sb("ochi", AR + 0, [128, 4, S], F32R)
    oclo = sb("oclo", AR + 8, [128, 4, S], F32R)
    oc_tok = {}

    def att_c():
        units = [(n, h) for n in range(4) for h in range(4)]
        info = {}

        def s1(u):
            n, h = units[u]
            prev = info[u - 3]["pt"] if u >= 3 else None
            P2 = [Pc[2 * (u % 3)], Pc[2 * (u % 3) + 1]]
            o = 24 + 16 * (u % 4)
            la = []
            for c in range(2):
                b = 4 + c
                base = 64 * c
                oo = o + 8 * c
                t = mm(ps[b][:], qcT[base:base + 64, h, n * 128:(n + 1) * 128], kcT[base:base + 64, h, :], True, True,
                       rc_all, bank_free[b])
                v = V(lambda e, b=b, oo=oo: e.tensor_reduce(st[:, oo:oo + 1], ps[b][:], AX.X, ALU.max), t, a_done)
                v = V(lambda e, oo=oo: e.tensor_scalar(st[:, oo + 1:oo + 2], st[:, oo:oo + 1], -0.125, None, ALU.mult), v)
                a = A(lambda e, b=b, oo=oo, c=c: e.activation(P2[c][:], ps[b][:], ACT.Exp, bias=st[:, oo + 1:oo + 2],
                                                              scale=0.125, accum_out=st[:, oo + 2:oo + 3]), v, prev,
                      a_done)
                bank_free[b] = [a]
                la.append(a)
            info[u] = dict(P=P2, tok=la, o=o)

        def s1b(u):
            i = info[u]
            o, P2, h = i["o"], i["P"], units[u][1]
            v = V(lambda e: e.reciprocal(st[:, o + 3:o + 4], st[:, o + 10:o + 11]), i["tok"])
            v = V(lambda e: e.scalar_tensor_tensor(st[:, o + 4:o + 5], st[:, o + 3:o + 4], lam, st[:, o + 2:o + 3],
                                                   ALU.mult, ALU.mult), v, t_lam)
            V(lambda e: e.reciprocal(st[:, 16 + 4 * (units[u][0] % 2) + h:17 + 4 * (units[u][0] % 2) + h], st[:, o + 2:o + 3]))
            i["tok"] = V(lambda e: e.scalar_tensor_tensor(P2[0][:], P2[1][:], st[:, o + 4:o + 5], P2[0][:], ALU.mult,
                                                          ALU.add), v)
            i["rtok"] = i["tok"]
            i["P"] = P2[0]

        def s2(u):
            i = info[u]
            for k in range(4):
                t = tr(ps[6][:, k * 128:(k + 1) * 128], i["P"][:, k * 128:(k + 1) * 128], i["tok"], bank_free[6])
            i["pt"] = t
            a = A(lambda e: e.activation(PTc[u % 3][:], ps[6][:], ACT.Copy), t,
                  info[u - 3]["pv"] if u >= 3 else None, a_done)
            bank_free[6] = [a]
            i["ev"] = a

        def s3(u):
            n, h = units[u]
            i = info[u]
            for k in range(4):
                t = mm(ps[7][:, h * 128:(h + 1) * 128], PTc[u % 3][:, k * 128:(k + 1) * 128],
                       vc[:, k, h * 128:(h + 1) * 128], k == 0, k == 3, i["ev"], bank_free[7])
            i["pv"] = t
            if h == 3:
                hv = lambda ap: ap.rearrange("p (h d) -> p h d", h=4)
                r0 = st[:, 16 + 4 * (n % 2):20 + 4 * (n % 2)].unsqueeze(2).to_broadcast([128, 4, 128])
                v = V(lambda e: e.tensor_tensor(hv(ocs[:]), hv(ps[7][:]), r0, ALU.mult), t, i["rtok"], a_done,
                      Q.last("tensor"))
                bank_free[7] = [v]
                a = A(lambda e: e.activation(oc[:], ocs[:], ACT.Square), v, a_done)
                info["raw"] = (n, a)

        def s3b():
            n, a = info.pop("raw")
            hv = lambda ap: ap.rearrange("p (h d) -> p h d", h=4)
            v = V(lambda e: e.tensor_reduce(st[:, 100:104], hv(oc[:]), AX.X, ALU.add), a)
            g = G(lambda e: e.tensor_scalar(st[:, 104:108], st[:, 100:104], 1.0 / 128, EPS, ALU.mult, ALU.add), v)
            g = G(lambda e: e.tensor_tensor(st[:, 108:112], st[:, 104:108], col("mhalf", 0, 4), ALU.pow), g)
            g = G(lambda e: e.tensor_scalar(st[:, 112:116], st[:, 108:112], 1.0 - LAM0, 0.0, ALU.mult, ALU.add), g)
            info["ocs"] = (n, G(lambda e: e.tensor_tensor(hv(ocs[:]), hv(ocs[:]),
                                                          st[:, 112:116].unsqueeze(2).to_broadcast([128, 4, 128]),
                                                          ALU.mult), g))

        def s4():
            n, v = info.pop("ocs")
            for k in range(4):
                t = tr(ps[6][:, k * 128:(k + 1) * 128], ocs[:, k * 128:(k + 1) * 128], v, bank_free[6])
            src = ps[6][:].rearrange("p (j t) -> p j t", j=4)
            hi, lo = ochi[:, :, n * 128:(n + 1) * 128], oclo[:, :, n * 128:(n + 1) * 128]
            a = A(lambda e: e.activation(hi, src, ACT.Copy, scale=col("subln")), t, a_done)
            oc_tok[n] = V(lambda e: e.scalar_tensor_tensor(lo, src, col("subln"), hi.bitcast(F32), ALU.mult,
                                                           ALU.subtract), a)
            bank_free[6] = [oc_tok[n]]

        for u in range(len(units) + 6):
            if u < len(units):
                s1(u)
            if 1 <= u <= len(units):
                s1b(u - 1)
            if 2 <= u < len(units) + 2:
                s2(u - 2)
            if "ocs" in info:
                s4()
            if "raw" in info:
                s3b()
            if 3 <= u < len(units) + 3:
                s3(u - 3)
            yield

    background.append(att_c())
    for half in range(2):
        branch_group("bA%d" % half, half, lambda k: (oahi[:, k, :], oalo[:, k, :]), lambda k: oa_tok, half, False, rate=2)
    gis = [gate_group("gC%d" % half, rate=2) for half in range(2)]
    drain()
    h_free1 = Q.last("tensor")
    oct = [oc_tok[n] for n in range(4)]
    x = sb("x", AR + 88, [128, 4, D])
    c_done = Q.last("tensor", "vector", "scalar", "gpsimd")
    tx2 = load(x[:], x_dram, s_x[0], c_done)
    m_ready = {}
    for half in range(2):
        def evac(b, p, t, half=half):
            gi = gis[half]
            k = 4 * half + b
            m, gt = merged[:, k, :], gate[gi][:, b, :]
            v = V(lambda e: e.scalar_tensor_tensor(gt, gt, 1.0, p[:], ALU.add, ALU.mult), t, gate_tok[gi, b])
            g = G(lambda e: e.tensor_tensor(m, m, gt, ALU.add), v, mtok[half, b])
            a = A(lambda e: e.activation(hThi[:, k, :], m, ACT.Copy, scale=0.5), g, h_free1)
            m_ready[k] = V(lambda e: e.scalar_tensor_tensor(hTlo[:, k, :], m, 0.5, hThi[:, k, :].bitcast(F32),
                                                            ALU.mult, ALU.subtract), a)
            return [v]
        gemm("bC%d" % half, lambda k: (ochi[:, k, :], oclo[:, k, :]), lambda k: oct, evac)

    xs = sb("xs", AR + 16, [128, 4, D])
    junk = sb("junk", AR + 130, [128, 512])

    def residual(names, act, ready, junk_free=None):
        toks = {}
        for half in range(2):
            def evac(b, p, t, half=half):
                xa = x[:, b, half * 512:half * 512 + 512]
                v = V(lambda e: e.tensor_tensor(xa, p[:], xa, ALU.add), t, tx2)
                toks[half, b] = half_square(x, b, half, junk[:], v, junk_free)
                return [v]
            gemm(names % half, act, ready, evac, banks=1)
        return [[toks[0, b], toks[1, b]] for b in range(4)]

    xt = residual("wo%d", hT, lambda k: m_ready[k], Q.last("tensor", "vector", "scalar", "gpsimd"))

    achi = sb("achi", AR + 0, [128, 22, S], F32R)
    aclo = sb("aclo", AR + 44, [128, 22, S], F32R)
    ft = [sb(f"ft{i}", AR + 104 + 2 * i, [128, S]) for i in range(8)]
    ft_free = [[] for _ in range(8)]

    def ffn(tag, conv):
        a_free = Q.last("tensor", "vector", "scalar", "gpsimd")
        ready = {}
        for j in range(11):
            pend = {}

            def evac(b, p, t, j=j):
                f = 2 * j + b % 2
                i = 4 * (j % 2) + b
                if conv:
                    c = f + 22 * (b // 2)
                    dst = ft[i]
                    a = A(lambda e: e.activation(dst[:], p[:], ACT.Identity, bias=col("cb2", c),
                                                 scale=col("cw2", 88 + c)), t, a_free, ft_free[i])
                    v = V(lambda e: e.scalar_tensor_tensor(dst[:, 1:S], p[:, 0:S - 1], col("cw2", 44 + c),
                                                           dst[:, 1:S], ALU.mult, ALU.add), a)
                    v = V(lambda e: e.scalar_tensor_tensor(dst[:, 2:S], p[:, 0:S - 2], col("cw2", c),
                                                           dst[:, 2:S], ALU.mult, ALU.add), v)
                    free = [v]
                    if b < 2:
                        pend[b] = v
                        return free
                    g = ft[i - 2]

                    def tail(v=v, g=g, dst=dst, f=f, i=i, u=pend[b - 2]):
                        a = A(lambda e: e.activation(g[:], g[:], ACT.Silu), u)
                        w = V(lambda e: e.tensor_tensor(g[:], g[:], dst[:], ALU.mult), v, a)
                        a = A(lambda e: e.activation(achi[:, f, :], g[:], ACT.Copy), w, a_free)
                        ready[f] = V(lambda e: e.tensor_tensor(aclo[:, f, :], g[:], achi[:, f, :].bitcast(F32),
                                                               ALU.subtract), a)
                        ft_free[i] = [ready[f]]
                        ft_free[i - 2] = [ready[f]]

                    later(b - 1, tail)
                    return free
                else:
                    if b < 2:
                        pend[b] = A(lambda e: e.activation(ft[i][:], p[:], ACT.Silu), t, a_free, ft_free[i])
                        free = [pend[b]]
                    else:
                        g = ft[i - 2]
                        v = V(lambda e: e.tensor_tensor(g[:], g[:], p[:], ALU.mult), t, pend[b - 2])
                        free = [v]
                if b >= 2:
                    g = ft[i - 2]
                    a = A(lambda e: e.activation(achi[:, f, :], g[:], ACT.Copy), v, a_free)
                    ready[f] = V(lambda e: e.tensor_tensor(aclo[:, f, :], g[:], achi[:, f, :].bitcast(F32),
                                                           ALU.subtract), a)
                    ft_free[i] = [ready[f]]
                    ft_free[i - 2] = [ready[f]]
                return free
            gemm("%s%d" % (tag, j), hT, hready, evac, banks=1)
        flush()
        return lambda k: (achi[:, k, :], aclo[:, k, :]), lambda k: ready[k]

    norm(x, xs, "g2", xt, Q.last("tensor"), Q.last("tensor", "vector", "scalar", "gpsimd"))
    act, ready = ffn("up", False)
    xt = residual("dn%d", act, ready)

    norm(x, xs, "g3", xt, Q.last("tensor"), Q.last("tensor", "vector", "scalar", "gpsimd"))
    b2 = Q.last("tensor", "vector", "scalar", "gpsimd")
    sqT = sb("sqT", AR + 0, [128, 4, S])
    skT = sb("skT", AR + 8, [128, 4, S])
    sv = sb("sv", AR + 16, [128, 4, 512])
    ohi = sb("ohi", AR + 24, [128, 8, S], F32R)
    olo = sb("olo", AR + 40, [128, 8, S], F32R)
    Qf = sb("Qf", AR + 56, [66, 8, S])
    Kf = sb("Kf", AR + 72, [66, 8, S])
    fv = sb("fv", AR + 104, [128, 4, 512])
    W5 = [sb(f"W5_{i}", AR + 112 + 2 * i, [128, 512]) for i in range(6)]
    PT2 = [sb(f"PT2_{i}", AR + 124 + 2 * i, [128, 512]) for i in range(2)]
    mk = sb("mk", AR + 128, [128, 640])
    st2 = sb("st2", AR + 130.5, [128, 96])
    s_mk = sem("s_mk")
    t_mk = load(mk[:], d["mask2"], s_mk, b2)
    r2 = {}

    def copy_evac(dst, key, scale):
        def evac(b, p, t):
            a = A(lambda e: e.activation(dst[:, b, :], p[:], ACT.Copy, scale=scale), t, b2)
            r2[key, b] = a
            return [a]
        return evac

    gemm("sq", hT, hready, copy_evac(sqT, "sq", 0.125))
    gemm("sk", hT, hready, copy_evac(skT, "sk", 1.0))
    gemm("sv", hT, hready, copy_evac(sv, "sv", 1.0))
    rs = [r2[k] for k in sorted(r2)]
    o_tok = {}

    def out_norm(n, src, j0, gname, key, *after):
        a = A(lambda e: e.activation(W5[4][:], src, ACT.Square, accum_out=st2[:, 80:81]), *after, Q.last("vector", "tensor"))
        g = G(lambda e: e.tensor_scalar(st2[:, 81:82], st2[:, 80:81], 1.0 / 512, EPS, ALU.mult, ALU.add), a)
        g = G(lambda e: e.tensor_tensor(st2[:, 82:83], st2[:, 81:82], col("mhalf"), ALU.pow), g)
        v = V(lambda e: e.tensor_scalar(W5[5][:], src, st2[:, 82:83], None, ALU.mult), g, Q.last("tensor"))

        def later():
            for k in range(4):
                t = tr(ps[6][:, k * 128:(k + 1) * 128], W5[5][:, k * 128:(k + 1) * 128], v, bank_free[6])
            fr = []
            for k in range(4):
                hi = ohi[:, j0 + k, n * 128:(n + 1) * 128]
                lo = olo[:, j0 + k, n * 128:(n + 1) * 128]
                p = ps[6][:, k * 128:(k + 1) * 128]
                a = A(lambda e, hi=hi, p=p, k=k: e.activation(hi, p, ACT.Copy, scale=col(gname, k)), t, b2, fr)
                fr = [a]
            for k in range(4):
                hi = ohi[:, j0 + k, n * 128:(n + 1) * 128]
                lo = olo[:, j0 + k, n * 128:(n + 1) * 128]
                p = ps[6][:, k * 128:(k + 1) * 128]
                w = V(lambda e, hi=hi, lo=lo, p=p, k=k: e.scalar_tensor_tensor(lo, p, col(gname, k), hi.bitcast(F32),
                                                                              ALU.mult, ALU.subtract), a)
            o_tok[key, n] = w
            bank_free[6] = [w]
        return v, later

    def att_s():
        units = [(n, h) for n in range(4) for h in range(8)]
        info = {}
        pend = []

        def s1(u):
            n, h = units[u]
            b, base, j = 4 + u % 2, 64 * (h % 2), h // 2
            W = 128 * (n + 1)
            i0 = 2 * (u % 2)
            nr, L = W5[i0], W5[i0 + 1]
            mm(ps[b][:, 0:W], sqT[base:base + 64, j, n * 128:(n + 1) * 128], skT[base:base + 64, j, 0:W],
               True, False, rs, bank_free[b])
            t = mm(ps[b][:, n * 128:W], ident, mk[:, 512:640], False, True, t_mk)
            prev = info[u - 2]["pt"] if u >= 2 else None
            a = A(lambda e: e.activation(L[:, 0:W], ps[b][:, 0:W], ACT.Abs), t, prev, b2)
            v = V(lambda e: e.tensor_scalar(nr[:, 0:W], ps[b][:, 0:W], -1.0, 0.0, ALU.mult, ALU.min), a)
            a = A(lambda e: e.activation(L[:, 0:W], L[:, 0:W], ACT.Exp, scale=-1.0), a)
            a = A(lambda e: e.activation(L[:, 0:W], L[:, 0:W], ACT.Ln, bias=col("one")), a)
            v = V(lambda e: e.tensor_tensor_scan(nr[:, 0:W][:, ::-1], nr[:, 0:W][:, ::-1], L[:, 0:W][:, ::-1], 0.0,
                                                 ALU.add, ALU.subtract), v, a)
            v = V(lambda e: e.tensor_tensor(L[:, 0:W], ps[b][:, 0:W], nr[:, 0:W], ALU.add), v)
            bank_free[b] = [v]
            a = A(lambda e: e.activation(L[:, 0:W], L[:, 0:W], ACT.Exp), v)
            info[u] = dict(T=L, tok=a, W=W)

        def s2(u):
            i = info[u]
            W = i["W"]
            for k in range(W // 128):
                t = tr(ps[6][:, k * 128:(k + 1) * 128], i["T"][:, k * 128:(k + 1) * 128], i["tok"], bank_free[6])
            i["pt"] = t
            v = V(lambda e: e.tensor_copy(PT2[u % 2][:, 0:W], ps[6][:, 0:W]), t,
                  info[u - 2]["pv"] if u >= 2 else None, b2)
            bank_free[6] = [v]
            i["ev"] = v

        def s3(u):
            n, h = units[u]
            i = info[u]
            for k in range(n + 1):
                t = mm(ps[7][:, h * 64:(h + 1) * 64], PT2[u % 2][:, k * 128:(k + 1) * 128],
                       sv[:, k, h * 64:(h + 1) * 64], k == 0, k == n, i["ev"], bank_free[7])
            i["pv"] = t
            if h == 7:
                v, later = out_norm(n, ps[7][:], 4, "gsb", "s", t)
                bank_free[7] = [v]
                pend.append(later)

        for u in range(len(units) + 3):
            if u < len(units):
                s1(u)
            if 1 <= u <= len(units):
                s2(u - 1)
            if pend:
                pend.pop()()
            if 2 <= u < len(units) + 2:
                s3(u - 2)
            yield

    fz = [sb(f"fz{i}", AR + 88 + 2 * i, [8, S]) for i in range(0)]
    fw = [W5[i] for i in range(4)]
    s_F = sem("s_F")
    fF = {}

    def evac_fl(b, p, t):
        z, e_, m_, s_ = (w[0:8, :] for w in fw)
        v = V(lambda e: e.tensor_scalar(z, p[0:8, :], col("fb", p=8), None, ALU.add), t, b2)
        a = A(lambda e: e.activation(e_, z, ACT.Abs), v)
        a = A(lambda e: e.activation(e_, e_, ACT.Exp, scale=-1.0), a)
        a = A(lambda e: e.activation(e_, e_, ACT.Ln, bias=col("one", p=8)), a)
        v2 = V(lambda e: e.tensor_scalar(m_, z, 0.0, None, ALU.min), v)
        v3 = V(lambda e: e.tensor_tensor_scan(s_, m_, e_, 0.0, ALU.add, ALU.subtract), v2, a)
        v4 = V(lambda e: e.tensor_scalar(z, s_, 8.0, None, ALU.mult), v3)
        v5 = V(lambda e: e.tensor_scalar(m_, s_, -8.0, None, ALU.mult), v3)
        m1 = V(lambda e: e.memset(Qf[64:66, :, :], 1.0), b2)
        m2 = V(lambda e: e.memset(Kf[64:66, :, :], 1.0))
        fF[0] = load(Qf[65:66, :, :], z, s_F, v4, m1)
        fF[1] = load(Kf[64:65, :, :], m_, s_F, v5, m2)
        return [v]

    A(lambda e: e.preload_act_table_set("natural_log_exp_and_others"), b2)
    gemm("fl", hT, hready, evac_fl)
    W5_guard = [fF[0], fF[1]]
    b2 = b2 + W5_guard
    background.append(att_s())

    def head_evac(dst, key):
        def evac(b, p, t):
            a = A(lambda e: e.activation(dst[0:64, 2 * b, :], p[0:64, :], ACT.Copy), t, b2)
            a2 = A(lambda e: e.activation(dst[0:64, 2 * b + 1, :], p[64:128, :], ACT.Copy))
            r2[key, b] = a2
            return [a2]
        return evac

    gemm("fq", hT, hready, head_evac(Qf, "fq"), rate=2)
    gemm("fk", hT, hready, head_evac(Kf, "fk"), rate=2)
    gemm("fv", hT, hready, copy_evac(fv, "fv", 1.0), rate=2)
    drain()
    rf = [r2[k, b] for k in ("fq", "fk", "fv") for b in range(4)] + [fF[0], fF[1]]
    s_done = Q.last("tensor", "vector", "scalar", "gpsimd")

    def att_f():
        units = [(n, h) for n in range(4) for h in range(8)]
        info = {}
        pend = []

        def s1(u):
            n, h = units[u]
            b = 4 + u % 2
            W = 128 * (n + 1)
            T = W5[u % 3]
            t = mm(ps[b][:, 0:W], Qf[:, h, n * 128:(n + 1) * 128], Kf[:, h, 0:W], True, True, rf, bank_free[b])
            c = 4 * (u % 4)
            m0 = 128 * (3 - n)
            v = V(lambda e: e.tensor_tensor_reduce(T[:, 0:W], ps[b][:, 0:W], mk[:, m0:m0 + W], 0.125, -3e38, ALU.add,
                                                   ALU.max, st2[:, c:c + 1]), t, t_mk, s_done,
                  info[u - 3]["pt"] if u >= 3 else None)
            bank_free[b] = [v]
            v = V(lambda e: e.tensor_scalar(st2[:, c + 1:c + 2], st2[:, c:c + 1], -1.0, None, ALU.mult), v)
            sm = st2[:, 16 + 8 * (n % 2) + h:17 + 8 * (n % 2) + h]
            a = A(lambda e: e.activation(T[:, 0:W], T[:, 0:W], ACT.Exp, bias=st2[:, c + 1:c + 2], accum_out=sm), v)
            info[u] = dict(T=T, tok=a, W=W)

        def s2(u):
            i = info[u]
            W = i["W"]
            for k in range(W // 128):
                t = tr(ps[6][:, k * 128:(k + 1) * 128], i["T"][:, k * 128:(k + 1) * 128], i["tok"], bank_free[6])
            i["pt"] = t
            v = V(lambda e: e.tensor_copy(PT2[u % 2][:, 0:W], ps[6][:, 0:W]), t,
                  info[u - 2]["pv"] if u >= 2 else None, s_done)
            bank_free[6] = [v]
            i["ev"] = v

        def s3(u):
            n, h = units[u]
            i = info[u]
            for k in range(n + 1):
                t = mm(ps[7][:, h * 64:(h + 1) * 64], PT2[u % 2][:, k * 128:(k + 1) * 128],
                       fv[:, k, h * 64:(h + 1) * 64], k == 0, k == n, i["ev"], bank_free[7])
            i["pv"] = t
            if h == 7:
                c = 16 + 8 * (n % 2)
                v = V(lambda e: e.reciprocal(st2[:, 40:48], st2[:, c:c + 8]), i["tok"])
                v = V(lambda e: e.tensor_tensor(W5[3][:].rearrange("p (h d) -> p h d", h=8),
                                                ps[7][:].rearrange("p (h d) -> p h d", h=8),
                                                st2[:, 40:48].unsqueeze(2).to_broadcast([128, 8, 64]), ALU.mult),
                      v, t, Q.last("scalar", "tensor"))
                bank_free[7] = [v]
                v, later = out_norm(n, W5[3][:], 0, "gfox", "f", v)
                pend.append(later)

        for u in range(len(units) + 3):
            if u < len(units):
                s1(u)
            if 1 <= u <= len(units):
                s2(u - 1)
            if pend:
                pend.pop()()
            if 2 <= u < len(units) + 2:
                s3(u - 2)
            yield

    background.append(att_f())
    drain()
    ot = [o_tok[k] for k in sorted(o_tok)]
    xt = residual("xo%d", lambda k: (ohi[:, k, :], olo[:, k, :]), lambda k: ot)
    norm(x, xs, "g4", xt, Q.last("tensor"), Q.last("tensor", "vector", "scalar", "gpsimd"))
    act, ready = ffn("vp", True)
    fg = sb("fg", AR + 104, [128, D])
    s_fg = sem("s_fg")
    t_fg = load(fg[:], d["fg"], s_fg, Q.last("tensor", "vector", "scalar", "gpsimd"))
    xt = residual("vd%d", act, ready)

    fin = Q.last("tensor", "vector", "scalar", "gpsimd")
    s_out = sem("s_out")
    o_dram = out.rearrange("b (i p) c -> p (b i) c", p=128)
    for i in range(4):
        g = row_rstd(i, xt[i])
        v = V(lambda e, i=i: e.scalar_tensor_tensor(xs[:, i, :], x[:, i, :], small[:, 8 + i:9 + i], fg[:], ALU.mult,
                                                    ALU.mult), g, t_fg, fin)
        t_out = load(o_dram[:, i, :], xs[:, i, :], s_out, v)
    t_out.used = True
    assert state["split"] == n_slots
    Q.number()

    with nc.Block() as block:
        @block.sync
        def _(e):
            Q.run("sync", e)
            e.wait_ge(s_out, 64)

        @block.tensor
        def _(e):
            Q.run("tensor", e)

        @block.vector
        def _(e):
            Q.run("vector", e)

        @block.scalar
        def _(e):
            Q.run("scalar", e)

        @block.gpsimd
        def _(e):
            Q.run("gpsimd", e)


def _tables():
    f = np.float32
    t = {}
    pos = np.arange(S, dtype=f)
    inv = f(10000.0) ** (-np.arange(0, 64, 2, dtype=f) / f(64))
    ang = pos[:, None] * inv[None, :]
    c, s = np.cos(ang).astype(f), np.sin(ang).astype(f)
    tile = lambda a: np.ascontiguousarray(a.reshape(4, 128, -1).transpose(1, 0, 2))
    t["cos"] = tile(np.concatenate([c, c], 1)).reshape(128, 256)
    t["sin"] = tile(np.concatenate([-s, s], 1)).reshape(128, 256)
    tt = pos / f(S - 1)
    bands = np.arange(1, 17, dtype=f)
    a2 = (f(2.0 * math.pi) * pos[:, None] * bands[None, :] / f(S)).astype(f)
    z = np.concatenate([tt[:, None], np.cos(a2), np.sin(a2)], -1).astype(f)
    par = np.concatenate([np.arange(0, S, 2), np.arange(1, S, 2)])
    t["zT"] = np.ascontiguousarray(z[par].T)
    deltas = np.abs(np.linspace(math.log(1e-2) / 1.5, math.log(1e-2) / 0.3, 512, dtype=f))
    t["dec"] = tile(np.exp(-tt[:, None] * deltas[None, :])[par].astype(f))
    k = np.concatenate([np.arange(0, S, 2), np.arange(S - 1, 0, -2)])
    ph = (np.outer(par, 2 * k[:256] + 1) % 2048) * (math.pi / 1024)
    t["cu"], t["su"] = tile(np.cos(ph).astype(f)), tile(-np.sin(ph).astype(f))
    ph = (np.outer(2 * np.arange(256) + 1, 2 * k + 1) % 4096) * (math.pi / 2048)
    p, m = np.cos(ph) + np.sin(ph), np.cos(ph) - np.sin(ph)
    half = lambda a: np.ascontiguousarray(a.astype(f).reshape(2, 128, 512).transpose(1, 0, 2))
    t["fp"], t["fm"] = half(p), half(m)
    t["ip"], t["im"] = tile(p.T.astype(f)), tile(m.T.astype(f))
    i, j = np.arange(128)[:, None], np.arange(128)[None, :]
    zero = np.zeros((128, 128), f)
    n = f(NEG)
    t["maskA"] = np.concatenate([np.where(j >= i, f(0), n), zero, np.where(j <= i, f(0), n)], 1).astype(f)
    t["mask2"] = np.concatenate([zero, zero, zero, np.where(j <= i, f(0), n), np.where(j < i, f(0), n)], 1).astype(f)
    return t


def _layout(inp):
    f = np.float32
    g = {k: np.asarray(v) for k, v in inp.items()}
    tb = _tables()
    VEC, NV = vec_layout()
    vec = np.zeros((128, NV), f)

    def put(name, a, p=128):
        o, w = VEC[name]
        vec[0:p, o:o + w] = a

    cols = lambda v: v.reshape(-1, 128).T
    row = lambda v: np.broadcast_to(v.reshape(1, -1), (128, v.size))
    put("g1", cols(g["norm1_g"]))
    put("g2", cols(g["norm2_g"]))
    put("g3", cols(g["attn_norm_g_2"]))
    put("g4", cols(g["ffn_norm_g_2"]))
    put("cw", cols(g["conv_w"]))
    put("cb", cols(g["conv_b"]))
    put("hd", cols(g["hy_d"]))
    put("gfox", cols(g["fox_out_g_2"]))
    put("gsb", cols(g["sb_out_g_2"]))
    put("cw2", cols(g["conv_w_2"]))
    put("cb2", cols(g["conv_b_2"]))
    put("subln", cols(g["subln_c"]))
    put("sink", row(g["sink_a"]))
    put("fb", g["forget_bias_2"].reshape(8, 1), 8)
    for a, b in (("b1", "filt_b1"), ("f1", "filt_f1"), ("b2", "filt_b2"), ("f2", "filt_f2")):
        put(a, g[b].reshape(64, 1), 64)
    for a, b in (("qna", "qn_a"), ("kna", "kn_a"), ("qnc", "qn_c"), ("knc", "kn_c"), ("lq1", "lam_q1"),
                 ("lk1", "lam_k1"), ("lq2", "lam_q2"), ("lk2", "lam_k2")):
        put(a, row(g[b]))
    put("ident", np.eye(128, dtype=f))
    put("one", 1.0)
    put("half", 0.5)
    put("mhalf", -0.5)
    put("wS0", 0.5)
    put("wD0", 0.5)
    vec[0, VEC["wS0"][0]] = 1.0
    vec[0, VEC["wD0"][0]] = 0.0
    put("cos", tb.pop("cos"))
    put("sin", tb.pop("sin"))
    put("w1", g["filt_w1"][0], 33)
    put("w2", g["filt_w2"][0], 64)

    TABLE, OFFS, total = slot_table()
    ws = np.empty(total, f)

    def pack(name, w):
        first, n_s, n, _ = TABLE[name]
        a = w.reshape(n_s, 2, 128, n).transpose(0, 2, 1, 3)
        o = OFFS[first][0]
        ws[o:o + a.size] = np.ascontiguousarray(a).reshape(-1)

    w = g["w_in"][0]
    perm = [0, 4, 1, 5, 2, 6, 3, 7]
    hp = np.concatenate([np.arange(h * 64, h * 64 + 64) for h in perm])
    pack("qa", w[:, :512][:, hp])
    pack("kva", w[:, 512:768])
    for i in range(3):
        pack("hy%d" % i, w[:, 768 + 512 * i:1280 + 512 * i])
    for i, nm in enumerate(("qc", "kc", "vc")):
        pack(nm, w[:, 2304 + 512 * i:2816 + 512 * i])
    for i, nm in enumerate(("gA", "gB", "gC")):
        for j in range(2):
            o = 3840 + 1024 * i + 512 * j
            pack("%s%d" % (nm, j), w[:, o:o + 512])
    for nm, src in (("bA", g["w_oa"][0][hp]), ("bB", g["w_ob"][0]), ("bC", g["w_oc"][0]), ("wo", g["w_out"][0]),
                    ("dn", g["ffn_w2"][0]), ("xo", g["w_out_2"][0]), ("vd", g["w_down_2"][0])):
        for j in range(2):
            pack("%s%d" % (nm, j), src[:, 512 * j:512 * j + 512])
    for tag, a, b in (("up", g["ffn_w1"][0], g["ffn_w3"][0]),
                      ("vp", g["w_up_2"][0][:, :2816], g["w_up_2"][0][:, 2816:])):
        for j in range(11):
            c = slice(256 * j, 256 * j + 256)
            pack("%s%d" % (tag, j), np.concatenate([a[:, c], b[:, c]], 1))
    w = g["w_in_2"][0]
    for nm, o in (("fq", 0), ("fk", 512), ("fv", 1024), ("sq", 1544), ("sk", 2056), ("sv", 2568)):
        pack(nm, w[:, o:o + 512])
    pad = np.zeros((1024, 128), f)
    pad[:, 0:8] = w[:, 1536:1544]
    pack("fl", pad)
    arrays = dict(tb)
    arrays["vec"] = vec
    arrays["ws"] = ws
    arrays["x"] = g["x"]
    arrays["w3"] = g["filt_w3"][0]
    arrays["fg"] = np.ascontiguousarray(row(g["final_norm_g_2"]))
    return {k: np.ascontiguousarray(v) for k, v in arrays.items()}


def kernel(**inputs):
    import concourse.bacc as bacc
    from concourse.bass_utils import run_bass_kernel_spmd

    nc = bacc.Bacc("TRN2", target_bir_lowering=False, num_devices=1)
    arrays = _layout(inputs)
    d = {k: nc.dram_tensor("in_" + k, a.shape, F32, kind="ExternalInput").ap() for k, a in arrays.items()}
    out = nc.dram_tensor("out", (1, S, D), F32, kind="ExternalOutput").ap()
    build(nc, d, out)
    r = run_bass_kernel_spmd(nc, [{"in_" + k: a for k, a in arrays.items()}], core_ids=[0])
    return r.results[0]["out"]
```

```python
import math
import numpy as np
import concourse.bass as bass
from concourse import mybir

F32 = mybir.dt.float32
F32R = mybir.dt.float32r
ALU = mybir.AluOpType
ACT = mybir.ActivationFunctionType
AX = mybir.AxisListType

S = 512
D = 1024
NEG = -1e30
EPS = 1e-6
LAM0 = 0.2
RAW, HL, LA = 3, 3, 2


def vec_layout():
    names = [
        ("g1", 8), ("g2", 8), ("g3", 8), ("g4", 8), ("cw", 36), ("cb", 12), ("hd", 8), ("gfox", 4), ("gsb", 4),
        ("cw2", 132), ("cb2", 44), ("subln", 1), ("sink", 8), ("fb", 1), ("b1", 1), ("f1", 1), ("b2", 1), ("f2", 1),
        ("qna", 64), ("kna", 64), ("qnc", 64), ("knc", 64), ("lq1", 64), ("lk1", 64), ("lq2", 64), ("lk2", 64),
        ("ident", 128), ("one", 1), ("half", 1), ("mhalf", 8), ("cos", 256), ("sin", 256),
        ("w1", 64), ("w2", 64),
    ]
    at, o = {}, 0
    for n, w in names:
        at[n] = (o, w)
        o += w
    return at, o


def groups():
    out = []
    for i in range(3):
        out.append(("hy%d" % i, 8, 512, "feat"))
    out += [("gB0", 8, 512, "feat"), ("gB1", 8, 512, "feat"), ("qa", 8, 512, "tok"), ("kva", 8, 256, "tok"),
            ("bB0", 4, 512, "feat"), ("bB1", 4, 512, "feat"), ("qc", 8, 512, "tok"), ("kc", 8, 512, "tok"),
            ("vc", 8, 512, "tok"), ("gA0", 8, 512, "feat"), ("gA1", 8, 512, "feat"), ("bA0", 4, 512, "feat"),
            ("bA1", 4, 512, "feat"), ("gC0", 8, 512, "feat"), ("gC1", 8, 512, "feat"), ("bC0", 4, 512, "feat"),
            ("bC1", 4, 512, "feat"), ("wo0", 8, 512, "tok"), ("wo1", 8, 512, "tok")]
    for i in range(11):
        out.append(("up%d" % i, 8, 512, "feat"))
    out += [("dn0", 22, 512, "tok"), ("dn1", 22, 512, "tok")]
    out += [("sq", 8, 512, "feat"), ("sk", 8, 512, "feat"), ("fl", 8, 128, "feat"), ("sv", 8, 512, "tok"),
            ("fq", 8, 512, "feat"), ("fk", 8, 512, "feat"), ("fv", 8, 512, "tok"),
            ("xo0", 8, 512, "tok"), ("xo1", 8, 512, "tok")]
    for i in range(11):
        out.append(("vp%d" % i, 8, 512, "feat"))
    out += [("vd0", 22, 512, "tok"), ("vd1", 22, 512, "tok")]
    return out


def slot_table():
    table, offs, o = {}, [], 0
    for name, nk, n, mode in groups():
        first = len(offs)
        for _ in range(nk // 2):
            offs.append((o, 2 * n))
            o += 128 * 2 * n
        table[name] = (first, nk // 2, n, mode)
    return table, offs, o


class Item:
    def __init__(self, eng, fn, after, sem=None):
        self.eng, self.fn, self.after, self.sem = eng, fn, after, sem
        self.used, self.value = False, 0


def flat(xs):
    for x in xs:
        if x is None:
            continue
        if isinstance(x, (list, tuple)):
            yield from flat(x)
        else:
            yield x


class Queues:
    IN_ORDER = ("vector", "scalar", "gpsimd")
    ENGINES = ("tensor", "vector", "scalar", "gpsimd", "sync")

    def __init__(self, nc):
        self.nc = nc
        self.q = {e: [] for e in self.ENGINES}
        self.sem = {e: nc.alloc_semaphore("done_" + e) for e in self.ENGINES[:4]}
        self.dma_count = {}

    def put(self, eng, fn, after):
        it = Item(eng, fn, list(flat(after)))
        if eng in self.IN_ORDER and self.q[eng]:
            it.after.append(self.q[eng][-1])
        for a in it.after:
            a.used = True
        self.q[eng].append(it)
        return it

    def dma(self, eng, out, in_, sem, after):
        it = Item(eng, lambda e: e.dma_start(out, in_), list(flat(after)), sem)
        for a in it.after:
            a.used = True
        n = self.dma_count.get(id(sem), 0) + 16
        self.dma_count[id(sem)] = n
        it.value = n
        self.q[eng].append(it)
        return it

    def last(self, *engs):
        return [self.q[e][-1] for e in engs if self.q[e]]

    def number(self):
        for e in self.ENGINES[:4]:
            n = 0
            for it in self.q[e]:
                if it.sem is None and it.used:
                    n += 1
                    it.value = n

    def run(self, name, eng):
        seen = {}
        for it in self.q[name]:
            need = {}
            for a in it.after:
                sem = a.sem if a.sem is not None else self.sem[a.eng]
                if a.value > need.get(id(sem), (0, None))[0]:
                    need[id(sem)] = (a.value, sem)
            for k, (v, sem) in need.items():
                if seen.get(k, 0) < v:
                    eng.wait_ge(sem, v)
                    seen[k] = v
            ins = it.fn(eng)
            if it.sem is not None:
                ins.then_inc(it.sem, 16)
            elif it.used:
                ins.then_inc(self.sem[name], 1)


def build(nc, d, out):
    B0 = 16512
    VEC, NV = vec_layout()
    TABLE, OFFS, _ = slot_table()

    def sb(name, kb, shape, dt=F32):
        return nc.alloc_sbuf_tensor_at(name, shape, dt, offset=B0 + int(kb * 1024))

    AR = 75
    hThi = sb("hThi", 0, [128, 8, S], F32R)
    hTlo = sb("hTlo", 16, [128, 8, S], F32R)
    wraw = [sb(f"wraw{i}", 32 + 4 * i, [128, 1024]) for i in range(RAW)]
    whi = [sb(f"whi{i}", 44 + 4 * i, [128, 1024], F32R) for i in range(HL)]
    wlo = [sb(f"wlo{i}", 56 + 4 * i, [128, 1024], F32R) for i in range(HL)]
    vec = sb("vec", 68, [128, NV])
    ps = [nc.alloc_psum_tensor(f"ps{i}", [128, 512], F32) for i in range(8)]
    bank_free = [[] for _ in range(8)]

    Q = Queues(nc)

    def V(fn, *after):
        return Q.put("vector", fn, after)

    def A(fn, *after):
        return Q.put("scalar", fn, after)

    def G(fn, *after):
        return Q.put("gpsimd", fn, after)

    def P(fn, *after):
        return Q.put("tensor", fn, after)

    def sem(name):
        return nc.alloc_semaphore(name)

    def load(out_, in_, s, *after, eng="sync"):
        return Q.dma(eng, out_, in_, s, after)

    def col(name, i=0, n=1, p=128):
        o, _ = VEC[name]
        return vec[0:p, o + i:o + i + n]

    ident = col("ident", 0, 128)

    s_vec = sem("s_vec")
    t_vec = load(vec[:], d["vec"], s_vec)

    s_raw = [sem(f"s_raw{i}") for i in range(RAW)]
    dma_tok, hi_tok, lo_tok, pe_tok = {}, {}, {}, {}
    n_slots = len(OFFS)
    state = {"dma": 0, "split": 0}

    def raw_view(i):
        o, w = OFFS[i]
        return d["ws"][o:o + 128 * w].rearrange("(p c) -> p c", p=128), w

    def issue_dma(upto):
        while state["dma"] < min(upto, n_slots):
            i = state["dma"]
            src, w = raw_view(i)
            dma_tok[i] = load(wraw[i % RAW][:, 0:w], src, s_raw[i % RAW],
                              lo_tok[i - RAW] if i >= RAW else None)
            state["dma"] += 1

    on_pool = set()
    for nm in ('qc', 'kc', 'vc', 'hy0', 'hy1', 'hy2'):
        on_pool |= set(range(TABLE[nm][0], TABLE[nm][0] + TABLE[nm][1]))

    def issue_split(upto):
        while state["split"] < min(upto, n_slots):
            i = state["split"]
            issue_dma(i + 1)
            _, w = raw_view(i)
            r, h = wraw[i % RAW], i % HL
            hi_tok[i] = A(lambda e, r=r, h=h, w=w: e.activation(whi[h][:, 0:w], r[:, 0:w], ACT.Copy),
                          dma_tok[i], pe_tok[i - HL] if i >= HL else None)
            put = G if i in on_pool else V
            lo_tok[i] = put(lambda e, r=r, h=h, w=w: e.tensor_tensor(wlo[h][:, 0:w], r[:, 0:w],
                                                                 whi[h][:, 0:w].bitcast(F32), ALU.subtract),
                          hi_tok[i])
            state["split"] += 1
            issue_dma(i + RAW)

    background, deferred = [], []

    def later(n, fn):
        deferred.append([n, fn])

    def flush():
        for x in sorted(deferred, key=lambda x: x[0]):
            x[1]()
        deferred.clear()

    def tick():
        for x in deferred:
            x[0] -= 1
        due = [x for x in deferred if x[0] <= 0]
        deferred[:] = [x for x in deferred if x[0] > 0]
        for x in due:
            x[1]()

    def pump(n=1):
        for _ in range(n):
            if background:
                try:
                    next(background[0])
                except StopIteration:
                    background.pop(0)

    def drain():
        while background:
            pump()

    turn = [0]

    def gemm(name, act, ready, evac, rate=1, banks=0):
        first, n_s, n, mode = TABLE[name]
        b0 = 4 * turn[0] if banks == 1 else 3 if banks == 2 else 0
        turn[0] = (turn[0] + 1) % 2 if banks == 1 else 1
        nb = 4 if mode == "tok" else n // 128
        for s in range(n_s):
            i = first + s
            issue_split(i + 1 + LA)
            h = i % HL
            for b in range(nb):
                for kk in range(2):
                    k = 2 * s + kk
                    ahi, alo = act(k)
                    if mode == "tok":
                        c0, c1 = kk * n, kk * n + n
                        pairs = [(ahi[:, b * 128:b * 128 + 128], whi[h][:, c0:c1]),
                                 (ahi[:, b * 128:b * 128 + 128], wlo[h][:, c0:c1]),
                                 (alo[:, b * 128:b * 128 + 128], whi[h][:, c0:c1])]
                        o = ps[b0 + b][:, 0:n]
                    else:
                        c0 = kk * n + b * 128
                        pairs = [(whi[h][:, c0:c0 + 128], ahi), (whi[h][:, c0:c0 + 128], alo),
                                 (wlo[h][:, c0:c0 + 128], ahi)]
                        o = ps[b0 + b][:]
                    for j, (l, r) in enumerate(pairs):
                        st = s == 0 and kk == 0 and j == 0
                        sp = s == n_s - 1 and kk == 1 and j == 2
                        w = [lo_tok[i]] if (b == 0 and kk == 0 and j == 0) else []
                        if st:
                            w = w + [bank_free[b0 + b]]
                        if j == 0 and ready is not None:
                            w = w + [ready(k, b)]
                        last = P(lambda e, o=o, l=l, r=r, st=st, sp=sp: e.matmul(o, l, r, start=st, stop=sp), *w)
                if s == n_s - 1:
                    bank_free[b0 + b] = evac(b, ps[b0 + b], last)
                if b < nb - 1:
                    pump((b + 1) * rate // nb - b * rate // nb)
            pe_tok[i] = last
            tick()
            pump(rate - (nb - 1) * rate // nb)

    def mm(o, l, r, st, sp, *after):
        return P(lambda e: e.matmul(o, l, r, start=st, stop=sp), *after)

    def tr(o, i, *after, n=128):
        return P(lambda e: e.transpose(o, i, ident[0:n, 0:n] if n < 128 else ident), t_vec, *after)

    def split_out(hi, lo, src, scale, *after):
        a = A(lambda e: e.activation(hi, src, ACT.Copy, scale=scale), *after)
        v = V(lambda e: e.scalar_tensor_tensor(lo, src, scale, hi.bitcast(F32), ALU.mult, ALU.subtract), a)
        return v

    small = sb("small", 68 + (NV * 4 + 31) // 32 * 32 / 1024, [128, 64])
    assert NV * 4 + 64 * 4 <= 7 * 1024, NV

    h_ready = {}

    def hT(k):
        return hThi[:, k, :], hTlo[:, k, :]

    def half_square(x, i, half, junk, *after):
        return A(lambda e: e.activation(junk, x[:, i, half * 512:half * 512 + 512], ACT.Square,
                                        accum_out=small[:, 48 + 2 * i + half:49 + 2 * i + half]), *after)

    def row_rstd(i, halves):
        c = 48 + 2 * i
        g = G(lambda e: e.tensor_scalar(small[:, i:i + 1], small[:, c:c + 1], 1.0 / D, EPS, ALU.mult, ALU.add),
              halves[0], t_vec)
        g = G(lambda e: e.tensor_scalar(small[:, 4 + i:5 + i], small[:, c + 1:c + 2], 1.0 / D, small[:, i:i + 1],
                                        ALU.mult, ALU.add), halves[1], g)
        return G(lambda e: e.tensor_tensor(small[:, 8 + i:9 + i], small[:, 4 + i:5 + i], col("mhalf"), ALU.pow), g)

    def scaled_rows(x, xs, xs_free):
        toks = []

        def row(i, halves):
            r = row_rstd(i, halves)
            toks.append(V(lambda e: e.tensor_scalar(xs[:, i, :], x[:, i, :], small[:, 8 + i:9 + i], None, ALU.mult),
                          r, xs_free()))
        return row, toks

    def norm(xs, g, toks, h_free, early):
        def across(i, k):
            b = (4 + k) % 8
            return tr(ps[b][:, i * 128:(i + 1) * 128], xs[:, i, k * 128:(k + 1) * 128], toks[i],
                      bank_free[b] if i == 0 else None)

        for i in range(early):
            for k in range(8):
                across(i, k)
        for k in range(8):
            b = (4 + k) % 8
            for i in range(early, 4):
                t = across(i, k)
            v = split_out(hThi[:, k, :], hTlo[:, k, :], ps[b][:], col(g, k), t, h_free)
            bank_free[b] = [v]
            h_ready[k] = v
        turn[0] = 1
        return v

    s_x = [sem(f"s_x{i}") for i in range(4)]
    s_z = sem("s_z")
    x1 = sb("x1", AR + 32, [128, 4, D])
    x_dram = d["x"].rearrange("b (i p) c -> p (b i) c", p=128)
    zT = sb("zT", AR + 126, [33, S])
    t_z = load(zT[:], d["zT"], s_z)
    tx = [load(x1[:, i, :], x_dram[:, i, :], s_x[i]) for i in range(4)]
    junk1 = sb("junk1", AR, [128, 512])
    issue_dma(RAW)

    s_f = sem("s_f")
    w3 = sb("w3", AR + 88, [64, 4, 512])
    cu = sb("cu", AR + 48, [128, 4, 256])
    su = sb("su", AR + 52, [128, 4, 256])
    dec = sb("dec", AR + 80, [128, 4, 512])
    fs = sb("fs", AR + 64, [128, 4, 512])
    fd = sb("fd", AR + 72, [128, 4, 512])
    sq = [sb(f"sq{i}", AR + 32 + 2 * i, [128, 512]) for i in range(4)]
    acc = sb("acc", AR + 40, [128, 512])
    h1 = sb("h1", AR + 128, [64, S])
    h2 = sb("h2", AR + 96, [64, S])
    ma = [sb(f"ma{i}", AR + 104 + 2 * i, [64, S]) for i in range(4)]
    et = [sb("et0", AR + 102, [128, 512]), sb("et1", AR + 130, [128, 512])]
    Cre = [sb(f"Cre{o}", AR + 16 * o, [128, 4, 512]) for o in range(2)]
    Cim = [sb(f"Cim{o}", AR + 16 * o + 8, [128, 4, 512]) for o in range(2)]
    fwd = [sb("fp", AR + 56, [128, 2, 512]), sb("fm", AR + 60, [128, 2, 512])]
    inv = [sb("ip", AR + 88, [128, 4, 256]), sb("im", AR + 92, [128, 4, 256])]

    t_w3 = load(w3[:], d["w3"].rearrange("h (g c) -> h g c", g=4), s_f)
    t_f = load(dec[:], d["dec"], s_f)
    t_f = load(cu[:], d["cu"], s_f)
    t_f = load(su[:], d["su"], s_f)
    t_f = load(fwd[0][:], d["fp"], s_f)
    t_f = load(fwd[1][:], d["fm"], s_f)

    TWO_PI = 2 * math.pi
    MAGIC = 1.5 * 2 ** 23
    C1 = 6.28125
    C2 = TWO_PI - C1

    def sine(dst, src, b, f, t):
        t = V(lambda e: e.tensor_scalar(ma[0][:], src, col(b, p=64), col(f, p=64), ALU.add, ALU.mult), t)
        u = V(lambda e: e.tensor_scalar(ma[1][:], ma[0][:], 1 / TWO_PI, MAGIC, ALU.mult, ALU.add), t)
        u = V(lambda e: e.tensor_scalar(ma[2][:], ma[1][:], MAGIC, None, ALU.subtract), u)
        u = V(lambda e: e.scalar_tensor_tensor(ma[3][:], ma[2][:], -C1, ma[0][:], ALU.mult, ALU.add), u)
        u = V(lambda e: e.scalar_tensor_tensor(ma[1][:], ma[2][:], -C2, ma[3][:], ALU.mult, ALU.add), u)
        u = V(lambda e: e.tensor_scalar(ma[3][:], ma[1][:], 3.1415925, -3.1415925, ALU.min, ALU.max), u)
        return t, A(lambda e: e.activation(dst, ma[3][:], ACT.Sin), u)

    row, row_toks = scaled_rows(x1, x1, lambda: None)
    for i in range(4):
        row(i, [half_square(x1, i, h, junk1[:], tx[i]) for h in range(2)])
    issue_split(LA)
    norm_tok = norm(x1, "g1", row_toks, None, 0)
    x_done = Q.last("tensor", "scalar", "vector")
    w3v = w3[:]
    ma_done = []
    rn_tok = {}
    lam = small[:, 40:41]
    t_lam = []

    def filters():
        f_free = []
        bf, t_h1 = sine(h1[:], ps[6][0:64, :], "b1", "f1",
                        mm(ps[6][0:64, :], col("w1", 0, 64, p=33), zT[:], True, True, t_z, t_vec, bank_free[6]))
        bank_free[6] = [bf]
        yield
        bf, t_h2 = sine(h2[:], ps[7][0:64, :], "b2", "f2",
                        mm(ps[7][0:64, :], col("w2", 0, 64, p=64), h1[:], True, True, t_h1, bank_free[7]))
        bank_free[7] = [bf]
        yield
        t_ws = []
        for o in range(2):
            f, b = w3v[:, 2 * o, :], w3v[:, 2 * o + 1, :]
            v = V(lambda e, b=b, f=f: e.tensor_tensor(ma[0][:], f, b, ALU.add), t_f, t_h2)
            v = V(lambda e, b=b, f=f: e.tensor_tensor(b, f, b, ALU.subtract), v)
            t_ws.append(V(lambda e, f=f: e.tensor_copy(f, ma[0][:]), v))
        ma_done.extend(Q.last("vector", "scalar", "tensor"))
        yield
        v1 = V(lambda e: e.tensor_tensor_reduce(et[0][:, 0:64], col("lq1", 0, 64), col("lk1", 0, 64), 1.0, 0.0, ALU.mult,
                                                ALU.add, small[:, 36:37]), t_vec)
        v2 = V(lambda e: e.tensor_tensor_reduce(et[0][:, 64:128], col("lq2", 0, 64), col("lk2", 0, 64), 1.0, 0.0,
                                                ALU.mult, ALU.add, small[:, 37:38]))
        a = A(lambda e: e.activation(small[:, 38:40], small[:, 36:38], ACT.Exp), v1, v2)
        v = V(lambda e: e.tensor_tensor(small[:, 41:42], small[:, 39:40], small[:, 38:39], ALU.subtract), a)
        t_lam.append(V(lambda e: e.tensor_scalar(lam, small[:, 41:42], LAM0, None, ALU.subtract), v))
        yield

        sq_free = [None] * 4
        acc_free = None
        for o in range(2):
            td, acc_tok = [], acc_free
            for tt in range(4):
                now = []
                for j, dst in enumerate((fs, fd)):
                    b = 4 + j
                    t = mm(ps[b][:], h2[:, tt * 128:(tt + 1) * 128], w3v[:, 2 * o + j, :], True, True,
                           t_h2, t_ws[o], bank_free[b])
                    v = V(lambda e, b=b, dst=dst, tt=tt: e.tensor_tensor(dst[:, tt, :], ps[b][:], dec[:, tt, :],
                                                                         ALU.mult), t, t_f, f_free)
                    bank_free[b] = [v]
                    td.append(v)
                    i = 2 * (tt % 2) + j
                    a = A(lambda e, i=i, dst=dst, tt=tt: e.activation(sq[i][:], dst[:, tt, :], ACT.Square), v, x_done,
                          sq_free[i])
                    if tt == 0 and j == 1:
                        a = A(lambda e, i=i: e.activation(sq[i][0:1, :], sq[i - 1][0:1, :], ACT.Copy))
                    now.append(a)
                    if tt == 0 and j == 0:
                        continue
                    p, q = (sq[0], sq[1]) if tt == 0 else (acc, sq[i])
                    acc_tok = G(lambda e, p=p, q=q: e.tensor_tensor(acc[:], p[:], q[:], ALU.add), a, acc_tok)
                    sq_free[i] = acc_tok
                    if tt == 0:
                        sq_free[0] = acc_tok
                yield
            for kt in range(2):
                for j, (tab, src, dst) in enumerate(((cu, fs, Cre[o]), (su, fd, Cim[o]))):
                    be, bo = 4 + 2 * j, 5 + 2 * j
                    for b, t0 in ((be, 0), (bo, 2)):
                        for t1 in range(2):
                            t = mm(ps[b][:], tab[:, t0 + t1, kt * 128:(kt + 1) * 128], src[:, t0 + t1, :], t1 == 0, t1 == 1,
                                   td, t_f, bank_free[b])
                        if b == be:
                            a = A(lambda e, be=be, j=j: e.activation(et[j][:], ps[be][:], ACT.Copy), t,
                                  Q.last("vector"))
                    v1 = V(lambda e, bo=bo, j=j, dst=dst, kt=kt: e.tensor_tensor(dst[:, kt, :], ps[bo][:], et[j][:], ALU.add),
                           t, a, x_done)
                    if j == 0:
                        v2 = V(lambda e, bo=bo, dst=dst, kt=kt: e.tensor_tensor(dst[:, 2 + kt, :], et[0][:], ps[bo][:],
                                                                                ALU.subtract))
                    else:
                        v2 = V(lambda e, bo=bo, dst=dst, kt=kt: e.tensor_tensor(dst[:, 2 + kt, :], ps[bo][:], et[1][:],
                                                                                ALU.subtract))
                    bank_free[be] = [a]
                    bank_free[bo] = [v2]
                yield
            for c in range(4):
                t = mm(ps[6][:, c:c + 1], acc[:, c * 128:(c + 1) * 128], col("half"), True, True, acc_tok, bank_free[6])
            acc_free = t
            v = V(lambda e: e.tensor_scalar(small[:, 24:28], ps[6][:, 0:4], EPS, None, ALU.add), t)
            bank_free[6] = [v]
            g = G(lambda e: e.tensor_tensor(small[:, 28:32], small[:, 24:28], col("mhalf", 0, 4), ALU.pow), v)
            V(lambda e, o=o: e.tensor_scalar(small[:, 16 + 4 * o:20 + 4 * o], small[:, 28:32], 1.0 / 1024, None,
                                             ALU.mult), g)
            rn_tok[o] = V(lambda e, o=o: e.tensor_scalar(small[:, 56 + 4 * o:60 + 4 * o], small[:, 28:32], -1.0 / 1024,
                                                         None, ALU.mult), g)
            f_free = Q.last("tensor", "scalar", "vector")

    uT = [sb(f"uT{i}", AR + 104 + 8 * i, [128, 4, S]) for i in range(3)]
    tok = sb("tok", AR + 48, [128, 4, 512])
    U = sb("U", AR + 64, [128, 4, 512])
    W = sb("W", AR + 72, [128, 4, 512])
    tm = [sb(f"tm{i}", AR + 80 + 2 * i, [128, 512]) for i in range(4)]
    sd = sb("sd", AR + 96, [128, 4, 512])
    dv = [sb(f"dv{i}", AR + 128 + 2 * i, [128, 512]) for i in range(2)]
    obhi = sb("obhi", AR + 0, [128, 4, S], F32R)
    oblo = sb("oblo", AR + 8, [128, 4, S], F32R)
    gate = [sb(f"gate{i}", AR + 32 + 8 * i, [128, 4, S]) for i in range(2)]

    vT, x1T, x2T = uT
    ob_tok = [None]

    def hyena():
        f_done.extend(Q.last("tensor", "vector", "scalar", "gpsimd"))
        t_inv = load(inv[0][:], d["ip"], s_inv, f_done)
        t_inv = load(inv[1][:], d["im"], s_inv, f_done)
        src, src_tok = vT, [u_tok[0, b] for b in range(4)]
        sd_free, tok_free, y_free = f_done, f_done, f_done
        sdt = [None] * 4

        def both(c, src, *after):
            lo_, hi_ = src[:, c, 0:256], src[:, c, 256:512][:, ::-1]
            g = G(lambda e: e.tensor_tensor(sd[:, c, 0:256], lo_, hi_, ALU.add), *after)
            v = V(lambda e: e.tensor_tensor(sd[:, c, 256:512], lo_, hi_, ALU.subtract), *after)
            sdt[c] = [g, v]

        for o in range(2):
            tk = []
            if o == 0:
                for c in range(4):
                    both(c, src, src_tok[c], sd_free)
            yield
            for tt in range(4):
                b = 4 + tt
                for c in range(4):
                    t = tr(ps[b][:, c * 128:(c + 1) * 128], sd[:, c, tt * 128:(tt + 1) * 128], sdt[c], bank_free[b])
                a = A(lambda e, b=b, tt=tt: e.activation(tok[:, tt, :], ps[b][:], ACT.Copy), t, tok_free)
                bank_free[b] = [a]
                tk.append(a)
            sd_free = Q.last("tensor")
            yield
            yt = []
            for ft in range(4):
                bp, bm = (4, 5) if ft % 2 == 0 else (6, 7)
                for bk, tab, s0 in ((bp, fwd[0], 0 if ft < 2 else 2), (bm, fwd[1], 2 if ft < 2 else 0)):
                    for tt in range(2):
                        t = mm(ps[bk][:], tab[:, tt, ft * 128:(ft + 1) * 128], tok[:, s0 + tt, :], tt == 0, tt == 1,
                               tk[s0 + tt], bank_free[bk])
                cre, cim = Cre[o][:, ft, :], Cim[o][:, ft, :]
                t0, t1 = tm[2 * (ft % 2)], tm[2 * (ft % 2) + 1]
                tm_free = yt[-2] if len(yt) >= 2 else y_free
                V(lambda e, bp=bp, cre=cre, ft=ft: e.tensor_tensor(U[:, ft, :], ps[bp][:], cre, ALU.mult), t, y_free)
                v1 = V(lambda e, bm=bm, cim=cim, t0=t0: e.tensor_tensor(t0[:], ps[bm][:], cim, ALU.mult), tm_free)
                G(lambda e, ft=ft, t0=t0: e.tensor_tensor(U[:, ft, :], U[:, ft, :], t0[:], ALU.subtract), v1)
                V(lambda e, bp=bp, cim=cim, ft=ft: e.tensor_tensor(W[:, ft, :], ps[bp][:], cim, ALU.mult))
                v3 = V(lambda e, bm=bm, cre=cre, t1=t1: e.tensor_tensor(t1[:], ps[bm][:], cre, ALU.mult))
                g = G(lambda e, ft=ft, t1=t1: e.tensor_tensor(W[:, ft, :], W[:, ft, :], t1[:], ALU.add), v3)
                bank_free[bp] = [v3]
                bank_free[bm] = [v3]
                yt.append(g)
                yield
            tok_free = Q.last("tensor")
            nt = []
            for c in range(4):
                b = 4 + c
                z = dv[c % 2]
                z0, z1 = z[:, 0:256], z[:, 256:512][:, ::-1]
                s_, d_ = ps[b][:, 0:256], ps[b][:, 256:512]
                rp, rm = small[:, 16 + 4 * o + c:17 + 4 * o + c], small[:, 56 + 4 * o + c:57 + 4 * o + c]
                a = A(lambda e, c=c, o=o, src=src, z=z: e.activation(z[:], src[:, c, :], ACT.Copy,
                                                                     scale=col("hd", 4 * o + c)), Q.last("vector"))
                for ap, parts in ((s_, ((U, 0, 0), (U, 0, 1), (W, 1, 2), (W, 1, 3))),
                                  (d_, ((W, 1, 0), (W, 1, 1), (U, 0, 2), (U, 0, 3)))):
                    for i, (y, tb, ft) in enumerate(parts):
                        t = mm(ap, y[:, ft, c * 128:(c + 1) * 128], inv[tb][:, ft, :], i == 0, i == 3, yt[ft], t_inv,
                               bank_free[b])
                for out_, in_, r in ((z0, s_, rp), (z0, d_, rp), (z1, s_, rp), (z1, d_, rm)):
                    v = V(lambda e, out_=out_, in_=in_, r=r: e.scalar_tensor_tensor(out_, in_, r, out_, ALU.mult, ALU.add),
                          t, a, rn_tok[o])
                bank_free[b] = [v]
                g = uT[1 + o]
                v = V(lambda e, c=c, g=g, z=z: e.tensor_tensor(g[:, c, :], g[:, c, :], z[:], ALU.mult), v,
                      u_tok[1 + o, c])
                nt.append(v)
                if o == 0:
                    both(c, g, v, sd_free)
                else:
                    a = A(lambda e, c=c: e.activation(obhi[:, c, :], x2T[:, c, :], ACT.Copy), v, y0_done)
                    ob_tok[0] = V(lambda e, c=c: e.tensor_tensor(oblo[:, c, :], x2T[:, c, :],
                                                                 obhi[:, c, :].bitcast(F32), ALU.subtract), a)
                yield
            y_free = Q.last("tensor")
            y0_done = Q.last("vector", "gpsimd")
            src, src_tok = x1T, nt

    s_inv = sem("s_inv")
    hready = lambda k, b: h_ready[k]
    u_tok = {}
    f_done = []
    background += [filters(), hyena()]
    for gidx in range(3):
        def evac(b, p, t, gidx=gidx):
            assert ma_done
            f = gidx * 4 + b
            dst = uT[gidx][:, b, :]
            a = A(lambda e: e.activation(dst, p[:], ACT.Identity, bias=col("cb", f), scale=col("cw", 12 + f)),
                  t, ma_done)
            v = V(lambda e: e.scalar_tensor_tensor(dst[:, 1:S], p[:, 0:S - 1], col("cw", f), dst[:, 1:S],
                                                   ALU.mult, ALU.add), a)
            v = V(lambda e: e.scalar_tensor_tensor(dst[:, 0:S - 1], p[:, 1:S], col("cw", 24 + f),
                                                   dst[:, 0:S - 1], ALU.mult, ALU.add), v)
            u_tok[gidx, b] = v
            return [v]
        gemm("hy%d" % gidx, hT, hready, evac, rate=2)
    gate_n = [0]
    gate_tok, gate_free, mtok = {}, [f_done, f_done], {}

    def gate_group(name, rate=1):
        i = gate_n[0] % 2
        gate_n[0] += 1

        def evac(b, p, t):
            a = A(lambda e: e.activation(gate[i][:, b, :], p[:], ACT.Tanh, scale=0.5), t, gate_free[i], x_done)
            gate_tok[i, b] = a
            return [a]
        gemm(name, hT, hready, evac, rate=rate)
        return i

    for half in range(2):
        gate_group("gB%d" % half, rate=2)
    drain()
    hy_done = Q.last("tensor", "vector", "scalar", "gpsimd")

    rt = sb("rt", AR + 64, [128, 8, 4, 64])
    raw = [sb(f"raw{i}", AR + 72 + 2 * i, [128, 512]) for i in range(4)]
    tp = [sb(f"tp{i}", AR + 80 + 2 * i, [128, 512]) for i in range(3)]
    cosv = col("cos", 0, 256).rearrange("p (t d) -> p t d", t=4)
    sinv = col("sin", 0, 256).rearrange("p (t d) -> p t d", t=4)
    def rope_tables():
        for gi, nm in enumerate(("qna", "kna", "qnc", "knc")):
            o, _ = VEC[nm]
            g0 = vec[:, o:o + 64].unsqueeze(1).to_broadcast([128, 4, 64])
            glo = vec[:, o:o + 32].unsqueeze(1).to_broadcast([128, 4, 32])
            ghi = vec[:, o + 32:o + 64].unsqueeze(1).to_broadcast([128, 4, 32])
            V(lambda e, gi=gi, g0=g0: e.tensor_tensor(rt[:, 2 * gi, :, :], cosv, g0, ALU.mult), hy_done, t_vec)
            V(lambda e, gi=gi, ghi=ghi: e.tensor_tensor(rt[:, 2 * gi + 1, :, 0:32], sinv[:, :, 0:32], ghi, ALU.mult))
            V(lambda e, gi=gi, glo=glo: e.tensor_tensor(rt[:, 2 * gi + 1, :, 32:64], sinv[:, :, 32:64], glo, ALU.mult))
            yield

    background.append(rope_tables())
    nsink = small[:, 24:32]
    t_nsink = V(lambda e: e.tensor_scalar(nsink, col("sink", 0, 8), -1.0, None, ALU.mult), hy_done)

    qaT = sb("qaT", AR + 86, [128, 4, S])
    kaT = sb("kaT", AR + 94, [128, 1, S])
    va = sb("va", AR + 96, [128, 4, 128])
    T8 = [sb(f"T8_{i}", AR + (98, 99.5, 101, 0)[i], [128, 384]) for i in range(4)]
    PT = [sb(f"PT{i}", AR + (102.5, 104, 1.5)[i], [128, 384]) for i in range(3)]
    b_done = []
    tq = [tp[2], sb("tq1", AR + 129.5, [128, 512])]
    maskA = sb("maskA", AR + 105.5, [128, 384])
    st = sb("st", AR + 107, [128, 128])
    qcT = sb("qcT", AR + 107.5, [128, 4, S])
    kcT = sb("kcT", AR + 115.5, [128, 4, S])
    vc = sb("vc", AR + 123.5, [128, 4, 512])
    oahi = sb("oahi", AR + 48, [128, 4, S], F32R)
    oalo = sb("oalo", AR + 56, [128, 4, S], F32R)
    merged = sb("merged", AR + 16, [128, 8, S])
    s_m = sem("s_m")
    t_maskA = load(maskA[:], d["maskA"], s_m, hy_done)

    raw_free = [[] for _ in range(4)]
    tp_free = [[] for _ in range(2)]
    tq_free = [[], []]
    steps = []

    def rope(b, p, t, H, ti, dst, toks, key):
        W = H * 64
        hv = lambda ap: ap.rearrange("p (h d) -> p h d", h=H)
        r, q0, q1 = raw[b][:, 0:W], tp[b % 2][:, 0:W], tq[b % 2][:, 0:W]
        s0 = 64 + 16 * b
        ss_, ms_, rs_ = (st[:, s0 + i * 8:s0 + i * 8 + H] for i in (0, 1, 0))
        done = A(lambda e: e.activation(r, p[:, 0:W], ACT.Copy), t, raw_free[b], hy_done)
        a = A(lambda e: e.activation(q0, r, ACT.Square), done, tp_free[b % 2])
        v = V(lambda e: e.tensor_reduce(ss_, hv(q0), AX.X, ALU.add), a)
        tp_free[b % 2] = [v]
        g = G(lambda e: e.tensor_scalar(ms_, ss_, 1.0 / 64, EPS, ALU.mult, ALU.add), v)
        g_rs = G(lambda e: e.tensor_tensor(rs_, ms_, col("mhalf", 0, H), ALU.pow), g)
        nj = W // 128

        cg = rt[:, 2 * ti, b, :].unsqueeze(1).to_broadcast([128, H, 64])
        sa = rt[:, 2 * ti + 1, b, 0:32].unsqueeze(1).to_broadcast([128, H, 32])
        sb_ = rt[:, 2 * ti + 1, b, 32:64].unsqueeze(1).to_broadcast([128, H, 32])
        r1, r2_ = hv(r)[:, :, 0:32], hv(r)[:, :, 32:64]
        o1, o2 = hv(q1)[:, :, 0:32], hv(q1)[:, :, 32:64]
        tok = {}

        def scale():
            tok[0] = V(lambda e: e.tensor_tensor(hv(r), hv(r), rs_.unsqueeze(2).to_broadcast([128, H, 64]), ALU.mult),
                       g_rs)
            G(lambda e: e.tensor_tensor(o1, r2_, sa, ALU.mult), tok[0], tq_free[b % 2])
            tok[1] = G(lambda e: e.tensor_tensor(o2, r1, sb_, ALU.mult))

        def times_cos():
            tok[2] = V(lambda e: e.tensor_tensor(hv(q0), hv(r), cg, ALU.mult), tok[0], tp_free[b % 2])

        def add():
            tok[3] = V(lambda e: e.tensor_tensor(r, q0, q1, ALU.add), tok[2], tok[1])
            tp_free[b % 2] = tq_free[b % 2] = [tok[3]]

        def across():
            for j in range(nj):
                t = tr(ps[4 + b % 2][:, j * 128:(j + 1) * 128], r[:, j * 128:(j + 1) * 128], tok[3], bank_free[4 + b % 2])
            raw_free[b] = [t]
            a = A(lambda e: e.activation(dst[:, :, b * 128:(b + 1) * 128],
                                         ps[4 + b % 2][:, 0:W].rearrange("p (j t) -> p j t", j=nj), ACT.Copy), t, hy_done)
            bank_free[4 + b % 2] = [a]
            toks[key, b] = a

        steps.append((scale, times_cos, add))
        later(3 + b // 2, across)
        if b % 2:
            two = tuple(steps)
            steps.clear()

            def products():
                for i in range(2):
                    for step in two:
                        step[i]()

            def sums():
                for step in two:
                    step[2]()

            later(1 + b // 2, products)
            later(2 + b // 2, sums)
        return [done]

    ra = {}

    def evac_kva(b, p, t):
        a2 = A(lambda e: e.activation(va[:, b, :], p[:, 128:256], ACT.Copy), t, hy_done)
        return rope(b, p, t, 2, 1, kaT, ra, "k") + [a2]

    gemm("qa", hT, hready, lambda b, p, t: rope(b, p, t, 8, 0, qaT, ra, "q"), rate=2)
    drain()
    gemm("kva", hT, hready, evac_kva)

    def att_a():
        units = [(n, h) for n in range(4) for h in range(8)]
        info = {}
        while len(ra) < 8 or not b_done:
            yield
        ra_all = list(ra.values())

        def s1(u):
            n, h = units[u]
            b, j, base, kv = 4 + u % 2, h % 4, 64 * (h // 4), h // 4
            k0, k1 = max(n - 1, 0), min(n + 1, 3)
            W = 128 * (k1 - k0 + 1)
            m0 = 0 if n > 0 else 128
            t = mm(ps[b][:, 0:W], qaT[base:base + 64, j, n * 128:(n + 1) * 128], kaT[base:base + 64, 0, k0 * 128:k0 * 128 + W],
                   True, True, ra_all, bank_free[b])
            T = T8[u % 4]
            c = 24 + 8 * (u % 4)
            prev = info[u - 4]["pt"] if u >= 4 else b_done
            v = V(lambda e: e.tensor_tensor_reduce(T[:, 0:W], ps[b][:, 0:W], maskA[:, m0:m0 + W], -0.125, nsink[:, h:h + 1],
                                                   ALU.add, ALU.min, st[:, c:c + 1]), t, t_maskA, prev, t_nsink)
            bank_free[b] = [v]
            a1 = A(lambda e: e.activation(T[:, 0:W], T[:, 0:W], ACT.Exp, bias=st[:, c:c + 1], scale=-1.0,
                                          accum_out=st[:, c + 2:c + 3]), v)
            a2 = A(lambda e: e.activation(st[:, c + 3:c + 4], col("sink", h), ACT.Exp, bias=st[:, c:c + 1]))
            info[u] = dict(k0=k0, W=W, T=T, c=c, tok=[a1, a2])

        def s1b(u):
            i = info[u]
            c, T, W = i["c"], i["T"], i["W"]
            v = V(lambda e: e.tensor_tensor(st[:, c + 4:c + 5], st[:, c + 2:c + 3], st[:, c + 3:c + 4], ALU.add),
                  i["tok"])
            v = V(lambda e: e.reciprocal(st[:, c + 5:c + 6], st[:, c + 4:c + 5]), v)
            i["tok"] = V(lambda e: e.tensor_scalar(T[:, 0:W], T[:, 0:W], st[:, c + 5:c + 6], None, ALU.mult), v)

        def s2(u):
            i = info[u]
            for k in range(i["W"] // 128):
                t = tr(ps[6][:, k * 128:(k + 1) * 128], i["T"][:, k * 128:(k + 1) * 128], i["tok"], bank_free[6])
            i["pt"] = t
            W = i["W"]
            prev = info[u - 3]["pv"] if u >= 3 else b_done
            a = A(lambda e: e.activation(PT[u % 3][:, 0:W], ps[6][:, 0:W], ACT.Copy), t, prev, hy_done)
            bank_free[6] = [a]
            i["ev"] = a

        def s3(u):
            n, h = units[u]
            i = info[u]
            j, base, kv = h % 4, 64 * (h // 4), h // 4
            nk = i["W"] // 128
            for k in range(nk):
                t = mm(ps[7][base:base + 64, j * 128:(j + 1) * 128], va[:, i["k0"] + k, kv * 64:kv * 64 + 64],
                       PT[u % 3][:, k * 128:(k + 1) * 128], k == 0, k == nk - 1, i["ev"], bank_free[7])
            i["pv"] = t
            if h == 7:
                hi = oahi[:, :, n * 128:(n + 1) * 128]
                lo = oalo[:, :, n * 128:(n + 1) * 128]
                src = ps[7][:].rearrange("p (j t) -> p j t", j=4)
                a = A(lambda e: e.activation(hi, src, ACT.Copy), t, hy_done)
                v = V(lambda e: e.tensor_tensor(lo, src, hi.bitcast(F32), ALU.subtract), a)
                bank_free[7] = [v]
                info["oa", n] = v

        for u in range(len(units) + 4):
            if 3 <= u < len(units) + 3:
                s2(u - 3)
            if u < len(units):
                s1(u)
            if 1 <= u <= len(units):
                s1b(u - 1)
            if u >= 4:
                s3(u - 4)
            yield
        oa_tok.extend(info["oa", n] for n in range(4))

    oa_tok = []
    def branch_group(name, gi, act, ready, half, first, rate=1):
        def evac(b, p, t):
            m = merged[:, 4 * half + b, :]
            gt = gate[gi][:, b, :]
            if first:
                v = V(lambda e: e.scalar_tensor_tensor(m, gt, 1.0, p[:], ALU.add, ALU.mult), t, gate_tok[gi, b],
                      hy_done)
                mtok[half, b] = v
                return [v]
            v = V(lambda e: e.scalar_tensor_tensor(gt, gt, 1.0, p[:], ALU.add, ALU.mult), t, gate_tok[gi, b])
            mtok[half, b] = G(lambda e: e.tensor_tensor(m, m, gt, ALU.add), v, mtok[half, b])
            return [v]
        gemm(name, act, ready, evac, rate=rate)
        gate_free[gi] = Q.last("vector", "gpsimd")

    background.append(att_a())
    for half in range(2):
        branch_group("bB%d" % half, half, lambda k: (obhi[:, k, :], oblo[:, k, :]), lambda k, b: ob_tok[0], half, True, rate=2)
    b_done.extend(Q.last("tensor"))

    rc = {}

    def evac_vc(b, p, t):
        a = A(lambda e: e.activation(vc[:, b, :], p[:], ACT.Copy), t, hy_done, tq_free[1])
        rc["v", b] = a
        return [a]

    gemm("qc", hT, hready, lambda b, p, t: rope(b, p, t, 8, 2, qcT, rc, "q"), rate=2)
    gemm("kc", hT, hready, lambda b, p, t: rope(b, p, t, 8, 3, kcT, rc, "k"), rate=2)
    gemm("vc", hT, hready, evac_vc, rate=2)
    flush()
    for half in range(2):
        gate_group("gA%d" % half, rate=2)
    drain()
    a_done = Q.last("tensor", "vector", "scalar", "gpsimd")
    rc_all = [rc[k] for k in sorted(rc)]

    Pc = [sb(f"Pc{i}", AR + 72 + 2 * i, [128, 512]) for i in range(6)]
    oc = sb("oc", AR + 84, [128, 512])
    ocs = sb("ocs", AR + 86, [128, 512])
    PTc = [sb(f"PTc{i}", AR + 88 + 2 * i, [128, 512]) for i in range(3)]
    ochi = sb("ochi", AR + 0, [128, 4, S], F32R)
    oclo = sb("oclo", AR + 8, [128, 4, S], F32R)
    oc_tok = {}

    def att_c():
        units = [(n, h) for n in range(4) for h in range(4)]
        info = {}

        def s1(u):
            n, h = units[u]
            prev = info[u - 3]["pt"] if u >= 3 else None
            P2 = [Pc[2 * (u % 3)], Pc[2 * (u % 3) + 1]]
            o = 24 + 16 * (u % 4)
            la = []
            for c in range(2):
                b = 4 + c
                base = 64 * c
                oo = o + 8 * c
                t = mm(ps[b][:], qcT[base:base + 64, h, n * 128:(n + 1) * 128], kcT[base:base + 64, h, :], True, True,
                       rc_all, bank_free[b])
                v = V(lambda e, b=b, oo=oo: e.tensor_reduce(st[:, oo:oo + 1], ps[b][:], AX.X, ALU.max), t, a_done)
                v = V(lambda e, oo=oo: e.tensor_scalar(st[:, oo + 1:oo + 2], st[:, oo:oo + 1], -0.125, None, ALU.mult), v)
                a = A(lambda e, b=b, oo=oo, c=c: e.activation(P2[c][:], ps[b][:], ACT.Exp, bias=st[:, oo + 1:oo + 2],
                                                              scale=0.125, accum_out=st[:, oo + 2:oo + 3]), v, prev,
                      a_done)
                bank_free[b] = [a]
                la.append(a)
            info[u] = dict(P=P2, tok=la, o=o)

        def s1b(u):
            i = info[u]
            o, P2, h = i["o"], i["P"], units[u][1]
            v = V(lambda e: e.reciprocal(st[:, o + 3:o + 4], st[:, o + 10:o + 11]), i["tok"])
            v = V(lambda e: e.scalar_tensor_tensor(st[:, o + 4:o + 5], st[:, o + 3:o + 4], lam, st[:, o + 2:o + 3],
                                                   ALU.mult, ALU.mult), v, t_lam)
            V(lambda e: e.reciprocal(st[:, 16 + 4 * (units[u][0] % 2) + h:17 + 4 * (units[u][0] % 2) + h], st[:, o + 2:o + 3]))
            i["tok"] = V(lambda e: e.scalar_tensor_tensor(P2[0][:], P2[1][:], st[:, o + 4:o + 5], P2[0][:], ALU.mult,
                                                          ALU.add), v)
            i["rtok"] = i["tok"]
            i["P"] = P2[0]

        def s2(u):
            i = info[u]
            for k in range(4):
                t = tr(ps[6][:, k * 128:(k + 1) * 128], i["P"][:, k * 128:(k + 1) * 128], i["tok"], bank_free[6])
            i["pt"] = t
            a = A(lambda e: e.activation(PTc[u % 3][:], ps[6][:], ACT.Copy), t,
                  info[u - 3]["pv"] if u >= 3 else None, a_done)
            bank_free[6] = [a]
            i["ev"] = a

        def s3(u):
            n, h = units[u]
            i = info[u]
            for k in range(4):
                t = mm(ps[7][:, h * 128:(h + 1) * 128], PTc[u % 3][:, k * 128:(k + 1) * 128],
                       vc[:, k, h * 128:(h + 1) * 128], k == 0, k == 3, i["ev"], bank_free[7])
            i["pv"] = t
            if h == 3:
                hv = lambda ap: ap.rearrange("p (h d) -> p h d", h=4)
                r0 = st[:, 16 + 4 * (n % 2):20 + 4 * (n % 2)].unsqueeze(2).to_broadcast([128, 4, 128])
                v = V(lambda e: e.tensor_tensor(hv(ocs[:]), hv(ps[7][:]), r0, ALU.mult), t, i["rtok"], a_done,
                      Q.last("tensor"))
                bank_free[7] = [v]
                a = A(lambda e: e.activation(oc[:], ocs[:], ACT.Square), v, a_done)
                info["raw"] = (n, a)

        def s3b():
            n, a = info.pop("raw")
            hv = lambda ap: ap.rearrange("p (h d) -> p h d", h=4)
            v = V(lambda e: e.tensor_reduce(st[:, 100:104], hv(oc[:]), AX.X, ALU.add), a)
            g = G(lambda e: e.tensor_scalar(st[:, 104:108], st[:, 100:104], 1.0 / 128, EPS, ALU.mult, ALU.add), v)
            g = G(lambda e: e.tensor_tensor(st[:, 108:112], st[:, 104:108], col("mhalf", 0, 4), ALU.pow), g)
            g = G(lambda e: e.tensor_scalar(st[:, 112:116], st[:, 108:112], 1.0 - LAM0, 0.0, ALU.mult, ALU.add), g)
            info["ocs"] = (n, G(lambda e: e.tensor_tensor(hv(ocs[:]), hv(ocs[:]),
                                                          st[:, 112:116].unsqueeze(2).to_broadcast([128, 4, 128]),
                                                          ALU.mult), g))

        def s4():
            n, v = info.pop("ocs")
            for k in range(4):
                t = tr(ps[6][:, k * 128:(k + 1) * 128], ocs[:, k * 128:(k + 1) * 128], v, bank_free[6])
            src = ps[6][:].rearrange("p (j t) -> p j t", j=4)
            hi, lo = ochi[:, :, n * 128:(n + 1) * 128], oclo[:, :, n * 128:(n + 1) * 128]
            a = A(lambda e: e.activation(hi, src, ACT.Copy, scale=col("subln")), t, a_done)
            oc_tok[n] = V(lambda e: e.scalar_tensor_tensor(lo, src, col("subln"), hi.bitcast(F32), ALU.mult,
                                                           ALU.subtract), a)
            bank_free[6] = [oc_tok[n]]

        for u in range(len(units) + 6):
            if 2 <= u < len(units) + 2:
                s2(u - 2)
            if u < len(units):
                s1(u)
            if 1 <= u <= len(units):
                s1b(u - 1)
            if "ocs" in info:
                s4()
            if "raw" in info:
                s3b()
            if 3 <= u < len(units) + 3:
                s3(u - 3)
            yield

    background.append(att_c())
    for half in range(2):
        branch_group("bA%d" % half, half, lambda k: (oahi[:, k, :], oalo[:, k, :]), lambda k, b: oa_tok, half, False, rate=2)
    gis = [gate_group("gC%d" % half, rate=2) for half in range(2)]
    drain()
    h_free1 = Q.last("tensor")
    oct = [oc_tok[n] for n in range(4)]
    x = sb("x", AR + 88, [128, 4, D])
    c_done = Q.last("tensor", "vector", "scalar", "gpsimd")
    tx2 = load(x[:], x_dram, s_x[0], c_done)
    m_ready = {}
    for half in range(2):
        def evac(b, p, t, half=half):
            gi = gis[half]
            k = 4 * half + b
            m, gt = merged[:, k, :], gate[gi][:, b, :]
            v = V(lambda e: e.scalar_tensor_tensor(gt, gt, 1.0, p[:], ALU.add, ALU.mult), t, gate_tok[gi, b])
            if half and b % 2:
                g = V(lambda e: e.tensor_tensor(m, m, gt, ALU.add), v, mtok[half, b])
            else:
                g = G(lambda e: e.tensor_tensor(m, m, gt, ALU.add), v, mtok[half, b])

            def split():
                a = A(lambda e: e.activation(hThi[:, k, :], m, ACT.Copy, scale=0.5), g, h_free1)
                m_ready[k] = V(lambda e: e.scalar_tensor_tensor(hTlo[:, k, :], m, 0.5, hThi[:, k, :].bitcast(F32),
                                                                ALU.mult, ALU.subtract), a)
            later(1, split)
            return [v]
        gemm("bC%d" % half, lambda k: (ochi[:, k, :], oclo[:, k, :]), lambda k, b: oct, evac)

    xs = sb("xs", AR + 16, [128, 4, D])
    junk = sb("junk", AR + 130, [128, 512])

    def residual(names, act, ready, row, junk_free=None):
        toks = {}
        for half in range(2):
            def evac(b, p, t, half=half):
                xa = x[:, b, half * 512:half * 512 + 512]
                v = V(lambda e: e.tensor_tensor(xa, p[:], xa, ALU.add), t, tx2)
                if half and b:
                    row(b - 1, [toks[0, b - 1], toks[1, b - 1]])
                toks[half, b] = half_square(x, b, half, junk[:], v, junk_free)
                return [v]
            gemm(names % half, act, ready, evac, banks=1)
        row(3, [toks[0, 3], toks[1, 3]])

    row, row_toks = scaled_rows(x, xs, lambda: Q.last("tensor", "vector", "scalar", "gpsimd"))
    residual("wo%d", hT, lambda k, b: m_ready[k], row, Q.last("tensor", "vector", "scalar", "gpsimd"))

    achi = sb("achi", AR + 0, [128, 22, S], F32R)
    aclo = sb("aclo", AR + 44, [128, 22, S], F32R)
    ft = [sb(f"ft{i}", AR + 104 + 2 * i, [128, S]) for i in range(8)]
    ft_free = [[] for _ in range(8)]

    def ffn(tag, conv):
        a_free = Q.last("tensor", "vector", "scalar", "gpsimd")
        ready = {}
        for j in range(11):
            pend = {}

            def evac(b, p, t, j=j):
                f = 2 * j + b % 2
                i = 4 * (j % 2) + b
                if conv:
                    c = f + 22 * (b // 2)
                    dst = ft[i]
                    a = A(lambda e: e.activation(dst[:], p[:], ACT.Identity, bias=col("cb2", c),
                                                 scale=col("cw2", 88 + c)), t, a_free, ft_free[i])
                    v = V(lambda e: e.scalar_tensor_tensor(dst[:, 1:S], p[:, 0:S - 1], col("cw2", 44 + c),
                                                           dst[:, 1:S], ALU.mult, ALU.add), a)
                    v = V(lambda e: e.scalar_tensor_tensor(dst[:, 2:S], p[:, 0:S - 2], col("cw2", c),
                                                           dst[:, 2:S], ALU.mult, ALU.add), v)
                    free = [v]
                    if b < 2:
                        pend[b] = v
                        return free
                    g = ft[i - 2]

                    def tail(v=v, g=g, dst=dst, f=f, i=i, u=pend[b - 2]):
                        a = A(lambda e: e.activation(g[:], g[:], ACT.Silu), u)
                        w = V(lambda e: e.tensor_tensor(g[:], g[:], dst[:], ALU.mult), v, a)
                        a = A(lambda e: e.activation(achi[:, f, :], g[:], ACT.Copy), w, a_free)
                        ready[f] = V(lambda e: e.tensor_tensor(aclo[:, f, :], g[:], achi[:, f, :].bitcast(F32),
                                                               ALU.subtract), a)
                        ft_free[i] = [ready[f]]
                        ft_free[i - 2] = [ready[f]]

                    later(b - 1, tail)
                    return free
                else:
                    if b < 2:
                        pend[b] = A(lambda e: e.activation(ft[i][:], p[:], ACT.Silu), t, a_free, ft_free[i])
                        free = [pend[b]]
                    else:
                        g = ft[i - 2]
                        v = V(lambda e: e.tensor_tensor(g[:], g[:], p[:], ALU.mult), t, pend[b - 2])
                        free = [v]
                if b >= 2:
                    g = ft[i - 2]
                    a = A(lambda e: e.activation(achi[:, f, :], g[:], ACT.Copy), v, a_free)
                    ready[f] = V(lambda e: e.tensor_tensor(aclo[:, f, :], g[:], achi[:, f, :].bitcast(F32),
                                                           ALU.subtract), a)
                    ft_free[i] = [ready[f]]
                    ft_free[i - 2] = [ready[f]]
                return free
            gemm("%s%d" % (tag, j), hT, hready, evac, banks=1)
        flush()
        return lambda k: (achi[:, k, :], aclo[:, k, :]), lambda k, b: ready[k]

    norm(xs, "g2", row_toks, Q.last("tensor"), 2)
    act, ready = ffn("up", False)
    row, row_toks = scaled_rows(x, xs, lambda: Q.last("tensor", "vector", "scalar", "gpsimd"))
    residual("dn%d", act, ready, row)

    norm(xs, "g3", row_toks, Q.last("tensor"), 2)
    b2 = Q.last("tensor", "vector", "scalar", "gpsimd")
    sqT = sb("sqT", AR + 0, [128, 4, S])
    skT = sb("skT", AR + 8, [128, 4, S])
    sv = sb("sv", AR + 16, [128, 4, 512])
    ohi = sb("ohi", AR + 24, [128, 8, S], F32R)
    olo = sb("olo", AR + 40, [128, 8, S], F32R)
    Qf = sb("Qf", AR + 56, [66, 8, S])
    Kf = sb("Kf", AR + 72, [66, 8, S])
    fv = sb("fv", AR + 104, [128, 4, 512])
    W5 = [sb(f"W5_{i}", AR + 112 + 2 * i, [128, 512]) for i in range(6)]
    PT2 = [sb(f"PT2_{i}", AR + 124 + 2 * i, [128, 512]) for i in range(2)]
    mk = sb("mk", AR + 128, [128, 640])
    st2 = sb("st2", AR + 130.5, [128, 96])
    s_mk = sem("s_mk")
    t_mk = load(mk[:], d["mask2"], s_mk, b2)
    r2 = {}

    def copy_evac(dst, key, scale):
        def evac(b, p, t):
            a = A(lambda e: e.activation(dst[:, b, :], p[:], ACT.Copy, scale=scale), t, b2)
            r2[key, b] = a
            return [a]
        return evac

    gemm("sq", hT, hready, copy_evac(sqT, "sq", 0.125))
    gemm("sk", hT, hready, copy_evac(skT, "sk", 1.0))
    fw = [W5[i] for i in range(4)]
    s_F = sem("s_F")
    fF = {}

    def evac_fl(b, p, t):
        z, e_, m_, s_ = (w[0:8, :] for w in fw)
        v = V(lambda e: e.tensor_scalar(z, p[0:8, :], col("fb", p=8), None, ALU.add), t, b2)
        a = A(lambda e: e.activation(e_, z, ACT.Abs), v)
        a = A(lambda e: e.activation(e_, e_, ACT.Exp, scale=-1.0), a)
        a = A(lambda e: e.activation(e_, e_, ACT.Ln, bias=col("one", p=8)), a)
        v2 = V(lambda e: e.tensor_scalar(m_, z, 0.0, None, ALU.min), v)
        v3 = V(lambda e: e.tensor_tensor_scan(s_, m_, e_, 0.0, ALU.add, ALU.subtract), v2, a)
        v4 = V(lambda e: e.tensor_scalar(z, s_, 8.0, None, ALU.mult), v3)
        v5 = V(lambda e: e.tensor_scalar(m_, s_, -8.0, None, ALU.mult), v3)
        m1 = G(lambda e: e.memset(Qf[64:66, :, :], 1.0), b2)
        m2 = G(lambda e: e.memset(Kf[64:66, :, :], 1.0))
        fF[0] = load(Qf[65:66, :, :], z, s_F, v4, m1)
        fF[1] = load(Kf[64:65, :, :], m_, s_F, v5, m2)
        return [v]

    A(lambda e: e.preload_act_table_set("natural_log_exp_and_others"), b2)
    gemm("fl", hT, hready, evac_fl, banks=2)
    w5_free = [fF[0], fF[1]]
    o_tok = {}
    on_free = [None]

    def out_norm(n, j0, gname, key, bank, pend, *after):
        a = A(lambda e: e.activation(W5[4][:], W5[3][:], ACT.Square, accum_out=st2[:, 80:81]), *after)

        def scale():
            g = G(lambda e: e.tensor_scalar(st2[:, 81:82], st2[:, 80:81], 1.0 / 512, EPS, ALU.mult, ALU.add), a)
            g = G(lambda e: e.tensor_tensor(st2[:, 82:83], st2[:, 81:82], col("mhalf"), ALU.pow), g)
            g = G(lambda e: e.tensor_scalar(W5[5][:], W5[3][:], st2[:, 82:83], 0.0, ALU.mult, ALU.add), g, on_free[0])
            on_free.append(g)

        def across():
            g = on_free.pop()
            for k in range(4):
                t = tr(ps[bank][:, k * 128:(k + 1) * 128], W5[5][:, k * 128:(k + 1) * 128], g, bank_free[bank])
            on_free[0] = t
            for k in range(4):
                hi = ohi[:, j0 + k, n * 128:(n + 1) * 128]
                p = ps[bank][:, k * 128:(k + 1) * 128]
                a = A(lambda e, hi=hi, p=p, k=k: e.activation(hi, p, ACT.Copy, scale=col(gname, k)), t, o_free[key])
            on_free.append(a)

        def rest():
            a = on_free.pop()
            for k in range(4):
                hi = ohi[:, j0 + k, n * 128:(n + 1) * 128]
                lo = olo[:, j0 + k, n * 128:(n + 1) * 128]
                p = ps[bank][:, k * 128:(k + 1) * 128]
                w = V(lambda e, hi=hi, lo=lo, p=p, k=k: e.scalar_tensor_tensor(lo, p, col(gname, k), hi.bitcast(F32),
                                                                              ALU.mult, ALU.subtract), a)
            o_tok[key, n] = w
            bank_free[bank] = [w]

        def both():
            across()
            rest()

        pend.extend([scale, nothing, both] if bank == 6 else [scale, nothing, across, rest])

    Lb = [sb(f"Lb{i}", AR + 32 + 2 * i if i < 4 else AR + 54, [128, 512]) for i in range(5)]
    zb = [sb(f"zb{i}", AR + 48 + 2 * i, [128, 512]) for i in range(3)]
    nb_ = W5[0:3]
    o_free = {"s": b2}
    left = []
    pairs = [(n, h) for two in ((3, 0), (2, 1)) for h in range(8) for n in two]
    nothing = lambda: None

    def att_s():
        units = pairs
        info = {}
        pend = []

        def s1(u):
            n, h = units[u]
            b, base, j = 4, 64 * (h % 2), h // 2
            W = 128 * (n + 1)
            nr, L, z = nb_[u % 3], Lb[u % 5], zb[u % 3]
            mm(ps[b][:, 0:W], sqT[base:base + 64, j, n * 128:(n + 1) * 128], skT[base:base + 64, j, 0:W],
               True, False, rs, bank_free[b])
            t = mm(ps[b][:, n * 128:W], ident, mk[:, 512:640], False, True, t_mk)
            a = A(lambda e: e.activation(z[:, 0:W], ps[b][:, 0:W], ACT.Copy), t, info[u - 3]["sum"] if u >= 3 else b2)
            bank_free[b] = [a]
            v1 = V(lambda e: e.scalar_tensor_tensor(L[:, 0:W], z[:, 0:W], -1.0, z[:, 0:W], ALU.mult, ALU.max), a,
                   info[u - 5]["pt"] if u >= 5 else b2)
            v2 = V(lambda e: e.tensor_scalar(nr[:, 0:W], z[:, 0:W], -1.0, 0.0, ALU.mult, ALU.min), w5_free)
            info[u] = dict(nr=nr, L=L, z=z, W=W, abs=v1, neg=v2)

        def s1b(u):
            i = info[u]
            L, W = i["L"], i["W"]
            a = A(lambda e: e.activation(L[:, 0:W], L[:, 0:W], ACT.Exp, scale=-1.0), i["abs"])
            i["ln"] = A(lambda e: e.activation(L[:, 0:W], L[:, 0:W], ACT.Ln, bias=col("one")), a)

        def s1c(u):
            i = info[u]
            nr, L, z, W = i["nr"], i["L"], i["z"], i["W"]
            v = V(lambda e: e.tensor_tensor_scan(nr[:, 0:W][:, ::-1], nr[:, 0:W][:, ::-1], L[:, 0:W][:, ::-1], 0.0,
                                                 ALU.add, ALU.subtract), i["neg"], i["ln"])
            i["sum"] = G(lambda e: e.tensor_tensor(L[:, 0:W], z[:, 0:W], nr[:, 0:W], ALU.add), v)

        def s1d(u):
            i = info[u]
            L, W = i["L"], i["W"]
            i["tok"] = A(lambda e: e.activation(L[:, 0:W], L[:, 0:W], ACT.Exp), i["sum"])

        def s2(u):
            i = info[u]
            W = i["W"]
            for k in range(W // 128):
                t = tr(ps[6][:, k * 128:(k + 1) * 128], i["L"][:, k * 128:(k + 1) * 128], i["tok"], bank_free[6])
            i["pt"] = t
            v = V(lambda e: e.tensor_copy(PT2[u % 2][:, 0:W], ps[6][:, 0:W]), t,
                  info[u - 2]["pv"] if u >= 2 else b2)
            bank_free[6] = [v]
            i["ev"] = v

        def s3(u):
            n, h = units[u]
            i = info[u]
            b = 5 if n > 1 else 7
            rv = [r2["sv", k] for k in range(n + 1)]
            for k in range(n + 1):
                t = mm(ps[b][:, h * 64:(h + 1) * 64], PT2[u % 2][:, k * 128:(k + 1) * 128],
                       sv[:, k, h * 64:(h + 1) * 64], k == 0, k == n, i["ev"], rv, bank_free[b])
            i["pv"] = t
            if h == 7:
                if left:
                    left.pop(0)()
                a = A(lambda e: e.activation(W5[3][:], ps[b][:], ACT.Copy), t, w5_free, Q.last("gpsimd"))
                bank_free[b] = [a]
                last_two = u >= 30
                out_norm(n, 0, "gsb", "s", 3 if last_two else 6, left if last_two else pend, a)

        N = len(units)
        for u in range(N + 5):
            if 2 <= u < N + 2:
                s1c(u - 2)
            if 4 <= u < N + 4:
                s2(u - 4)
            if u < N:
                s1(u)
            if 1 <= u <= N:
                s1b(u - 1)
            if 2 <= u < N + 2:
                s1d(u - 2)
            if pend:
                pend.pop(0)()
            if 5 <= u < N + 5:
                s3(u - 5)
            yield

    rs = [r2[k, b] for k in ("sq", "sk") for b in range(4)]
    background.append(att_s())
    gemm("sv", hT, hready, copy_evac(sv, "sv", 1.0))

    def head_evac(dst, key):
        def evac(b, p, t):
            if b % 2:
                V(lambda e: e.tensor_copy(dst[0:64, 2 * b, :], p[0:64, :]), t, b2)
                a = V(lambda e: e.tensor_copy(dst[0:64, 2 * b + 1, :], p[64:128, :]))
            else:
                A(lambda e: e.activation(dst[0:64, 2 * b, :], p[0:64, :], ACT.Copy), t, b2)
                a = A(lambda e: e.activation(dst[0:64, 2 * b + 1, :], p[64:128, :], ACT.Copy))
            r2[key, b] = a
            return [a]
        return evac

    rfv = []
    Tf = [sb(f"Tf{i}", AR + 2 * i, [128, 512]) for i in range(6)]
    PTf = [sb(f"PTf{i}", AR + 12 + 2 * i, [128, 512]) for i in range(4)]

    def att_f():
        s_done = Q.last("tensor", "vector", "scalar", "gpsimd")
        rf = [r2[k, b] for k in ("fq", "fk") for b in range(4)] + [fF[0], fF[1]]
        o_free["f"] = s_done
        units = pairs
        info = {}
        pend = [nothing, nothing] + left

        def s1(u):
            n, h = units[u]
            b = (4, 5, 7)[u] if u < 3 else u % 3
            W = 128 * (n + 1)
            T = Tf[u % 6]
            t = mm(ps[b][:, 0:W], Qf[:, h, n * 128:(n + 1) * 128], Kf[:, h, 0:W], True, True, rf, bank_free[b])
            c = u % 6
            m0 = 128 * (3 - n)
            v = V(lambda e: e.tensor_tensor_reduce(T[:, 0:W], ps[b][:, 0:W], mk[:, m0:m0 + W], -0.125, 3e38, ALU.add,
                                                   ALU.min, st2[:, c:c + 1]), t, t_mk,
                  info[u - 6]["pt"] if u >= 6 else s_done)
            bank_free[b] = [v]
            sm = st2[:, 48 + 8 * n + h:49 + 8 * n + h]
            a = A(lambda e: e.activation(T[:, 0:W], T[:, 0:W], ACT.Exp, bias=st2[:, c:c + 1], scale=-1.0, accum_out=sm), v)
            info[u] = dict(T=T, tok=a, W=W)

        def s2(u):
            i = info[u]
            W = i["W"]
            b = 4 + u % 2
            for k in range(W // 128):
                t = tr(ps[b][:, k * 128:(k + 1) * 128], i["T"][:, k * 128:(k + 1) * 128], i["tok"], bank_free[b])
            i["pt"] = t
            pv = info[u - 4]["pv"] if u >= 4 else s_done
            if u % 2:
                i["ev"] = A(lambda e: e.activation(PTf[u % 4][:, 0:W], ps[b][:, 0:W], ACT.Copy), t, pv)
            else:
                i["ev"] = V(lambda e: e.tensor_copy(PTf[u % 4][:, 0:W], ps[b][:, 0:W]), t, pv)
            bank_free[b] = [i["ev"]]

        def s3(u):
            n, h = units[u]
            i = info[u]
            b = 6 if n > 1 else 7
            for k in range(n + 1):
                t = mm(ps[b][:, h * 64:(h + 1) * 64], PTf[u % 4][:, k * 128:(k + 1) * 128],
                       fv[:, k, h * 64:(h + 1) * 64], k == 0, k == n, i["ev"], rfv, bank_free[b])
            i["pv"] = t
            if h == 7:
                c = 48 + 8 * n
                v = V(lambda e: e.reciprocal(st2[:, 40:48], st2[:, c:c + 8]), i["tok"])
                v = V(lambda e: e.tensor_tensor(W5[3][:].rearrange("p (h d) -> p h d", h=8),
                                                ps[b][:].rearrange("p (h d) -> p h d", h=8),
                                                st2[:, 40:48].unsqueeze(2).to_broadcast([128, 8, 64]), ALU.mult),
                      v, t, Q.last("gpsimd"))
                bank_free[b] = [v]
                out_norm(n, 4, "gfox", "f", 3, pend, v)

        N = len(units)
        for u in range(N + 6):
            while u == 3 and not rfv:
                yield
            if u < N:
                s1(u)
            if 3 <= u < N + 3:
                s2(u - 3)
            if pend:
                pend.pop(0)()
            if 5 <= u < N + 5:
                s3(u - 5)
            yield
        for i, fn in enumerate(pend):
            later(1 if i < len(pend) - 2 else 2, fn)

    background.append(att_f())
    gemm("fq", hT, hready, head_evac(Qf, "fq"), rate=2)
    gemm("fk", hT, hready, head_evac(Kf, "fk"), rate=4)
    gemm("fv", hT, hready, copy_evac(fv, "fv", 1.0), rate=4)
    rfv.extend(r2["fv", b] for b in range(4))
    drain()
    row, row_toks = scaled_rows(x, xs, lambda: Q.last("tensor", "vector", "scalar", "gpsimd"))
    residual("xo%d", lambda k: (ohi[:, k, :], olo[:, k, :]), lambda k, b: o_tok["s" if k < 4 else "f", b], row)
    norm(xs, "g4", row_toks, Q.last("tensor"), 2)
    act, ready = ffn("vp", True)
    fg = sb("fg", AR + 104, [128, D])
    s_fg = sem("s_fg")
    t_fg = load(fg[:], d["fg"], s_fg, Q.last("tensor", "vector", "scalar", "gpsimd"))
    s_out = sem("s_out")
    o_dram = out.rearrange("b (i p) c -> p (b i) c", p=128)
    outs = []

    def out_row(i, halves):
        g = row_rstd(i, halves)
        for h in range(2):
            c = slice(512 * h, 512 * h + 512)
            v = V(lambda e, c=c: e.scalar_tensor_tensor(xs[:, i, c], x[:, i, c], small[:, 8 + i:9 + i], fg[:, c],
                                                        ALU.mult, ALU.mult), g, t_fg,
                  Q.last("tensor", "vector", "scalar", "gpsimd"))
            outs.append(load(o_dram[:, i, c], xs[:, i, c], s_out, v))

    residual("vd%d", act, ready, out_row)
    t_out = outs[-1]
    t_out.used = True
    assert state["split"] == n_slots
    Q.number()

    with nc.Block() as block:
        @block.sync
        def _(e):
            Q.run("sync", e)
            e.wait_ge(s_out, 16 * len(outs))

        @block.tensor
        def _(e):
            Q.run("tensor", e)

        @block.vector
        def _(e):
            Q.run("vector", e)

        @block.scalar
        def _(e):
            Q.run("scalar", e)

        @block.gpsimd
        def _(e):
            Q.run("gpsimd", e)


def _tables():
    f = np.float32
    t = {}
    pos = np.arange(S, dtype=f)
    inv = f(10000.0) ** (-np.arange(0, 64, 2, dtype=f) / f(64))
    ang = pos[:, None] * inv[None, :]
    c, s = np.cos(ang).astype(f), np.sin(ang).astype(f)
    tile = lambda a: np.ascontiguousarray(a.reshape(4, 128, -1).transpose(1, 0, 2))
    t["cos"] = tile(np.concatenate([c, c], 1)).reshape(128, 256)
    t["sin"] = tile(np.concatenate([-s, s], 1)).reshape(128, 256)
    tt = pos / f(S - 1)
    bands = np.arange(1, 17, dtype=f)
    a2 = (f(2.0 * math.pi) * pos[:, None] * bands[None, :] / f(S)).astype(f)
    z = np.concatenate([tt[:, None], np.cos(a2), np.sin(a2)], -1).astype(f)
    par = np.concatenate([np.arange(0, S, 2), np.arange(1, S, 2)])
    t["zT"] = np.ascontiguousarray(z[par].T)
    deltas = np.abs(np.linspace(math.log(1e-2) / 1.5, math.log(1e-2) / 0.3, 512, dtype=f))
    t["dec"] = tile(np.exp(-tt[:, None] * deltas[None, :])[par].astype(f))
    k = np.concatenate([np.arange(0, S, 2), np.arange(S - 1, 0, -2)])
    ph = (np.outer(par, 2 * k[:256] + 1) % 2048) * (math.pi / 1024)
    t["cu"], t["su"] = tile(np.cos(ph).astype(f)), tile(-np.sin(ph).astype(f))
    ph = (np.outer(2 * np.arange(256) + 1, 2 * k + 1) % 4096) * (math.pi / 2048)
    p, m = np.cos(ph) + np.sin(ph), np.cos(ph) - np.sin(ph)
    half = lambda a: np.ascontiguousarray(a.astype(f).reshape(2, 128, 512).transpose(1, 0, 2))
    t["fp"], t["fm"] = half(p), half(m)
    t["ip"], t["im"] = tile(p.T.astype(f)), tile(m.T.astype(f))
    i, j = np.arange(128)[:, None], np.arange(128)[None, :]
    zero = np.zeros((128, 128), f)
    n = f(NEG)
    t["maskA"] = np.concatenate([np.where(j >= i, f(0), n), zero, np.where(j <= i, f(0), n)], 1).astype(f)
    t["mask2"] = np.concatenate([zero, zero, zero, np.where(j <= i, f(0), n), np.where(j < i, f(0), n)], 1).astype(f)
    return t


def _layout(inp):
    f = np.float32
    g = {k: np.asarray(v) for k, v in inp.items()}
    tb = _tables()
    VEC, NV = vec_layout()
    vec = np.zeros((128, NV), f)

    def put(name, a, p=128):
        o, w = VEC[name]
        vec[0:p, o:o + w] = a

    cols = lambda v: v.reshape(-1, 128).T
    row = lambda v: np.broadcast_to(v.reshape(1, -1), (128, v.size))
    put("g1", cols(g["norm1_g"]))
    put("g2", cols(g["norm2_g"]))
    put("g3", cols(g["attn_norm_g_2"]))
    put("g4", cols(g["ffn_norm_g_2"]))
    put("cw", cols(g["conv_w"]))
    put("cb", cols(g["conv_b"]))
    put("hd", cols(g["hy_d"]))
    put("gfox", cols(g["fox_out_g_2"]))
    put("gsb", cols(g["sb_out_g_2"]))
    put("cw2", cols(g["conv_w_2"]))
    put("cb2", cols(g["conv_b_2"]))
    put("subln", cols(g["subln_c"]))
    put("sink", row(g["sink_a"]))
    put("fb", g["forget_bias_2"].reshape(8, 1), 8)
    for a, b in (("b1", "filt_b1"), ("f1", "filt_f1"), ("b2", "filt_b2"), ("f2", "filt_f2")):
        put(a, g[b].reshape(64, 1), 64)
    for a, b in (("qna", "qn_a"), ("kna", "kn_a"), ("qnc", "qn_c"), ("knc", "kn_c"), ("lq1", "lam_q1"),
                 ("lk1", "lam_k1"), ("lq2", "lam_q2"), ("lk2", "lam_k2")):
        put(a, row(g[b]))
    put("ident", np.eye(128, dtype=f))
    put("one", 1.0)
    put("half", 0.5)
    put("mhalf", -0.5)
    put("cos", tb.pop("cos"))
    put("sin", tb.pop("sin"))
    put("w1", g["filt_w1"][0], 33)
    put("w2", g["filt_w2"][0], 64)

    TABLE, OFFS, total = slot_table()
    ws = np.empty(total, f)

    def pack(name, w):
        first, n_s, n, _ = TABLE[name]
        a = w.reshape(n_s, 2, 128, n).transpose(0, 2, 1, 3)
        o = OFFS[first][0]
        ws[o:o + a.size] = np.ascontiguousarray(a).reshape(-1)

    w = g["w_in"][0]
    perm = [0, 4, 1, 5, 2, 6, 3, 7]
    hp = np.concatenate([np.arange(h * 64, h * 64 + 64) for h in perm])
    pack("qa", w[:, :512][:, hp])
    pack("kva", w[:, 512:768])
    for i in range(3):
        pack("hy%d" % i, w[:, 768 + 512 * i:1280 + 512 * i])
    for i, nm in enumerate(("qc", "kc", "vc")):
        pack(nm, w[:, 2304 + 512 * i:2816 + 512 * i])
    for i, nm in enumerate(("gA", "gB", "gC")):
        for j in range(2):
            o = 3840 + 1024 * i + 512 * j
            pack("%s%d" % (nm, j), w[:, o:o + 512])
    for nm, src in (("bA", g["w_oa"][0][hp]), ("bB", g["w_ob"][0]), ("bC", g["w_oc"][0]), ("wo", g["w_out"][0]),
                    ("dn", g["ffn_w2"][0]), ("xo", np.roll(g["w_out_2"][0], 512, axis=0)), ("vd", g["w_down_2"][0])):
        for j in range(2):
            pack("%s%d" % (nm, j), src[:, 512 * j:512 * j + 512])
    for tag, a, b in (("up", g["ffn_w1"][0], g["ffn_w3"][0]),
                      ("vp", g["w_up_2"][0][:, :2816], g["w_up_2"][0][:, 2816:])):
        for j in range(11):
            c = slice(256 * j, 256 * j + 256)
            pack("%s%d" % (tag, j), np.concatenate([a[:, c], b[:, c]], 1))
    w = g["w_in_2"][0]
    for nm, o in (("fq", 0), ("fk", 512), ("fv", 1024), ("sq", 1544), ("sk", 2056), ("sv", 2568)):
        pack(nm, w[:, o:o + 512])
    pad = np.zeros((1024, 128), f)
    pad[:, 0:8] = w[:, 1536:1544]
    pack("fl", pad)
    arrays = dict(tb)
    arrays["vec"] = vec
    arrays["ws"] = ws
    arrays["x"] = g["x"]
    arrays["w3"] = g["filt_w3"][0]
    arrays["fg"] = np.ascontiguousarray(row(g["final_norm_g_2"]))
    return {k: np.ascontiguousarray(v) for k, v in arrays.items()}


def kernel(**inputs):
    import concourse.bacc as bacc
    from concourse.bass_utils import run_bass_kernel_spmd

    nc = bacc.Bacc("TRN2", target_bir_lowering=False, num_devices=1)
    arrays = _layout(inputs)
    d = {k: nc.dram_tensor("in_" + k, a.shape, F32, kind="ExternalInput").ap() for k, a in arrays.items()}
    out = nc.dram_tensor("out", (1, S, D), F32, kind="ExternalOutput").ap()
    build(nc, d, out)
    r = run_bass_kernel_spmd(nc, [{"in_" + k: a for k, a in arrays.items()}], core_ids=[0])
    return r.results[0]["out"]
```
